# Optimizing a Trainium2 kernel written in Bass

```python
import math
import jax
import jax.numpy as jnp
from jax import lax
import numpy as np

D_MODEL = 2048
BATCH = 1
SEQ = 256
DEPTH = 1
DEC_BATCH = 1
DEC_SEQ = 64
PAST_LEN = 256

CHUNK = 64
Q_BLOCK = 128
ATT_HEADS = 8
ATT_HD = 64
ATT_WIDTH = ATT_HEADS * 2 * ATT_HD
ROPE_DIM = ATT_HD // 4
ROPE_THETA = 500000.0
SSM_WIDTH = D_MODEL - ATT_WIDTH
SSM_P = 16
SSM_GROUPS = SSM_WIDTH // SSM_P
SSM_N = 64
DT_MIN = 0.001
DT_MAX = 0.1
IN_WIDTH = 3 * ATT_WIDTH + SSM_WIDTH
PEER_HEADS = 8
PEER_KEYS = 128
PEER_EXPERTS = PEER_KEYS * PEER_KEYS
PEER_QDIM = 256
PEER_HALF = PEER_QDIM // 2
PEER_TOPK = 16
PEER_BLOCK = 128
EPS = 1e-6
NEG_INF = -1e30

kernel_name = 'hymba_diffattn_s5_peer_stream_step'

def rms_norm(x, g):
    xf = x.astype(jnp.float32)
    y = xf * lax.rsqrt(jnp.mean(xf * xf, axis=-1, keepdims=True) + EPS)
    return (y * g.astype(jnp.float32)).astype(x.dtype)

def partial_rope(t, pos):
    half = ROPE_DIM // 2
    inv_freq = ROPE_THETA ** (-jnp.arange(half, dtype=jnp.float32) * (2.0 / ROPE_DIM))
    ang = pos.astype(jnp.float32)[:, None] * inv_freq[None, :]
    cos = jnp.cos(ang)[None, :, None, None, :]
    sin = jnp.sin(ang)[None, :, None, None, :]
    tf = t.astype(jnp.float32)
    t1 = tf[..., :half]
    t2 = tf[..., half:ROPE_DIM]
    out = jnp.concatenate([t1 * cos - t2 * sin, t2 * cos + t1 * sin, tf[..., ROPE_DIM:]], axis=-1)
    return out.astype(t.dtype)

def diff_lambda(lq1, lk1, lq2, lk2, lam_init):
    f32 = jnp.float32
    return (jnp.exp(jnp.sum(lq1.astype(f32) * lk1.astype(f32)))
            - jnp.exp(jnp.sum(lq2.astype(f32) * lk2.astype(f32))) + lam_init)

def diff_attn_block(q, k, v, q_chunk, k_chunk, lam):
    s = jnp.einsum('bqhcd,bkhcd->bhcqk', q, k).astype(jnp.float32) * (ATT_HD ** -0.5)
    visible = k_chunk[None, :] <= q_chunk[:, None]
    s = jnp.where(visible, s, NEG_INF)
    p = jax.nn.softmax(s, axis=-1)
    w = p[:, :, 0] - lam * p[:, :, 1]
    return jnp.einsum('bhqk,bkhe->bqhe', w.astype(v.dtype), v)

def ssm_mixer(u, h0_re, h0_im, a_re, a_im, log_dt, b_re, b_im, c_re, c_im, d_skip, w_glu, b_glu):
    f32 = jnp.float32
    B, L, _ = u.shape
    uf = u.astype(f32).reshape(B, L, SSM_GROUPS, SSM_P)
    dt = jnp.exp(log_dt.astype(f32))[:, None]
    ar = a_re.astype(f32)
    ai = a_im.astype(f32)
    mag = jnp.exp(dt * ar)
    abar_r = mag * jnp.cos(dt * ai)
    abar_i = mag * jnp.sin(dt * ai)
    den = ar * ar + ai * ai
    nr = abar_r - 1.0
    ni = abar_i
    coef_r = (nr * ar + ni * ai) / den
    coef_i = (ni * ar - nr * ai) / den
    br = b_re.astype(f32)
    bi = b_im.astype(f32)
    bbar_r = coef_r[..., None] * br - coef_i[..., None] * bi
    bbar_i = coef_r[..., None] * bi + coef_i[..., None] * br
    bu_r = jnp.einsum('blgp,gnp->blgn', uf, bbar_r)
    bu_i = jnp.einsum('blgp,gnp->blgn', uf, bbar_i)
    a_r = jnp.broadcast_to(abar_r, (1, L, SSM_GROUPS, SSM_N))
    a_i = jnp.broadcast_to(abar_i, (1, L, SSM_GROUPS, SSM_N))

    def combine(e1, e2):
        a1r, a1i, b1r, b1i = e1
        a2r, a2i, b2r, b2i = e2
        return (a2r * a1r - a2i * a1i, a2r * a1i + a2i * a1r,
                a2r * b1r - a2i * b1i + b2r, a2r * b1i + a2i * b1r + b2i)

    pr, pi, hr, hi = lax.associative_scan(combine, (a_r, a_i, bu_r, bu_i), axis=1)
    if h0_re is not None:
        h0r = h0_re.astype(f32)[:, None]
        h0i = h0_im.astype(f32)[:, None]
        hr = hr + pr * h0r - pi * h0i
        hi = hi + pr * h0i + pi * h0r
    y = (jnp.einsum('blgn,gpn->blgp', hr, c_re.astype(f32))
         - jnp.einsum('blgn,gpn->blgp', hi, c_im.astype(f32))
         + d_skip.astype(f32).reshape(SSM_GROUPS, SSM_P) * uf)
    y = jax.nn.gelu(y.reshape(B, L, SSM_WIDTH))
    y = y * jax.nn.sigmoid(y @ w_glu.astype(f32) + b_glu.astype(f32))
    return y.astype(u.dtype), hr[:, -1].astype(u.dtype), hi[:, -1].astype(u.dtype)

def peer_ffn(x, w_peer_q, peer_keys, peer_u, peer_v):
    B, L, D = x.shape
    T = B * L
    xt = x.reshape(T, D)
    q = (xt @ w_peer_q).reshape(T, PEER_HEADS, 2, PEER_HALF)
    s = jnp.einsum('thcd,hcnd->thcn', q, peer_keys).astype(jnp.float32)
    sv, si = lax.top_k(s, PEER_TOPK)
    cand = (sv[:, :, 0, :, None] + sv[:, :, 1, None, :]).reshape(T, PEER_HEADS, PEER_TOPK * PEER_TOPK)
    cidx = (si[:, :, 0, :, None] * PEER_KEYS + si[:, :, 1, None, :]).reshape(T, PEER_HEADS, PEER_TOPK * PEER_TOPK)
    fv, fp = lax.top_k(cand, PEER_TOPK)
    eidx = jnp.take_along_axis(cidx, fp, axis=-1)
    g = jax.nn.softmax(fv, axis=-1).astype(x.dtype)
    nblk = -(-T // PEER_BLOCK)
    pad = nblk * PEER_BLOCK - T
    xp = jnp.pad(xt, ((0, pad), (0, 0))).reshape(nblk, PEER_BLOCK, D)
    ep = jnp.pad(eidx, ((0, pad), (0, 0), (0, 0))).reshape(nblk, PEER_BLOCK, PEER_HEADS, PEER_TOPK)
    gp = jnp.pad(g, ((0, pad), (0, 0), (0, 0))).reshape(nblk, PEER_BLOCK, PEER_HEADS, PEER_TOPK)

    def expert_block(args):
        xb, eb, gb = args
        u = jnp.take(peer_u, eb, axis=0)
        act = jax.nn.gelu(jnp.einsum('td,thkd->thk', xb, u))
        v = jnp.take(peer_v, eb, axis=0)
        return jnp.einsum('thk,thkd->td', gb * act, v)

    out = lax.map(expert_block, (xp, ep, gp)).reshape(nblk * PEER_BLOCK, D)[:T]
    return out.reshape(B, L, D)

def hybrid_layer(x, pos, past_k, past_v, h0_re, h0_im, lam_init, params):
    (norm1_g, w_in, q_norm_g, k_norm_g, lambda_q1, lambda_k1, lambda_q2, lambda_k2, subln_g,
     ssm_a_re, ssm_a_im, ssm_log_dt, ssm_b_re, ssm_b_im, ssm_c_re, ssm_c_im, ssm_d, w_glu, b_glu,
     w_out, norm2_g, w_peer_q, peer_keys, peer_u, peer_v) = params
    B, L, _ = x.shape
    proj = rms_norm(x, norm1_g) @ w_in
    q = proj[..., :ATT_WIDTH].reshape(B, L, ATT_HEADS, 2, ATT_HD)
    k = proj[..., ATT_WIDTH:2 * ATT_WIDTH].reshape(B, L, ATT_HEADS, 2, ATT_HD)
    v = proj[..., 2 * ATT_WIDTH:3 * ATT_WIDTH].reshape(B, L, ATT_HEADS, 2 * ATT_HD)
    u = proj[..., 3 * ATT_WIDTH:]
    q = partial_rope(rms_norm(q, q_norm_g), pos)
    k = partial_rope(rms_norm(k, k_norm_g), pos)
    lam = diff_lambda(lambda_q1, lambda_k1, lambda_q2, lambda_k2, lam_init)
    q_chunk = pos // CHUNK
    if past_k is None:
        nb = L // Q_BLOCK
        qb = jnp.moveaxis(q.reshape(B, nb, Q_BLOCK, ATT_HEADS, 2, ATT_HD), 1, 0)
        qcb = q_chunk.reshape(nb, Q_BLOCK)
        o = lax.map(lambda a: diff_attn_block(a[0], k, v, a[1], q_chunk, lam), (qb, qcb))
        o = jnp.moveaxis(o, 0, 1).reshape(B, L, ATT_HEADS, 2 * ATT_HD)
    else:
        P = past_k.shape[1]
        k_all = jnp.concatenate([past_k, k], axis=1)
        v_all = jnp.concatenate([past_v, v], axis=1)
        k_chunk = jnp.arange(P + L, dtype=jnp.int32) // CHUNK
        o = diff_attn_block(q, k_all, v_all, q_chunk, k_chunk, lam)
    o = rms_norm(o, subln_g) * (1.0 - lam_init)
    s, h_re, h_im = ssm_mixer(u, h0_re, h0_im, ssm_a_re, ssm_a_im, ssm_log_dt, ssm_b_re, ssm_b_im,
                              ssm_c_re, ssm_c_im, ssm_d, w_glu, b_glu)
    mix = jnp.concatenate([o.reshape(B, L, ATT_WIDTH), s], axis=-1)
    x = x + mix @ w_out
    x = x + peer_ffn(rms_norm(x, norm2_g), w_peer_q, peer_keys, peer_u, peer_v)
    return x, k, v, h_re, h_im

def setup_inputs(seed: int = 0) -> dict:
    key = jax.random.key(seed)
    ks = jax.random.split(key, 32)
    f32 = jnp.float32

    def nrm(k, shape, scale):
        return scale * jax.random.normal(k, shape, f32)

    a_im_base = jnp.pi * jnp.arange(SSM_N, dtype=f32)
    return {
        'x_prompt': nrm(ks[0], (BATCH, SEQ, D_MODEL), 1.0),
        'x_sample': nrm(ks[1], (DEC_BATCH, DEC_SEQ, D_MODEL), 1.0),
        'cache_k': nrm(ks[2], (DEPTH, DEC_BATCH, PAST_LEN, ATT_HEADS, 2, ATT_HD), 1.0),
        'cache_v': nrm(ks[3], (DEPTH, DEC_BATCH, PAST_LEN, ATT_HEADS, 2 * ATT_HD), 1.0),
        'state_ssm_re': nrm(ks[4], (DEPTH, DEC_BATCH, SSM_GROUPS, SSM_N), 0.5),
        'state_ssm_im': nrm(ks[5], (DEPTH, DEC_BATCH, SSM_GROUPS, SSM_N), 0.5),
        'norm1_g': 1.0 + nrm(ks[6], (DEPTH, D_MODEL), 0.02),
        'w_in': nrm(ks[7], (DEPTH, D_MODEL, IN_WIDTH), D_MODEL ** -0.5),
        'q_norm_g': 1.0 + nrm(ks[8], (DEPTH, ATT_HD), 0.02),
        'k_norm_g': 1.0 + nrm(ks[9], (DEPTH, ATT_HD), 0.02),
        'lambda_q1': nrm(ks[10], (DEPTH, ATT_HD), 0.1),
        'lambda_k1': nrm(ks[11], (DEPTH, ATT_HD), 0.1),
        'lambda_q2': nrm(ks[12], (DEPTH, ATT_HD), 0.1),
        'lambda_k2': nrm(ks[13], (DEPTH, ATT_HD), 0.1),
        'subln_g': 1.0 + nrm(ks[14], (DEPTH, 2 * ATT_HD), 0.02),
        'ssm_a_re': -0.5 + nrm(ks[15], (DEPTH, SSM_GROUPS, SSM_N), 0.01),
        'ssm_a_im': a_im_base + nrm(ks[16], (DEPTH, SSM_GROUPS, SSM_N), 0.01),
        'ssm_log_dt': jax.random.uniform(ks[17], (DEPTH, SSM_GROUPS), f32,
                                         minval=math.log(DT_MIN), maxval=math.log(DT_MAX)),
        'ssm_b_re': nrm(ks[18], (DEPTH, SSM_GROUPS, SSM_N, SSM_P), (2 * SSM_P) ** -0.5),
        'ssm_b_im': nrm(ks[19], (DEPTH, SSM_GROUPS, SSM_N, SSM_P), (2 * SSM_P) ** -0.5),
        'ssm_c_re': nrm(ks[20], (DEPTH, SSM_GROUPS, SSM_P, SSM_N), (2 * SSM_N) ** -0.5),
        'ssm_c_im': nrm(ks[21], (DEPTH, SSM_GROUPS, SSM_P, SSM_N), (2 * SSM_N) ** -0.5),
        'ssm_d': nrm(ks[22], (DEPTH, SSM_WIDTH), 1.0),
        'w_glu': nrm(ks[23], (DEPTH, SSM_WIDTH, SSM_WIDTH), SSM_WIDTH ** -0.5),
        'b_glu': nrm(ks[24], (DEPTH, SSM_WIDTH), 0.01),
        'w_out': nrm(ks[25], (DEPTH, D_MODEL, D_MODEL), D_MODEL ** -0.5),
        'norm2_g': 1.0 + nrm(ks[26], (DEPTH, D_MODEL), 0.02),
        'w_peer_q': nrm(ks[27], (DEPTH, D_MODEL, PEER_HEADS * PEER_QDIM), D_MODEL ** -0.5),
        'peer_keys': nrm(ks[28], (DEPTH, PEER_HEADS, 2, PEER_KEYS, PEER_HALF), PEER_HALF ** -0.5),
        'peer_u': nrm(ks[29], (DEPTH, PEER_EXPERTS, D_MODEL), D_MODEL ** -0.5),
        'peer_v': nrm(ks[30], (DEPTH, PEER_EXPERTS, D_MODEL), PEER_HEADS ** -0.5),
    }

def reference(x_prompt, x_sample, cache_k, cache_v, state_ssm_re, state_ssm_im,
              norm1_g, w_in, q_norm_g, k_norm_g, lambda_q1, lambda_k1, lambda_q2, lambda_k2, subln_g,
              ssm_a_re, ssm_a_im, ssm_log_dt, ssm_b_re, ssm_b_im, ssm_c_re, ssm_c_im, ssm_d,
              w_glu, b_glu, w_out, norm2_g, w_peer_q, peer_keys, peer_u, peer_v):
    Lp = x_prompt.shape[1]
    Ls = x_sample.shape[1]
    past = cache_k.shape[2]
    pos_p = jnp.arange(Lp, dtype=jnp.int32)
    pos_s = past + jnp.arange(Ls, dtype=jnp.int32)
    yp = x_prompt
    ys = x_sample
    kp_l, vp_l, hrp_l, hip_l = [], [], [], []
    ks_l, vs_l, hrs_l, his_l = [], [], [], []
    for layer in range(DEPTH):
        lam_init = 0.8 - 0.6 * math.exp(-0.3 * layer)
        params = (norm1_g[layer], w_in[layer], q_norm_g[layer], k_norm_g[layer],
                  lambda_q1[layer], lambda_k1[layer], lambda_q2[layer], lambda_k2[layer], subln_g[layer],
                  ssm_a_re[layer], ssm_a_im[layer], ssm_log_dt[layer], ssm_b_re[layer], ssm_b_im[layer],
                  ssm_c_re[layer], ssm_c_im[layer], ssm_d[layer], w_glu[layer], b_glu[layer],
                  w_out[layer], norm2_g[layer], w_peer_q[layer], peer_keys[layer],
                  peer_u[layer], peer_v[layer])
        yp, kp, vp, hrp, hip = hybrid_layer(yp, pos_p, None, None, None, None, lam_init, params)
        ys, kk, vv, hrs, his = hybrid_layer(ys, pos_s, cache_k[layer], cache_v[layer],
                                            state_ssm_re[layer], state_ssm_im[layer], lam_init, params)
        kp_l.append(kp); vp_l.append(vp); hrp_l.append(hrp); hip_l.append(hip)
        ks_l.append(kk); vs_l.append(vv); hrs_l.append(hrs); his_l.append(his)
    return (yp, ys, jnp.stack(kp_l), jnp.stack(vp_l), jnp.stack(hrp_l), jnp.stack(hip_l),
            jnp.stack(ks_l), jnp.stack(vs_l), jnp.stack(hrs_l), jnp.stack(his_l))


_drawn_inputs = setup_inputs


def setup_inputs(seed=0):
    import zlib

    import numpy as np

    out = dict(_drawn_inputs(seed))
    spreads = {}
    factors = {'q_norm_g': 2.694,
     'lambda_q1': 5.743,
     'subln_g': 8.311,
     'ssm_a_re': 47.285,
     'b_glu': 176.513,
     'norm2_g': 12.19,
     'ssm_c_re': 5.406,
     'ssm_c_im': 5.221,
     'w_glu': 2.759}
    for name, (base, spread) in spreads.items():
        noise = np.random.default_rng([zlib.crc32(name.encode()), seed]).standard_normal(out[name].shape)
        drawn = base * np.exp(spread * noise) if base else spread * noise
        out[name] = jnp.asarray(drawn.astype(out[name].dtype))
    for name, factor in factors.items():
        out[name] = (out[name] * factor).astype(out[name].dtype)
    return out
```

```python
import math

import numpy as np
import concourse.bass as bass
from concourse import mybir
from contextlib import ExitStack

F32 = mybir.dt.float32
BF16 = mybir.dt.bfloat16
U32 = mybir.dt.uint32
I32 = mybir.dt.int32
ALU = mybir.AluOpType
ACT = mybir.ActivationFunctionType
AX = mybir.AxisListType

P = 128
D = 2048
T_PROMPT, T_SAMPLE = 256, 64
T = T_PROMPT + T_SAMPLE
TILES = [(0, 128), (128, 128), (256, 64)]
NT = len(TILES)
DC = D // P
COLS = 512
BLOCK = 2048
HEADS, HD = 8, 64
PAST = 256
SSM_W, SSM_P, GROUPS, SSM_N = 1024, 16, 64, 64
GP = GROUPS // 2
STEP = 8
CH_PROMPT, CH_SAMPLE = T_PROMPT // STEP, T_SAMPLE // STEP
CH = CH_PROMPT + CH_SAMPLE
PH, PK, TOPK = 8, 128, 16
HC = 2 * PH
EPS = 1e-6
LAM_INIT = 0.8 - 0.6 * math.exp(-0.3 * 0)
SLOTS = 4
SECTIONS = 4
SEC = PK // SECTIONS
TOK = T // SEC
LOW = -3.0e38
TWO_PI = (6.28125, 0.0019350051879882812, 3.0199159819e-07)

N_IN, N_GLU, N_OUT, N_PQ = 32, 4, 16, 16
B_IN, B_GLU = 0, N_IN
B_OUT = B_GLU + N_GLU
B_PQ = B_OUT + N_OUT
B_EXP = B_PQ + N_PQ
U_BLK, V_BLK = range(2)


def build(nc, io):
    ctx = ExitStack()

    def sb(name, shape, dt=F32):
        return ctx.enter_context(nc.sbuf_tensor(name, shape, dt))

    def sem(name):
        return ctx.enter_context(nc.semaphore(name))

    with ctx:
        ARENA = 43900
        ring = sb("ring", [P, SLOTS, BLOCK])
        ident = sb("ident", [P, P])
        small = sb("small", [P, 976])
        arena = sb("arena", [P, ARENA])
        psum = ctx.enter_context(nc.psum_tensor("psum", [P, 8, COLS], F32))
        used = [0]

        def stat(*dims):
            n = math.prod(dims)
            used[0] += n
            assert used[0] <= 976, used
            r = small[:, used[0] - n:used[0]]
            return r.rearrange("p (a b) -> p a b", a=dims[0]) if len(dims) == 2 else r

        def at(word, *dims):
            n = math.prod(dims)
            assert word + n <= ARENA, (word, dims)
            r = arena[:, word:word + n]
            if len(dims) == 2:
                return r.rearrange("p (a b) -> p a b", a=dims[0])
            if len(dims) == 3:
                return r.rearrange("p (a b c) -> p a b c", a=dims[0], b=dims[1])
            return r

        def spread(ap, *shape):
            return ap.broadcast_to(list(shape))

        g1, g2 = stat(DC), stat(DC)
        iota = stat(PK)
        rope = stat(NT, 16)
        qk_g = stat(2, HD)
        sub_g = stat(2 * HD)
        h0 = stat(2 * GP)
        skip = stat(GROUPS)
        lam_in = stat(4, HD)
        ssq, var, rstd = stat(NT), stat(NT), stat(NT)
        nlam = stat(1)
        lam2 = stat(2)
        mx, nb, z, rz = stat(2, 2), stat(2, 2), stat(2, 2), stat(2, 2)
        hs, hv, hr = stat(32), stat(32), stat(32)

        xT = at(0, DC, T)
        x_tok = at(5120, NT, D)
        proj = at(5120, 4, NT, 1024)
        sq_full = at(17408, D)
        WX = [at(17408, GP, 128), at(21504, GP, 128)]
        CA = [at(25600, GP, 128), at(29696, GP, 128)]
        tmp_big = at(33792, GP, 128)
        PWR, PWI = at(37888, 9, GP), at(38176, 9, GP)
        AJR, AJI = at(38464, 8, GP), at(38720, 8, GP)
        bcin = at(38976, 4, 512)
        nci = at(41024, 512)
        prm = at(41536, 3, GP)
        sm_ = [at(41632 + 32 * i, GP) for i in range(11)]
        smi = at(41632 + 32 * 11, GP)
        k7 = at(42016, 1024)
        bbar = [at(42016, 512), at(42528, 512)]
        Tm = at(33792, STEP, 1024)
        mask = at(43040, 2, 256)
        dmask = at(43552, 16)
        qkT = at(0, 16, T)
        ckT, cv = at(5120, HEADS, PAST), at(7168, 2, 1024)
        sm = at(9216, 2, 2, T)
        wT = at(10496, 2, 3, 128)
        o_tok = at(14336, NT, 1024)
        sq_head = at(14336, 2048)
        rt = at(16384, 4, 256)
        sq_o = at(42016, 1024)
        X = at(0, STEP * 1024)
        Xg = at(10752, 2, 1024)
        UG = at(8192, GROUPS, CH)
        FS = at(10752, CH, 2 * GP)
        WTs = at(42016, 2, 512)
        HP = at(0, CH + 2, 2 * GP)
        t1, t2 = at(13312, 2, 64), at(13440, 2, 64)
        HCt = at(2688, 2 * GP, CH)
        Y = at(17408, STEP * 1024)
        y_tok = at(25600, NT, 1024)
        yT = at(28672, 8, T)
        z_tok = at(31232, NT, 1024)
        mixT = at(34304, DC, T)
        bglu = at(39424, 1024)
        x2 = at(0, NT, D)
        xn2 = at(6144, NT, D)
        xn2T = at(12288, DC, T)
        qT = at(17408, HC, T)
        keys = at(22528, D)
        sc = at(24576, NT, D)
        sc2 = at(30720, HC, PK)
        cand, cand2 = at(32768, PH, 256), at(34816, PH, 256)
        sv = at(36864, HC, TOPK)
        si = at(37120, HC * TOPK).bitcast(U32).rearrange("p (a b) -> p a b", a=HC)
        sif = at(37376, HC, TOPK)
        fv = at(37632, PH, TOPK)
        fp = at(37760, 128).bitcast(U32).rearrange("p (a b) -> p a b", a=PH)
        gate, pick_i, pick_j = at(6144, NT, 128), at(6528, NT, 128), at(6912, NT, 128)
        pa_u, pb_u = at(7296, 128).bitcast(U32), at(7424, 128).bitcast(U32)
        pa, pb = at(7552, PH, TOPK), at(7680, PH, TOPK)
        gm, gs = at(7808, PH), at(7816, PH)
        eq_k = at(7824, PH * TOPK, TOPK)
        acc = at(6144, DC, T)
        G = [at(17408, SEC, T), at(27648, SEC, T)]
        oneB = [at(37888 + 640 * i, 640).bitcast(BF16).rearrange("p (a b) -> p a b", a=TOK) for i in range(2)]
        oneA = [at(39168 + 480 * i, 480).bitcast(BF16).rearrange("p (a b) -> p a b", a=3) for i in range(2)]
        eqA = [at(40128, TOK, SEC), at(43008, TOK, SEC)]
        hg = at(40448, 2, T)
        iT, jT, gT = at(41088, T), at(41408, T), at(41728, T)
        gpart = at(42048, 480).bitcast(BF16).rearrange("p (a b) -> p a b", a=3)
        grest = at(42528, T)

        def bank(b, n=COLS):
            return psum[:, b, 0:n]

        names = """consts x0 x1 x2 ssq var std rst xn tr1 xT
            slot0 slot1 slot2 slot3 used in_mm in_out u_saved s5in
            lam_e lam s5dt s5exp s5sin s5w k7mm k7out k7st tz v_out k_out
            hvar hstd qk_ready qk_tr qkT  xg cache s_mm s_sm s_mx s_exp w_ready w_tr wT pv o_out
            ovar ostd o_ready x_in xs ug_tr ug wt_tr wt f_mm f_out hp hc h_out y_mm y_gl y_save y_in
            yT_tr yT glu_mm glu_b glu_s s_ready mix_tr mixT x_re out_mm out_x bg
            ssq2 var2 std2 xn2 tr2 xn2T keys pq_mm qT sc_mm sc_out gmx gex picks pick_tr pickT
            one gs_mm gs_out e_h e_g e_w e_o e_acc fin_tr fin y_out dve act pool rec rec1""".split()
        S = {n: sem(n) for n in names}

        def loaded(eng, block):
            eng.wait_ge(S[f"slot{block % SLOTS}"], 16 * (block // SLOTS + 1))

        class Chain:

            def __init__(self, eng, name):
                self.eng, self.sem, self.n = eng, S[name], 0

            def add(self, ins):
                self.n += 1
                ins.then_inc(self.sem, 1)

            def wait(self):
                self.eng.wait_ge(self.sem, self.n)

            def __call__(self, ins):
                self.add(ins)
                self.wait()

        block = ctx.enter_context(nc.Block())

        CONSTS = [(ident[:, :], io["ident"]), (g1, io["norm1_g"]), (g2, io["norm2_g"]),
                  (iota, io["iota"].partition_broadcast(P)), (rope, io["rope"]), (qk_g[:, 0, :], io["q_g"].partition_broadcast(P)),
                  (qk_g[:, 1, :], io["k_g"].partition_broadcast(P)), (sub_g, io["sub_g"].partition_broadcast(P)),
                  (h0[:, 0:GP], io["h0_re"]), (h0[:, GP:], io["h0_im"]), (mask, io["mask"]), (dmask, io["dmask"]),
                  (skip, io["skip"])] + [
                      (lam_in[:, i, :], io[n].partition_broadcast(P)) for i, n in enumerate(("lq1", "lq2", "lk1", "lk2"))]
        S5IN = [(prm[:, 0, :], io["a_re"]), (prm[:, 1, :], io["a_im"]), (prm[:, 2, :], io["log_dt"])] + [
            (bcin[:, i, :], io[n]) for i, n in enumerate(("b_re", "b_im", "c_re", "c_im"))]
        ALL_CONSTS = 16 * len(CONSTS)

        @block.sync
        def _(sp):
            for n, (t0, r) in enumerate(TILES):
                sp.dma_start(x_tok[0:r, n, :], io["x"][t0:t0 + r, :]).then_inc(S[f"x{n}"], 16)

            def turn(source, first, base, i, free=True):
                for s in range(SLOTS):
                    src = io[source][bass.ds(i * SLOTS + (first + s), 1)].rearrange("o p n -> (o p) n")
                    if free:
                        sp.wait_ge(S["used"], i * SLOTS + (base + s - SLOTS + 1))
                    sp.dma_start(ring[:, s, :], src).then_inc(S[f"slot{s}"], 16)

            turn("w_in", 0, B_IN, 0, free=False)
            with sp.Fori(1, N_IN // SLOTS) as i:
                turn("w_in", 0, B_IN, i)
            turn("w_glu", 0, B_GLU, 0)
            with sp.Fori(0, N_OUT // SLOTS) as i:
                turn("w_out", 0, B_OUT, i)
            with sp.Fori(0, N_PQ // SLOTS) as i:
                turn("w_pq", 0, B_PQ, i)
            for s in range(SECTIONS):
                with sp.Fori(0, SEC // SLOTS) as i:
                    turn("peer_u", s * SEC, B_EXP + 2 * s * SEC, i)
                with sp.Fori(0, SEC // SLOTS) as i:
                    turn("peer_v", s * SEC, B_EXP + (2 * s + 1) * SEC, i)
            for n, (t0, r) in enumerate(TILES):
                sp.wait_ge(S["fin"], 4 * (n + 1))
                sp.dma_start(io["y"][t0:t0 + r, :], x2[0:r, n, :]).then_inc(S["y_out"], 16)
            sp.wait_ge(S["y_out"], 16 * NT)

        @block.gpsimd
        def _(pool):
            for dst, src in S5IN:
                pool.dma_start(dst, src).then_inc(S["s5in"], 16)
            pool.wait_ge(S["in_out"], 2 * NT)
            for n, (t0, r) in enumerate(TILES):
                pool.dma_start(io["u_tmp"][t0:t0 + r, :], proj[0:r, 3, n, :]).then_inc(S["u_saved"], 16)
            pool.wait_ge(S["k7out"], 1)
            pool.memset(Tm, 0.0).then_inc(S["tz"], 1)
            pool.wait_ge(S["tz"], 1)
            for j in range(STEP):
                n = SSM_P * (j + 1)
                pool.dma_start(Tm[0:n, j, :], k7[P - n:P, :]).then_inc(S["k7st"], 16)
            pool.wait_ge(S["in_out"], 8 * NT)
            for n, (t0, r) in enumerate(TILES):
                pool.dma_start(io["v_all"][t0:t0 + r, :], proj[0:r, 2, n, :]).then_inc(S["v_out"], 16)
            pool.wait_ge(S["qk_ready"], NT)
            for n, (t0, r) in enumerate(TILES):
                pool.dma_start(io["k_all"][t0:t0 + r, :], proj[0:r, 1, n, :]).then_inc(S["k_out"], 16)
            pool.wait_ge(S["k_out"], 16 * NT)
            pool.wait_ge(S["qkT"], 12)
            pool.dma_start(ckT, io["cache_k"]).then_inc(S["cache"], 16)
            for b in range(2):
                pool.dma_start(cv[:, b, :], io["cache_v"][b * P:(b + 1) * P, :]).then_inc(S["cache"], 16)
            pool.wait_ge(S["pv"], NT * HEADS)
            pool.wait_ge(S["v_out"], 16 * NT)
            pool.wait_ge(S["u_saved"], 16 * NT)
            pool.dma_start(X[0:CH, :], io["u_tmp"].rearrange("(c i) n -> c (i n)", i=STEP)).then_inc(S["xs"], 16)
            pool.wait_ge(S["hp"], 1)
            pool.dma_start(io["states"][:, 0, :], HP[:, CH_PROMPT, :]).then_inc(S["h_out"], 16)
            pool.dma_start(io["states"][:, 1, :], HP[:, CH + 1, :]).then_inc(S["h_out"], 16)
            pool.wait_ge(S["y_gl"], 16)
            pool.dma_start(io["y_tmp"].rearrange("(c i) n -> c (i n)", i=STEP), Y[0:CH, :]).then_inc(S["y_save"], 16)
            pool.wait_ge(S["y_save"], 16)
            for n, (t0, r) in enumerate(TILES):
                pool.dma_start(y_tok[0:r, n, :], io["y_tmp"][t0:t0 + r, :]).then_inc(S["y_in"], 16)
            pool.dma_start(bglu, io["b_glu"].partition_broadcast(P)).then_inc(S["bg"], 16)
            pool.wait_ge(S["h_out"], 32)
            pool.wait_ge(S["y_mm"], 16)
            for n, (t0, r) in enumerate(TILES):
                pool.dma_start(x2[0:r, n, :], io["x"][t0:t0 + r, :]).then_inc(S["x_re"], 16)
            pool.wait_ge(S["mixT"], 12)
            pool.dma_start(keys, io["keys"]).then_inc(S["keys"], 16)

        @block.scalar
        def _(act):
            chain = Chain(act, "act")
            for dst, src in CONSTS:
                act.dma_start(dst, src).then_inc(S["consts"], 16)

            def root(source, n, var_sem, std_sem, ap):
                act.wait_ge(S[var_sem], n)
                act.activation(ap, ap, ACT.Sqrt).then_inc(S[std_sem], 1)

            for n, (t0, r) in enumerate(TILES):
                act.wait_ge(S[f"x{n}"], 16)
                act.activation(sq_full[0:r, :], x_tok[0:r, n, :], ACT.Square, accum_out=ssq[0:r, n:n + 1]).then_inc(S["ssq"], 1)
                act.wait_ge(S["ssq"], n + 1)
            for n, (t0, r) in enumerate(TILES):
                act.wait_ge(S["var"], n + 1)
                act.activation(var[0:r, n:n + 1], var[0:r, n:n + 1], ACT.Sqrt).then_inc(S["std"], 1)
            act.wait_ge(S["lam_e"], 1)
            act.activation(lam2, lam2, ACT.Exp).then_inc(S["lam"], 1)
            act.wait_ge(S["s5in"], 16 * len(S5IN))
            act.activation(prm[:, 2, :], prm[:, 2, :], ACT.Exp).then_inc(S["s5exp"], 1)
            act.wait_ge(S["s5dt"], 1)
            act.activation(sm_[0], sm_[0], ACT.Exp).then_inc(S["s5exp"], 1)
            act.wait_ge(S["s5dt"], 2)
            act.activation(sm_[1], sm_[1], ACT.Sin).then_inc(S["s5sin"], 1)
            act.activation(sm_[2], sm_[2], ACT.Sin).then_inc(S["s5sin"], 1)

            def evac_in(i, kind):
                for c2 in range(2):
                    for n, (t0, r) in enumerate(TILES):
                        dst = proj[0:r, bass.ds(kind, 1), n, c2 * COLS:(c2 + 1) * COLS].rearrange("p o n -> p (o n)")
                        act.wait_ge(S["in_mm"], i * (2 * NT) + (c2 * NT + n + 1))
                        act.activation(dst, psum[0:r, 3 * c2 + n, :], ACT.Copy).then_inc(S["in_out"], 1)

            evac_in(0, 3)
            with act.Fori(1, 4) as i:
                evac_in(i, i - 1)

            for n, (t0, r) in enumerate(TILES):
                act.wait_ge(S["hvar"], n + 1)
                act.activation(hv[0:r, :], hv[0:r, :], ACT.Sqrt).then_inc(S["hstd"], 1)
            for n, (t0, r) in enumerate(TILES):
                for j in range(4):
                    act.wait_ge(S["qk_tr"], 4 * n + j + 1)
                    act.activation(qkT[:, 4 * j:4 * j + 4, t0:t0 + r],
                                   bank((4 * n + j) % 8).rearrange("p (a b) -> p a b", a=4)[:, :, 0:r], ACT.Copy).then_inc(S["qkT"], 1)
            keys_of = [128, 256, 320]

            def weights_T(u):
                n, h = divmod(u, HEADS)
                r, kk = TILES[n][1], keys_of[n]
                act.wait_ge(S["w_tr"], u + 1)
                if u >= 2:
                    act.wait_ge(S["pv"], u - 1)
                full = kk // P
                src = bank(4 + u % 2).rearrange("p (a b) -> p a b", a=4)
                act.activation(wT[:, u % 2, 0:full, 0:r], src[:, 0:full, 0:r], ACT.Copy).then_inc(S["wT"], 1)
                if kk % P:
                    act.activation(wT[0:64, u % 2, full, 0:r], src[0:64, full, 0:r], ACT.Copy).then_inc(S["wT"], 1)
                else:
                    act.sem_inc(S["wT"], 1)

            for u in range(NT * HEADS):
                n, h = divmod(u, HEADS)
                r, kk = TILES[n][1], keys_of[n]
                for c in range(2):
                    act.wait_ge(S["s_mx"], u + 1)
                    act.activation(sm[0:r, u % 2, c, 0:kk], sm[0:r, u % 2, c, 0:kk], ACT.Exp,
                                   bias=nb[0:r, u % 2, c:c + 1], scale=HD ** -0.5,
                                   accum_out=z[0:r, u % 2, c:c + 1]).then_inc(S["s_exp"], 1)
                if u:
                    weights_T(u - 1)
            weights_T(NT * HEADS - 1)
            for n, (t0, r) in enumerate(TILES):
                act.wait_ge(S["ovar"], n + 1)
                act.activation(hv[0:r, 0:HEADS], hv[0:r, 0:HEADS], ACT.Sqrt).then_inc(S["ostd"], 1)

            for k in range(8):
                act.wait_ge(S["ug_tr"], k + 1)
                act.activation(UG[:, 8 * k:8 * k + 8, :], bank(k, 320).rearrange("p (a b) -> p a b", a=8), ACT.Copy).then_inc(S["ug"], 1)
            for q in range(16):
                act.wait_ge(S["wt_tr"], q + 1)
                if q >= 2:
                    act.wait_ge(S["f_mm"], q - 1)
                act.activation(WTs[:, q % 2, :], bank(6 + q % 2), ACT.Copy).then_inc(S["wt"], 1)
            for q in range(16):
                act.wait_ge(S["y_mm"], q + 1)
                dst = Y[0:CH, :].rearrange("p (j g n) -> p g j n", j=STEP, g=GROUPS)
                for g4 in range(4):
                    ins = act.activation(dst[:, 8 * (q // 2) + 2 * g4 + q % 2], psum[0:CH, q % 8, 128 * g4:128 * g4 + 128].rearrange("p (j n) -> p j n", j=STEP),
                                         ACT.Gelu_apprx_tanh)
                ins.then_inc(S["y_gl"], 1)
            for n, (t0, r) in enumerate(TILES):
                for j in range(2):
                    act.wait_ge(S["yT_tr"], 2 * n + j + 1)
                    act.activation(yT[:, 4 * j:4 * j + 4, t0:t0 + r],
                                   bank(2 * n + j).rearrange("p (a b) -> p a b", a=4)[:, :, 0:r], ACT.Copy).then_inc(S["yT"], 1)
            for c in range(2):
                for n, (t0, r) in enumerate(TILES):
                    act.wait_ge(S["glu_b"], 3 * c + n + 1)
                    zz = z_tok[0:r, n, c * COLS:(c + 1) * COLS]
                    act.activation(zz, zz, ACT.Sigmoid).then_inc(S["glu_s"], 1)
            for n, (t0, r) in enumerate(TILES):
                for j in range(4):
                    act.wait_ge(S["mix_tr"], 4 * n + j + 1)
                    act.activation(mixT[:, 4 * j:4 * j + 4, t0:t0 + r],
                                   bank((4 * n + j) % 8).rearrange("p (a b) -> p a b", a=4)[:, :, 0:r], ACT.Copy).then_inc(S["mixT"], 1)

            for n, (t0, r) in enumerate(TILES):
                act.wait_ge(S["out_x"], 9 + n + 1)
                act.activation(xn2[0:r, n, :], x2[0:r, n, :], ACT.Square, accum_out=ssq[0:r, n:n + 1]).then_inc(S["ssq2"], 1)
                act.wait_ge(S["ssq2"], n + 1)
            for n, (t0, r) in enumerate(TILES):
                act.wait_ge(S["var2"], n + 1)
                act.activation(var[0:r, n:n + 1], var[0:r, n:n + 1], ACT.Sqrt).then_inc(S["std2"], 1)
            for c in range(4):
                for k in range(4):
                    act.wait_ge(S["pq_mm"], 4 * c + k + 1)
                    act.activation(qT[:, 4 * c + k, :], bank(4 * (c % 2) + k, T), ACT.Copy).then_inc(S["qT"], 1)
            for n, (t0, r) in enumerate(TILES):
                for k in range(4):
                    act.wait_ge(S["sc_mm"], 4 * n + k + 1)
                    act.activation(sc[0:r, n, COLS * k:COLS * (k + 1)], psum[0:r, (4 * n + k) % 8, :], ACT.Copy).then_inc(S["sc_out"], 1)
            for n, (t0, r) in enumerate(TILES):
                act.wait_ge(S["gmx"], n + 1)
                act.activation(gate[0:r, n, :], gate[0:r, n, :], ACT.Exp).then_inc(S["gex"], 1)

            def gates_out(sec, i, k):
                dst = G[sec % 2][:, :, bass.ds(i * (4 * TOK) + k * TOK, TOK)].rearrange("p i t -> p t i")
                act.wait_ge(S["gs_mm"], i * 4 + (SEC * sec + k + 1))
                act.activation(dst, bank(2 + k % 2, TOK * SEC).rearrange("p (t i) -> p t i", t=TOK), ACT.Copy).then_inc(S["gs_out"], 1)

            with act.Fori(0, SEC // 4) as i:
                for k in range(4):
                    gates_out(0, i, k)
            for s in range(SECTIONS):
                def experts(i, wait_w):
                    for k in range(4):
                        act.wait_ge(S["e_h"], i * 4 + (SEC * s + k + 1))
                        if wait_w or k >= 2:
                            act.wait_ge(S["e_w"], i * 4 + (SEC * s + k - 1))
                        act.activation(hg[:, k % 2, :], bank(k % 2, T), ACT.Gelu_apprx_tanh).then_inc(S["e_g"], 1)
                        if s + 1 < SECTIONS:
                            gates_out(s + 1, i, k)
                if s == 0:
                    experts(0, False)
                with act.Fori(1 if s == 0 else 0, SEC // 4) as i:
                    experts(i, True)

        @block.vector
        def _(dve):
            chain = Chain(dve, "dve")

            def tt(out, a, b, op):
                return dve.tensor_tensor(out, a, b, op)

            def var_of(dst, src, n):
                return dve.tensor_scalar(dst, src, 1.0 / n, EPS, ALU.mult, ALU.add)

            def norm_rows(src, dst, ssq_s, var_s, std_s, xn_s):
                for n, (t0, r) in enumerate(TILES):
                    dve.wait_ge(S[ssq_s], n + 1)
                    var_of(var[0:r, n:n + 1], ssq[0:r, n:n + 1], D).then_inc(S[var_s], 1)
                for n, (t0, r) in enumerate(TILES):
                    dve.wait_ge(S[std_s], n + 1)
                    chain(dve.reciprocal(rstd[0:r, n:n + 1], var[0:r, n:n + 1]))
                    dve.tensor_scalar(dst[0:r, n, :], src[0:r, n, :], rstd[0:r, n:n + 1], None, ALU.mult).then_inc(S[xn_s], 1)

            def gain_out(dst, gain, tr_s, out_s):
                for n, (t0, r) in enumerate(TILES):
                    for j in range(4):
                        dve.wait_ge(S[tr_s], 4 * n + j + 1)
                        tt(dst[:, 4 * j:4 * j + 4, t0:t0 + r],
                           bank((4 * n + j) % 8).rearrange("p (a b) -> p a b", a=4)[:, :, 0:r],
                           spread(gain[:, 4 * j:4 * j + 4].unsqueeze(2), P, 4, r), ALU.mult).then_inc(S[out_s], 1)

            norm_rows(x_tok, x_tok, "ssq", "var", "std", "xn")
            dve.wait_ge(S["consts"], ALL_CONSTS)
            gain_out(xT, g1, "tr1", "xT")

            chain(tt(lam_in[:, 0:2, :], lam_in[:, 0:2, :], lam_in[:, 2:4, :], ALU.mult))
            dve.tensor_reduce(lam2, lam_in[:, 0:2, :], AX.X, ALU.add).then_inc(S["lam_e"], 1)
            dve.wait_ge(S["lam"], 1)
            chain(tt(nlam, lam2[:, 1:2], lam2[:, 0:1], ALU.subtract))
            chain(dve.tensor_scalar(nlam, nlam, -LAM_INIT, None, ALU.add))

            are, aim, dt = prm[:, 0, :], prm[:, 1, :], prm[:, 2, :]
            mag, half, full = sm_[0], sm_[1], sm_[2]
            ang, cosv, den, nr, cr, ci, ta, tb = sm_[3:11]
            dve.wait_ge(S["s5exp"], 1)
            tt(mag, dt, are, ALU.mult).then_inc(S["s5dt"], 1)
            chain(tt(ang, dt, aim, ALU.mult))
            chain(dve.tensor_scalar(ta, ang, 1.0 / (2 * math.pi), None, ALU.mult))
            chain(dve.tensor_copy(smi.bitcast(I32), ta))
            chain(dve.tensor_copy(tb, smi.bitcast(I32)))
            for part in TWO_PI:
                chain(dve.scalar_tensor_tensor(ang, tb, -part, ang, ALU.mult, ALU.add))
            chain(dve.tensor_scalar(full, ang, 3.1415925, -3.1415925, ALU.min, ALU.max))
            dve.tensor_scalar(half, ang, 0.5, None, ALU.mult).then_inc(S["s5dt"], 1)
            dve.wait_ge(S["s5exp"], 2)
            dve.wait_ge(S["s5sin"], 2)
            chain(tt(cosv, half, half, ALU.mult))
            chain(dve.tensor_scalar(cosv, cosv, -2.0, 1.0, ALU.mult, ALU.add))
            chain(dve.memset(PWR[:, 8, :], 1.0))
            chain(dve.memset(PWI[:, 8, :], 0.0))
            chain(tt(AJR[:, 0, :], mag, cosv, ALU.mult))
            chain(tt(AJI[:, 0, :], mag, full, ALU.mult))
            chain(tt(den, are, are, ALU.mult))
            chain(tt(ta, aim, aim, ALU.mult))
            chain(tt(den, den, ta, ALU.add))
            chain(dve.reciprocal(den, den))
            chain(dve.tensor_scalar(nr, AJR[:, 0, :], -1.0, None, ALU.add))
            chain(tt(cr, nr, are, ALU.mult))
            chain(tt(ta, AJI[:, 0, :], aim, ALU.mult))
            chain(tt(cr, cr, ta, ALU.add))
            chain(tt(cr, cr, den, ALU.mult))
            chain(tt(ci, AJI[:, 0, :], are, ALU.mult))
            chain(tt(ta, nr, aim, ALU.mult))
            chain(tt(ci, ci, ta, ALU.subtract))
            chain(tt(ci, ci, den, ALU.mult))

            def times(outr, outi, ar, ai, br, bi, tmp):
                chain(tt(outr, ar, br, ALU.mult))
                chain(tt(tmp, ai, bi, ALU.mult))
                chain(tt(outr, outr, tmp, ALU.subtract))
                chain(tt(outi, ar, bi, ALU.mult))
                chain(tt(tmp, ai, br, ALU.mult))
                chain(tt(outi, outi, tmp, ALU.add))

            for k in (1, 2, 4):
                shape = (P, k, GP)
                by = (spread(AJR[:, k - 1:k, :], *shape), spread(AJI[:, k - 1:k, :], *shape))
                scr = tmp_big[:, 0:1, :].rearrange("p a b -> p (a b)")[:, 0:k * GP].rearrange("p (a b) -> p a b", a=k)
                times(AJR[:, k:2 * k, :], AJI[:, k:2 * k, :], AJR[:, 0:k, :], AJI[:, 0:k, :], *by, scr)
            for k in range(1, 9):
                chain(dve.tensor_copy(PWR[:, 8 - k, :], AJR[:, k - 1, :]))
                chain(dve.tensor_copy(PWI[:, 8 - k, :], AJI[:, k - 1, :]))
            def per_channel(ap):
                return spread(ap.unsqueeze(2), P, GP, SSM_P)

            def grp(ap):
                return ap.rearrange("p (g n) -> p g n", g=GP)

            times(grp(bbar[0]), grp(bbar[1]), per_channel(cr), per_channel(ci), grp(bcin[:, 0, :]), grp(bcin[:, 1, :]),
                  grp(tmp_big.rearrange("p a b -> p (a b)")[:, 0:512]))

            four = (P, GP, STEP, SSM_P)

            def cols(ap):
                return ap.rearrange("p g (j n) -> p g j n", j=STEP)

            def steps(ap):
                return spread(ap.rearrange("p j g -> p g j").unsqueeze(3), *four)

            def chans(ap):
                return spread(grp(ap).unsqueeze(2), *four)

            qr, qi, br, bi = steps(PWR[:, 1:9, :]), steps(PWI[:, 1:9, :]), chans(bbar[0]), chans(bbar[1])
            chain(tt(cols(WX[0]), qr, br, ALU.mult))
            chain(tt(cols(CA[0]), qi, bi, ALU.mult))
            chain(tt(WX[0], WX[0], CA[0], ALU.subtract))
            chain(tt(cols(WX[1]), qr, bi, ALU.mult))
            chain(tt(cols(CA[1]), qi, br, ALU.mult))
            chain(tt(WX[1], WX[1], CA[1], ALU.add))
            chain(dve.tensor_scalar(nci, bcin[:, 3, :], -1.0, None, ALU.mult))
            dve.sem_inc(S["s5w"], 1)
            rr, ri, cre, cim, ncim = steps(AJR), steps(AJI), chans(bcin[:, 2, :]), chans(bcin[:, 3, :]), chans(nci)
            chain(tt(cols(CA[0]), rr, cre, ALU.mult))
            chain(tt(cols(tmp_big), ri, cim, ALU.mult))
            chain(tt(CA[0], CA[0], tmp_big, ALU.subtract))
            chain(tt(cols(CA[1]), rr, ncim, ALU.mult))
            chain(tt(cols(tmp_big), ri, cre, ALU.mult))
            chain(tt(CA[1], CA[1], tmp_big, ALU.subtract))
            a8 = lam_in.rearrange("p a b -> p (a b)")
            a8r, a8n = a8[:, 0:64], a8[:, 64:128]
            chain(dve.tensor_copy(a8r[:, 0:32], AJR[:, 7, :]))
            chain(dve.tensor_copy(a8r[:, 32:64], AJR[:, 7, :]))
            chain(dve.tensor_scalar(a8n[:, 0:32], AJI[:, 7, :], -1.0, None, ALU.mult))
            chain(dve.tensor_copy(a8n[:, 32:64], AJI[:, 7, :]))
            dve.sem_inc(S["s5w"], 1)
            dprod = tmp_big.rearrange("p a b -> p (a b)")[:, 0:1024].rearrange("p (g n) -> p g n", g=GROUPS)
            chain(tt(dprod, spread(skip.unsqueeze(2), P, GROUPS, SSM_P), spread(dmask.unsqueeze(1), P, GROUPS, SSM_P), ALU.mult))
            dve.wait_ge(S["k7mm"], 1)
            for b in range(2):
                chain(tt(k7.rearrange("p (g c n) -> p c g n", c=2, n=SSM_P)[:, b], bank(6 + b).rearrange("p (g n) -> p g n", g=GP),
                         dprod.rearrange("p (g c) n -> p c g n", c=2)[:, b], ALU.add))
            dve.sem_inc(S["k7out"], 1)

            dve.wait_ge(S["in_out"], 8 * NT)
            dve.wait_ge(S["u_saved"], 16 * NT)
            for n, (t0, r) in enumerate(TILES):
                v = proj[0:r, 0:2, n, :].rearrange("p k (h d) -> p k h d", d=HD)
                sq = sq_head[0:r, :].rearrange("p (k h d) -> p k h d", k=2, d=HD)
                heads = (r, 2, 16, HD)

                def per_head(ap):
                    return spread(ap[0:r, :].rearrange("p (k h) -> p k h", k=2).unsqueeze(3), *heads)

                chain(tt(sq, v, v, ALU.mult))
                chain(dve.tensor_reduce(hs[0:r, :], sq_head[0:r, :].rearrange("p (g d) -> p g d", d=HD), AX.X, ALU.add))
                var_of(hv[0:r, :], hs[0:r, :], HD).then_inc(S["hvar"], 1)
                dve.wait_ge(S["hstd"], n + 1)
                chain(dve.reciprocal(hr[0:r, :], hv[0:r, :]))
                chain(tt(v, v, per_head(hr), ALU.mult))
                chain(tt(v, v, spread(qk_g[0:r].unsqueeze(2), *heads), ALU.mult))
                half = (r, 2, 16, 8)
                a, b = v[:, :, :, 0:8], v[:, :, :, 8:16]
                cosr = spread(rope[0:r, n, 0:8].unsqueeze(1).unsqueeze(1), *half)
                sinr = spread(rope[0:r, n, 8:16].unsqueeze(1).unsqueeze(1), *half)
                m = [rt[0:r, k, :].rearrange("p (k h d) -> p k h d", k=2, d=8) for k in range(4)]
                for k, (e, f) in enumerate(((a, cosr), (b, sinr), (b, cosr), (a, sinr))):
                    chain(tt(m[k], e, f, ALU.mult))
                chain(tt(a, m[0], m[1], ALU.subtract))
                chain(tt(b, m[2], m[3], ALU.add))
                dve.sem_inc(S["qk_ready"], 1)

            keys_of = [128, 256, 320]

            def scores(u):
                n, h = divmod(u, HEADS)
                r, kk, b = TILES[n][1], keys_of[n], u % 2
                dve.wait_ge(S["s_mm"], u + 1)
                if u >= 2:
                    dve.wait_ge(S["w_tr"], u - 1)
                dst, src = sm[0:r, b, :, 0:kk], psum[0:r, 2 * b:2 * b + 2, 0:kk]
                if n < 2:
                    tt(dst, src, spread(mask[0:r, n:n + 1, 0:kk], r, 2, kk), ALU.add).then_inc(S["s_sm"], 1)
                else:
                    dve.tensor_copy(dst, src).then_inc(S["s_sm"], 1)
                dve.wait_ge(S["s_sm"], u + 1)
                chain(dve.tensor_reduce(mx[0:r, b, :], dst, AX.X, ALU.max))
                dve.tensor_scalar(nb[0:r, b, :], mx[0:r, b, :], -HD ** -0.5, None, ALU.mult).then_inc(S["s_mx"], 1)

            def weights(u):
                n, h = divmod(u, HEADS)
                r, kk, b = TILES[n][1], keys_of[n], u % 2
                dve.wait_ge(S["s_exp"], 2 * (u + 1))
                chain(dve.reciprocal(rz[0:r, b, :], z[0:r, b, :]))
                chain(tt(rz[0:r, b, 1:2], rz[0:r, b, 1:2], nlam[0:r], ALU.mult))
                chain(dve.tensor_scalar(sm[0:r, b, 0, 0:kk], sm[0:r, b, 0, 0:kk], rz[0:r, b, 0:1], None, ALU.mult))
                dve.scalar_tensor_tensor(sm[0:r, b, 0, 0:kk], sm[0:r, b, 1, 0:kk], rz[0:r, b, 1:2], sm[0:r, b, 0, 0:kk],
                                         ALU.mult, ALU.add).then_inc(S["w_ready"], 1)

            def head_out(u):
                n, h = divmod(u, HEADS)
                r = TILES[n][1]
                dve.wait_ge(S["pv"], u + 1)
                dve.tensor_copy(o_tok[0:r, n, 128 * h:128 * h + 128], psum[0:r, 6 + u % 2, 0:128]).then_inc(S["o_out"], 1)

            units = NT * HEADS
            for u in range(units + 2):
                if u < units:
                    scores(u)
                if 1 <= u <= units:
                    weights(u - 1)
                if u >= 2:
                    head_out(u - 2)
            dve.wait_ge(S["o_out"], units)
            dve.wait_ge(S["k7st"], 16 * STEP)
            for n, (t0, r) in enumerate(TILES):
                o = o_tok[0:r, n, :].rearrange("p (h d) -> p h d", h=HEADS)
                sq = sq_o[0:r, :].rearrange("p (h d) -> p h d", h=HEADS)
                chain(tt(sq, o, o, ALU.mult))
                chain(dve.tensor_reduce(hs[0:r, 0:HEADS], sq, AX.X, ALU.add))
                var_of(hv[0:r, 0:HEADS], hs[0:r, 0:HEADS], 2 * HD).then_inc(S["ovar"], 1)
                dve.wait_ge(S["ostd"], n + 1)
                chain(dve.reciprocal(hr[0:r, 0:HEADS], hv[0:r, 0:HEADS]))
                chain(dve.tensor_scalar(hr[0:r, 0:HEADS], hr[0:r, 0:HEADS], 1.0 - LAM_INIT, None, ALU.mult))
                chain(tt(o, o, spread(hr[0:r, 0:HEADS].unsqueeze(2), r, HEADS, 2 * HD), ALU.mult))
                tt(o, o, spread(sub_g[0:r].unsqueeze(1), r, HEADS, 2 * HD), ALU.mult).then_inc(S["o_ready"], 1)

            dve.wait_ge(S["xs"], 16)
            Xv = X[0:CH, :].rearrange("p (i g n) -> p g i n", i=STEP, g=GROUPS)
            for k in range(8):
                if k >= 2:
                    dve.wait_ge(S["ug_tr"], k - 1)
                dve.tensor_copy(Xg[0:CH, k % 2, :].rearrange("p (g i n) -> p g i n", g=8, i=STEP), Xv[:, 8 * k:8 * k + 8]).then_inc(S["xg"], 1)
            dve.wait_ge(S["f_mm"], 16)
            for ri in range(2):
                for b in range(3):
                    k = min(12, GP - 12 * b)
                    chain(dve.tensor_copy(FS[:, :, 32 * ri + 12 * b:32 * ri + 12 * b + k].rearrange("p c g -> p g c"),
                                          bank(3 * ri + b, 40 * k).rearrange("p (g c) -> p g c", g=k)))
            dve.sem_inc(S["f_out"], 1)
            chain(dve.memset(HP[:, 0, :], 0.0))
            chain(dve.tensor_copy(HP[:, CH_PROMPT + 1, :], h0))

            def chunk(i, old, new, add, k):
                a8rs, u1, u2 = spread(a8r.unsqueeze(1), P, k, 64), t1[:, 0:k, :], t2[:, 0:k, :]
                tt(u1, old, a8rs, ALU.mult).then_inc(S["rec"], 1)
                tt(u2[:, :, 0:GP], old[:, :, GP:], spread(a8n[:, 0:GP].unsqueeze(1), P, k, GP), ALU.mult).then_inc(S["rec"], 1)
                tt(u2[:, :, GP:], old[:, :, 0:GP], spread(a8n[:, GP:].unsqueeze(1), P, k, GP), ALU.mult).then_inc(S["rec"], 1)
                dve.wait_ge(S["rec"], i * 5 + 3)
                tt(u1, u1, u2, ALU.add).then_inc(S["rec"], 1)
                dve.wait_ge(S["rec"], i * 5 + 4)
                tt(new, u1, add, ALU.add).then_inc(S["rec"], 1)
                dve.wait_ge(S["rec"], i * 5 + 5)

            off = CH_PROMPT + 1
            for i in range(CH_SAMPLE):
                chunk(i, HP[:, i:i + off + 1:off, :], HP[:, i + 1:i + off + 2:off, :],
                      FS[:, i:i + CH_PROMPT + 1:CH_PROMPT, :], 2)
            with dve.Fori(CH_SAMPLE, CH_PROMPT) as i:
                chunk(i, HP[:, bass.ds(i, 1), :], HP[:, bass.ds(i + 1, 1), :], FS[:, bass.ds(i, 1), :], 1)
            dve.sem_inc(S["hp"], 1)
            dve.tensor_copy(HCt[:, :, 0:CH_PROMPT], HP[:, 0:CH_PROMPT, :].rearrange("p c x -> p x c")).then_inc(S["hc"], 1)
            dve.tensor_copy(HCt[:, :, CH_PROMPT:], HP[:, off:off + CH_SAMPLE, :].rearrange("p c x -> p x c")).then_inc(S["hc"], 1)

            dve.wait_ge(S["bg"], 16)
            for c in range(2):
                for n, (t0, r) in enumerate(TILES):
                    dve.wait_ge(S["glu_mm"], 3 * c + n + 1)
                    cc = slice(c * COLS, (c + 1) * COLS)
                    tt(z_tok[0:r, n, cc], psum[0:r, 3 * c + n, :], bglu[0:r, cc], ALU.add).then_inc(S["glu_b"], 1)
            dve.wait_ge(S["y_in"], 16 * NT)
            dve.wait_ge(S["glu_s"], 2 * NT)
            for n, (t0, r) in enumerate(TILES):
                tt(z_tok[0:r, n, :], z_tok[0:r, n, :], y_tok[0:r, n, :], ALU.mult).then_inc(S["s_ready"], 1)
            dve.wait_ge(S["x_re"], 16 * NT)
            for c in range(4):
                for n, (t0, r) in enumerate(TILES):
                    dve.wait_ge(S["out_mm"], 3 * c + n + 1)
                    xx = x2[0:r, n, c * COLS:(c + 1) * COLS]
                    tt(xx, psum[0:r, 3 * (c % 2) + n, :], xx, ALU.add).then_inc(S["out_x"], 1)

            norm_rows(x2, xn2, "ssq2", "var2", "std2", "xn2")
            gain_out(xn2T, g2, "tr2", "xn2T")

            def top16(rows, values, value_of, index_of, rest_of, count):
                for k in range(count):
                    chain.add(dve.max(value_of(k)[:, 0:8], values(k)))
                chain.wait()
                for k in range(count):
                    chain.add(dve.max_index(index_of(k)[:, 0:8], value_of(k)[:, 0:8], values(k)))
                    chain.add(dve.match_replace(rest_of(k), value_of(k)[:, 0:8], values(k), LOW))
                chain.wait()
                for k in range(count):
                    chain.add(dve.max(value_of(k)[:, 8:16], rest_of(k)))
                chain.wait()
                for k in range(count):
                    chain.add(dve.max_index(index_of(k)[:, 8:16], value_of(k)[:, 8:16], rest_of(k)))
                chain.wait()

            for n, (t0, r) in enumerate(TILES):
                dve.wait_ge(S["sc_out"], 4 * (n + 1))
                top16(r, lambda k: sc[0:r, n, PK * k:PK * (k + 1)], lambda k: sv[0:r, k, :], lambda k: si[0:r, k, :],
                      lambda k: sc2[0:r, k, :], HC)
                chain(dve.tensor_copy(sif[0:r], si[0:r]))
                four = (r, PH, TOPK, TOPK)
                s4 = sv[0:r].rearrange("p (h c) k -> p h c k", c=2)
                f4 = sif[0:r].rearrange("p (h c) k -> p h c k", c=2)
                chain(tt(cand[0:r].rearrange("p h (a b) -> p h a b", a=TOPK), spread(s4[:, :, 0, :].unsqueeze(3), *four),
                         spread(s4[:, :, 1, :].unsqueeze(2), *four), ALU.add))
                top16(r, lambda k: cand[0:r, k, :], lambda k: fv[0:r, k, :], lambda k: fp[0:r, k, :],
                      lambda k: cand2[0:r, k, :], PH)
                tt(gate[0:r, n, :].rearrange("p (h k) -> p h k", h=PH), fv[0:r], spread(fv[0:r, :, 0:1], r, PH, TOPK),
                   ALU.subtract).then_inc(S["gmx"], 1)
                fpu = fp[0:r].rearrange("p h k -> p (h k)")
                chain(dve.tensor_scalar(pa_u[0:r], fpu, 4, None, ALU.logical_shift_right))
                chain(dve.tensor_scalar(pb_u[0:r], fpu, 15, None, ALU.bitwise_and))
                for c, (pu, pf, pick) in enumerate(((pa_u, pa, pick_i), (pb_u, pb, pick_j))):
                    flat = pf[0:r].rearrange("p h k -> p (h k)")
                    chain(dve.tensor_copy(flat, pu[0:r]))
                    chain(tt(eq_k[0:r], spread(iota[0:r, 0:TOPK].unsqueeze(1), r, PH * TOPK, TOPK),
                             spread(flat.unsqueeze(2), r, PH * TOPK, TOPK), ALU.is_equal))
                    e4 = eq_k[0:r].rearrange("p (h k) a -> p h k a", h=PH)
                    chain(tt(e4, e4, spread(f4[:, :, c, :].unsqueeze(2), *four), ALU.mult))
                    chain(dve.tensor_reduce(pick[0:r, n, :], eq_k[0:r], AX.X, ALU.add))
                dve.wait_ge(S["gex"], n + 1)
                g3 = gate[0:r, n, :].rearrange("p (h k) -> p h k", h=PH)
                chain(dve.tensor_reduce(gs[0:r], g3, AX.X, ALU.add))
                chain(dve.reciprocal(gs[0:r], gs[0:r]))
                tt(g3, g3, spread(gs[0:r].unsqueeze(2), r, PH, TOPK), ALU.mult).then_inc(S["picks"], 1)
            for n, (t0, r) in enumerate(TILES):
                dve.wait_ge(S["pick_tr"], n + 1)
                for k, dst in enumerate((gT, iT, jT)):
                    chain(dve.tensor_copy(dst[:, t0:t0 + r], psum[:, n, 128 * k:128 * k + r]))
            chain(dve.tensor_copy(gpart[:, 0, :], gT))
            chain(tt(grest, gT, gpart[:, 0, :], ALU.subtract))
            chain(dve.tensor_copy(gpart[:, 1, :], grest))
            chain(tt(grest, grest, gpart[:, 1, :], ALU.subtract))
            chain(dve.tensor_copy(gpart[:, 2, :], grest))

            def one_hots(sec, i, k, free=True):
                tok = bass.ds(i * (4 * TOK) + k * TOK, TOK)
                base = SEC * sec + k
                if free:
                    dve.wait_ge(S["gs_mm"], i * 4 + (base - 1))
                keys_i = iota[:, SEC * sec:SEC * (sec + 1)]
                tt(eqA[k % 2], spread(keys_i.unsqueeze(1), P, TOK, SEC), spread(iT[:, tok].unsqueeze(2), P, TOK, SEC),
                   ALU.is_equal).then_inc(S["rec1"], 1)
                tt(oneB[k % 2], spread(iota.unsqueeze(1), P, TOK, PK), spread(jT[:, tok].unsqueeze(2), P, TOK, PK),
                   ALU.is_equal).then_inc(S["one"], 1)
                dve.wait_ge(S["rec1"], i * 4 + (base + 1))
                tt(oneA[k % 2].rearrange("p c (t i) -> p c t i", t=TOK), spread(eqA[k % 2].unsqueeze(1), P, 3, TOK, SEC),
                   spread(gpart[:, :, tok].unsqueeze(3), P, 3, TOK, SEC), ALU.mult).then_inc(S["one"], 1)

            for k in range(4):
                one_hots(0, 0, k, k >= 2)
            with dve.Fori(1, SEC // 4) as i:
                for k in range(4):
                    one_hots(0, i, k)
            for s in range(SECTIONS):
                dve.wait_ge(S["gs_out"], SEC * (s + 1))
                with dve.Fori(0, SEC // 4) as i:
                    for k in range(4):
                        if s + 1 < SECTIONS:
                            one_hots(s + 1, i, k)
                        dve.wait_ge(S["e_g"], i * 4 + (SEC * s + k + 1))
                        g = G[s % 2][:, bass.ds(i * 4 + k, 1), :].rearrange("p o t -> p (o t)")
                        tt(g, g, hg[:, k % 2, :], ALU.mult).then_inc(S["e_w"], 1)
                for half in range(2):
                    for k in range(8):
                        dve.wait_ge(S["e_o"], 8 * (2 * s + half) + k + 1)
                        a = acc[:, 8 * half + k, :]
                        if s == 0:
                            dve.tensor_copy(a, bank(k, T)).then_inc(S["e_acc"], 1)
                        else:
                            tt(a, bank(k, T), a, ALU.add).then_inc(S["e_acc"], 1)
            for n, (t0, r) in enumerate(TILES):
                for j in range(4):
                    dve.wait_ge(S["fin_tr"], 4 * n + j + 1)
                    xx = x2[0:r, n, COLS * j:COLS * (j + 1)]
                    tt(xx, psum[0:r, (4 * n + j) % 8, :], xx, ALU.add).then_inc(S["fin"], 1)

        @block.tensor
        def _(pe):
            def transposes(src_of, ready, tr, out, quads, extra=0):
                for n, (t0, r) in enumerate(TILES):
                    pe.wait_ge(S[ready], n + 1)
                    for j in range(quads):
                        m = quads * n + j
                        if m >= 8:
                            pe.wait_ge(S[out], m - 7)
                        for k in range(4):
                            ins = pe.transpose(psum[:, m % 8, 128 * k:128 * k + r], src_of(n, r, 4 * j + k), ident[0:r, 0:r])
                        ins.then_inc(S[tr], 1)

            def dense(i, g0, per_chunk, chunks, lhs, mm, out, first=False):
                for c in range(chunks):
                    for b in range(per_chunk):
                        g = c * per_chunk + b
                        s = (g0 + g) % SLOTS
                        pe.wait_ge(S[f"slot{s}"], i * (16 * chunks * per_chunk // SLOTS) + 16 * ((g0 + g) // SLOTS + 1))
                        for d in range(4):
                            dc = 4 * b + d
                            for n, (t0, r) in enumerate(TILES):
                                if dc == 0 and not (first and c < 2):
                                    pe.wait_ge(S[out], i * (NT * chunks) + (NT * (c - 2) + n + 1))
                                ins = pe.matmul(psum[0:r, 3 * (c % 2) + n, :], lhs[:, dc, t0:t0 + r],
                                                ring[:, s, COLS * d:COLS * (d + 1)], start=dc == 0, stop=dc == 4 * per_chunk - 1)
                                if dc == 4 * per_chunk - 1:
                                    if n < NT - 1:
                                        ins.then_inc(S[mm], 1)
                        if b < per_chunk - 1:
                            ins.then_inc(S["used"], 1)
                        else:
                            ins.then_inc(S[mm], 1)
                            pe.wait_ge(S[mm], i * (NT * chunks) + NT * (c + 1))
                            pe.sem_inc(S["used"], 1)

            pe.wait_ge(S["consts"], ALL_CONSTS)
            transposes(lambda n, r, dc: x_tok[0:r, n, 128 * dc:128 * (dc + 1)], "xn", "tr1", "xT", 4)
            pe.wait_ge(S["xT"], 12)
            dense(0, B_IN, 4, 2, xT, "in_mm", "in_out", first=True)
            with pe.Fori(1, 4) as i:
                dense(i, B_IN, 4, 2, xT, "in_mm", "in_out")

            pe.wait_ge(S["s5w"], 2)
            for g in range(GROUPS):
                pr, gp = slice(64 * (g % 2), 64 * (g % 2) + 64), g // 2
                out = psum[:, 6 + g % 2, 16 * gp:16 * gp + 16]
                pe.matmul(out, WX[0][pr, gp, :], bcin[pr, 2, 16 * gp:16 * gp + 16], start=True, stop=False)
                ins = pe.matmul(out, WX[1][pr, gp, :], nci[pr, 16 * gp:16 * gp + 16], start=False, stop=True)
            ins.then_inc(S["k7mm"], 1)

            pe.wait_ge(S["in_out"], 8 * NT)
            pe.wait_ge(S["k7out"], 1)
            transposes(lambda n, r, hh: proj[0:r, hh // 8, n, 128 * (hh % 8):128 * (hh % 8) + 128], "qk_ready", "qk_tr", "qkT", 4)
            pe.wait_ge(S["qkT"], 12)
            pe.wait_ge(S["cache"], 48)
            keys_of = [128, 256, 320]

            def scores(u):
                n, h = divmod(u, HEADS)
                (t0, r), kk = TILES[n], keys_of[n]
                if u >= 2:
                    pe.wait_ge(S["s_sm"], u - 1)
                for c in range(2):
                    hp = slice(64 * c, 64 * c + 64)
                    q, out = qkT[hp, h, t0:t0 + r], psum[0:r, 2 * (u % 2) + c, :]
                    if n < 2:
                        ins = pe.matmul(out[:, 0:kk], q, qkT[hp, 8 + h, 0:kk], start=True, stop=True)
                    else:
                        pe.matmul(out[:, 0:PAST], q, ckT[hp, h, :], start=True, stop=True)
                        ins = pe.matmul(out[:, PAST:kk], q, qkT[hp, 8 + h, t0:t0 + r], start=True, stop=True)
                ins.then_inc(S["s_mm"], 1)

            def values(u):
                n, h = divmod(u, HEADS)
                (t0, r), kk, b = TILES[n], keys_of[n], u % 2
                blocks = [min(P, kk - a) for a in range(0, kk, P)]
                pe.wait_ge(S["w_ready"], u + 1)
                if u >= 2:
                    pe.wait_ge(S["wT"], 2 * (u - 1))
                for k, w in enumerate(blocks):
                    ins = pe.transpose(psum[0:w, 4 + b, 128 * k:128 * k + r], sm[0:r, b, 0, 128 * k:128 * k + w], ident[0:r, 0:r])
                ins.then_inc(S["w_tr"], 1)
                pe.wait_ge(S["wT"], 2 * (u + 1))
                if u >= 2:
                    pe.wait_ge(S["o_out"], u - 1)
                for k, w in enumerate(blocks):
                    if n < 2:
                        v = proj[0:w, 2, k, 128 * h:128 * h + 128]
                    else:
                        v = cv[0:w, k, 128 * h:128 * h + 128] if k < 2 else proj[0:w, 2, 2, 128 * h:128 * h + 128]
                    ins = pe.matmul(psum[0:r, 6 + b, 0:128], wT[0:w, b, k, 0:r], v, start=k == 0, stop=k == len(blocks) - 1)
                ins.then_inc(S["pv"], 1)

            units = NT * HEADS
            for u in range(units + 1):
                if u < units:
                    scores(u)
                if u:
                    values(u - 1)

            pe.wait_ge(S["o_out"], units)
            for k in range(8):
                pe.wait_ge(S["xg"], k + 1)
                for j in range(8):
                    ins = pe.transpose(psum[:, k, CH * j:CH * (j + 1)], Xg[0:CH, k % 2, 128 * j:128 * (j + 1)], ident[0:CH, 0:CH])
                ins.then_inc(S["ug_tr"], 1)
            pe.wait_ge(S["ug"], 8)
            def state_matrices(q):
                if q >= 2:
                    pe.wait_ge(S["wt"], q - 1)
                for k in range(4):
                    ins = pe.transpose(psum[:, 6 + q % 2, 128 * k:128 * k + 128], WX[k % 2][:, 2 * q + k // 2, :], ident[:, :])
                ins.then_inc(S["wt_tr"], 1)

            def state_inputs(q):
                pe.wait_ge(S["wt"], q + 1)
                for k in range(8):
                    gp, ri, par = 2 * q + k // 4, (k // 2) % 2, k % 2
                    ins = pe.matmul(psum[64 * par:64 * par + 64, 3 * ri + gp // 12, CH * (gp % 12):CH * (gp % 12) + CH],
                                    WTs[:, q % 2, 128 * (2 * (k // 4) + ri) + 64 * par:128 * (2 * (k // 4) + ri) + 64 * par + 64],
                                    UG[:, 2 * gp + par, :], start=True, stop=True)
                ins.then_inc(S["f_mm"], 1)

            for q in range(17):
                if q < 16:
                    state_matrices(q)
                if q:
                    state_inputs(q - 1)
            pe.wait_ge(S["hc"], 2)
            pe.wait_ge(S["f_out"], 1)
            pe.wait_ge(S["k7st"], 16 * STEP)
            Tg = Tm.rearrange("p j (g n) -> p j g n", g=GROUPS)
            for q in range(16):
                if q >= 8:
                    pe.wait_ge(S["y_gl"], q - 7)
                for k in range(4):
                    g = 8 * (q // 2) + 2 * k + q % 2
                    pr, gp = slice(64 * (g % 2), 64 * (g % 2) + 64), g // 2
                    out = psum[0:CH, q % 8, 128 * k:128 * k + 128]
                    pe.matmul(out, UG[:, g, :], Tg[:, :, g, :], start=True, stop=False)
                    pe.matmul(out, HCt[pr, gp, :], CA[0][pr, gp, :], start=False, stop=False)
                    ins = pe.matmul(out, HCt[pr, GP + gp, :], CA[1][pr, gp, :], start=False, stop=True)
                ins.then_inc(S["y_mm"], 1)
            pe.wait_ge(S["y_gl"], 16)
            pe.wait_ge(S["y_in"], 16 * NT)
            for n, (t0, r) in enumerate(TILES):
                for j in range(2):
                    for k in range(4):
                        ins = pe.transpose(psum[:, 2 * n + j, 128 * k:128 * k + r],
                                           y_tok[0:r, n, 128 * (4 * j + k):128 * (4 * j + k + 1)], ident[0:r, 0:r])
                    ins.then_inc(S["yT_tr"], 1)
            pe.wait_ge(S["yT"], 6)
            dense(0, B_GLU, 2, 2, yT, "glu_mm", "glu_b", first=True)
            pe.wait_ge(S["glu_b"], 6)
            pe.wait_ge(S["o_ready"], NT)
            transposes(lambda n, r, dc: (o_tok if dc < 8 else z_tok)[0:r, n, 128 * (dc % 8):128 * (dc % 8) + 128], "s_ready", "mix_tr", "mixT", 4)
            pe.wait_ge(S["mixT"], 12)
            dense(0, B_OUT, 4, 4, mixT, "out_mm", "out_x", first=True)

            pe.wait_ge(S["out_x"], 12)
            transposes(lambda n, r, dc: xn2[0:r, n, 128 * dc:128 * (dc + 1)], "xn2", "tr2", "xn2T", 4)
            pe.wait_ge(S["xn2T"], 12)
            for c in range(4):
                for b in range(4):
                    g = B_PQ + 4 * c + b
                    loaded(pe, g)
                    for d in range(4):
                        for k in range(4):
                            if c >= 2 and b == d == 0:
                                pe.wait_ge(S["qT"], 4 * (c - 2) + k + 1)
                            ins = pe.matmul(psum[:, 4 * (c % 2) + k, 0:T], ring[:, g % SLOTS, COLS * d + 128 * k:COLS * d + 128 * (k + 1)],
                                            xn2T[:, 4 * b + d, :], start=b == d == 0, stop=b == d == 3)
                            if b == d == 3:
                                ins.then_inc(S["pq_mm"], 1)
                    if b < 3:
                        ins.then_inc(S["used"], 1)
                    else:
                        pe.wait_ge(S["pq_mm"], 4 * (c + 1))
                        pe.sem_inc(S["used"], 1)
            pe.wait_ge(S["qT"], 16)
            pe.wait_ge(S["keys"], 16)
            for n, (t0, r) in enumerate(TILES):
                for k in range(4):
                    m = 4 * n + k
                    if m >= 8:
                        pe.wait_ge(S["sc_out"], m - 7)
                    for j in range(4):
                        hc = 4 * k + j
                        ins = pe.matmul(psum[0:r, m % 8, 128 * j:128 * j + 128], qT[:, hc, t0:t0 + r], keys[:, 128 * hc:128 * (hc + 1)],
                                        start=True, stop=True)
                    ins.then_inc(S["sc_mm"], 1)
            pe.wait_ge(S["sc_out"], 12)
            for n, (t0, r) in enumerate(TILES):
                pe.wait_ge(S["picks"], n + 1)
                for k, src in enumerate((gate, pick_i, pick_j)):
                    ins = pe.transpose(psum[:, n, 128 * k:128 * k + r], src[0:r, n, :], ident[0:r, 0:r])
                ins.then_inc(S["pick_tr"], 1)

            def spread_gates(sec, i, k, free=True):
                base = SEC * sec + k
                pe.wait_ge(S["one"], i * 8 + 2 * (base + 1))
                if free:
                    pe.wait_ge(S["gs_out"], i * 4 + (base - 1))
                for t in range(TOK):
                    for c in range(3):
                        ins = pe.matmul(psum[:, 2 + k % 2, SEC * t:SEC * (t + 1)], oneB[k % 2][:, t, :],
                                        oneA[k % 2][:, c, SEC * t:SEC * (t + 1)], start=c == 0, stop=c == 2)
                ins.then_inc(S["gs_mm"], 1)

            for k in range(4):
                spread_gates(0, 0, k, k >= 2)
            with pe.Fori(1, SEC // 4) as i:
                for k in range(4):
                    spread_gates(0, i, k)
            for s in range(SECTIONS):
                def experts_in(i, first):
                    for k in range(4):
                        pe.wait_ge(S[f"slot{k}"], i * 16 + 16 * ((B_EXP + 2 * s * SEC) // SLOTS + 1))
                        if not first or k >= 2:
                            pe.wait_ge(S["e_g"], i * 4 + (SEC * s + k - 1))
                        for dc in range(DC):
                            ins = pe.matmul(psum[:, k % 2, 0:T], ring[:, k, 128 * dc:128 * (dc + 1)], xn2T[:, dc, :],
                                            start=dc == 0, stop=dc == DC - 1)
                        ins.then_inc(S["e_h"], 1)
                        pe.wait_ge(S["e_h"], i * 4 + (SEC * s + k + 1))
                        pe.sem_inc(S["used"], 1)
                        if s + 1 < SECTIONS:
                            spread_gates(s + 1, i, k)

                if s:
                    pe.wait_ge(S["e_acc"], 16 * s - 4)
                if s == 0:
                    experts_in(0, True)
                with pe.Fori(1 if s == 0 else 0, SEC // 4) as i:
                    experts_in(i, False)
                pe.wait_ge(S["e_w"], SEC * (s + 1))
                if s + 1 < SECTIONS:
                    pe.wait_ge(S["gs_out"], SEC * (s + 2))
                for half in range(2):
                    def experts_out(i, first, last):
                        for k in range(4):
                            pe.wait_ge(S[f"slot{k}"], i * 16 + 16 * ((B_EXP + (2 * s + 1) * SEC + half * SEC // 2) // SLOTS + 1))
                            for ii in range(2):
                                w = G[s % 2][:, bass.ds(i * 8 + 2 * k + ii, 1), :].rearrange("p o t -> p (o t)")
                                for dd in range(8):
                                    start, stop = first and k == ii == 0, last and k == 3 and ii == 1
                                    if start and (s or half):
                                        pe.wait_ge(S["e_acc"], 8 * (2 * s + half - 1) + dd + 1)
                                    ins = pe.matmul(bank(dd, T), ring[:, k, 1024 * ii + 128 * dd:1024 * ii + 128 * (dd + 1)], w,
                                                    start=start, stop=stop)
                                    if stop:
                                        ins.then_inc(S["e_o"], 1)
                            if last and k == 3:
                                pe.wait_ge(S["e_o"], 8 * (2 * s + half + 1))
                                pe.sem_inc(S["used"], 1)
                            else:
                                ins.then_inc(S["used"], 1)

                    experts_out(0, True, False)
                    with pe.Fori(1, SEC // 8 - 1) as i:
                        experts_out(i, False, False)
                    experts_out(SEC // 8 - 1, False, True)
            for n, (t0, r) in enumerate(TILES):
                for j in range(4):
                    m = 4 * n + j
                    if m == 0:
                        pe.wait_ge(S["e_acc"], 16 * SECTIONS)
                    if m >= 8:
                        pe.wait_ge(S["fin"], m - 7)
                    for k in range(4):
                        ins = pe.transpose(psum[0:r, m % 8, 128 * k:128 * k + 128], acc[:, 4 * j + k, t0:t0 + r], ident[:, :])
                    ins.then_inc(S["fin_tr"], 1)


def stream(w, order=None):
    rows, columns = w.shape
    b = w.reshape(rows // COLS, 4, P, columns // COLS, COLS).transpose(3, 0, 2, 1, 4)
    if order is not None:
        b = b[order]
    return np.ascontiguousarray(b.reshape(-1, P, BLOCK))


def states(a):
    a = a.reshape(GP, 2, SSM_N, *a.shape[2:])
    return np.ascontiguousarray(np.moveaxis(a, 0, 2).reshape(P, GP, *a.shape[3:]).reshape(P, -1))


def kernel(**inputs):
    import concourse.bacc as bacc
    from concourse.bass_utils import run_bass_kernel_spmd

    a = {k: np.asarray(v) for k, v in inputs.items()}
    x = np.concatenate([a["x_prompt"][0], a["x_sample"][0]])
    pos = np.arange(T, dtype=np.float32)
    inv = np.float32(500000.0) ** (-np.arange(8, dtype=np.float32) * np.float32(2.0 / 16))
    ang = (pos[:, None] * inv[None, :]).astype(np.float32)
    rope = np.zeros((P, NT, 16), np.float32)
    for n, (t0, r) in enumerate(TILES):
        rope[:r, n, 0:8] = np.cos(ang[t0:t0 + r])
        rope[:r, n, 8:16] = np.sin(ang[t0:t0 + r])
    mask = np.zeros((P, 2, 256), np.float32)
    for n in range(2):
        q_chunk = (np.arange(P) + 128 * n) // 64
        mask[:, n] = np.where(np.arange(256)[None, :] // 64 <= q_chunk[:, None], 0.0, -1e30)
    dmask = np.zeros((P, SSM_P), np.float32)
    dmask[P - SSM_P:] = np.eye(SSM_P)
    skip = np.concatenate([np.zeros((P - SSM_P, GROUPS), np.float32), a["ssm_d"][0].reshape(GROUPS, SSM_P).T])
    u = a["peer_u"][0].reshape(PK, P, DC, P)
    v = a["peer_v"][0].reshape(SECTIONS, SEC // 2, 2, P, 2, 1024)
    arrays = {
        "x": x, "ident": np.eye(P, dtype=np.float32), "iota": np.arange(P, dtype=np.float32), "rope": rope.reshape(P, -1),
        "mask": mask, "dmask": dmask, "skip": skip,
        "norm1_g": a["norm1_g"][0].reshape(DC, P).T, "norm2_g": a["norm2_g"][0].reshape(DC, P).T,
        "q_g": a["q_norm_g"][0], "k_g": a["k_norm_g"][0], "sub_g": a["subln_g"][0],
        "lq1": a["lambda_q1"][0], "lk1": a["lambda_k1"][0], "lq2": a["lambda_q2"][0], "lk2": a["lambda_k2"][0],
        "a_re": states(a["ssm_a_re"][0]), "a_im": states(a["ssm_a_im"][0]),
        "log_dt": states(np.broadcast_to(a["ssm_log_dt"][0][:, None], (GROUPS, SSM_N))),
        "b_re": states(a["ssm_b_re"][0]), "b_im": states(a["ssm_b_im"][0]),
        "c_re": states(a["ssm_c_re"][0].transpose(0, 2, 1)), "c_im": states(a["ssm_c_im"][0].transpose(0, 2, 1)),
        "h0_re": states(a["state_ssm_re"][0, 0]), "h0_im": states(a["state_ssm_im"][0, 0]),
        "cache_k": a["cache_k"][0, 0].reshape(PAST, HEADS, P).transpose(2, 1, 0),
        "cache_v": a["cache_v"][0, 0].reshape(PAST, 1024),
        "b_glu": a["b_glu"][0],
        "keys": a["peer_keys"][0].transpose(3, 0, 1, 2).reshape(P, D),
        "w_in": stream(a["w_in"][0], [6, 7, 0, 1, 2, 3, 4, 5]),
        "w_glu": stream(a["w_glu"][0]), "w_out": stream(a["w_out"][0]), "w_pq": stream(a["w_peer_q"][0]),
        "peer_u": u.transpose(0, 3, 2, 1).reshape(PK, P, BLOCK),
        "peer_v": v.transpose(0, 4, 1, 3, 2, 5).reshape(PK, P, BLOCK),
    }
    arrays = {k: np.ascontiguousarray(v) for k, v in arrays.items()}
    nc = bacc.Bacc("TRN2", target_bir_lowering=False, num_devices=1)
    io = {k: nc.dram_tensor(f"in_{k}", v.shape, F32, kind="ExternalInput").ap() for k, v in arrays.items()}
    outs = {"y": (T, D), "k_all": (T, 1024), "v_all": (T, 1024), "states": (P, 2, 2 * GP)}
    for k, shape in outs.items():
        io[k] = nc.dram_tensor(f"out_{k}", shape, F32, kind="ExternalOutput").ap()
    for k in ("u_tmp", "y_tmp"):
        io[k] = nc.dram_tensor(k, (T, 1024), F32, kind="Internal").ap()
    build(nc, io)
    res = run_bass_kernel_spmd(nc, [{f"in_{k}": v for k, v in arrays.items()}], core_ids=[0]).results[0]
    y, k, v, st = (np.asarray(res[f"out_{n}"]) for n in outs)
    st = st.reshape(2, SSM_N, 2, 2, GP).transpose(2, 3, 4, 0, 1).reshape(2, 2, 1, 1, GROUPS, SSM_N)
    kp, ks = (k[s].reshape(1, 1, -1, HEADS, 2, HD) for s in (slice(0, T_PROMPT), slice(T_PROMPT, T)))
    vp, vs = (v[s].reshape(1, 1, -1, HEADS, 2 * HD) for s in (slice(0, T_PROMPT), slice(T_PROMPT, T)))
    return (y[None, :T_PROMPT], y[None, T_PROMPT:], kp, vp, st[0, 0], st[0, 1], ks, vs, st[1, 0], st[1, 1])
```

```python
import math

import numpy as np
import concourse.bass as bass
from concourse import mybir
from contextlib import ExitStack

F32 = mybir.dt.float32
F32R = mybir.dt.float32r
BF16 = mybir.dt.bfloat16
U32 = mybir.dt.uint32
I32 = mybir.dt.int32
ALU = mybir.AluOpType
ACT = mybir.ActivationFunctionType
AX = mybir.AxisListType

P = 128
D = 2048
T_PROMPT, T_SAMPLE = 256, 64
T = T_PROMPT + T_SAMPLE
TILES = [(0, 128), (128, 128), (256, 64)]
NT = len(TILES)
DC = D // P
COLS = 512
BLOCK = 2048
HEADS, HD = 8, 64
PAST = 256
SSM_W, SSM_P, GROUPS, SSM_N = 1024, 16, 64, 64
GP = GROUPS // 2
STEP = 8
CH_PROMPT, CH_SAMPLE = T_PROMPT // STEP, T_SAMPLE // STEP
CH = CH_PROMPT + CH_SAMPLE
PH, PK, TOPK = 8, 128, 16
HC = 2 * PH
EPS = 1e-6
LAM_INIT = 0.8 - 0.6 * math.exp(-0.3 * 0)
SLOTS = 4
SECTIONS = 4
SEC = PK // SECTIONS
TOK = T // SEC
LOW = -3.0e38
TWO_PI = (6.28125, 0.0019350051879882812, 3.0199159819e-07)

N_IN, N_GLU, N_OUT, N_PQ = 32, 4, 16, 16
B_IN, B_GLU = 0, N_IN
B_OUT = B_GLU + N_GLU
B_PQ = B_OUT + N_OUT
B_EXP = B_PQ + N_PQ
U_BLK, V_BLK = range(2)


def build(nc, io):
    ctx = ExitStack()

    def sb(name, shape, dt=F32):
        return ctx.enter_context(nc.sbuf_tensor(name, shape, dt))

    def sem(name):
        return ctx.enter_context(nc.semaphore(name))

    with ctx:
        ARENA = 43590
        ring = sb("ring", [P, SLOTS, BLOCK])
        ident = sb("ident", [P, P])
        iota = sb("iota", [P, PK])[:, :]
        with ExitStack() as front:
            arena = front.enter_context(nc.sbuf_tensor("arena", [P, ARENA], F32))
            small = front.enter_context(nc.sbuf_tensor("small", [P, 960], F32))
        with ExitStack() as front:
            front.enter_context(nc.sbuf_tensor("arena_before_xn2T", [P, 12288], F32))
            xn2T = front.enter_context(nc.sbuf_tensor("xn2T", [P, DC, T], F32))[:, :, :]
            front.enter_context(nc.sbuf_tensor("arena_before_gates", [P, 23184 - 17408], F32))
            gates_T = front.enter_context(nc.sbuf_tensor("gates_T", [P, 2, T], F32))
        experts = sb("experts", [P, 28960])
        x_parts = sb("x_parts", [P, 2, DC, T], F32R)
        w_parts = sb("w_parts", [P, 4, 2, 512], F32R)
        h_parts = sb("h_parts", [P, 2, 2, T], F32R)
        psum = ctx.enter_context(nc.psum_tensor("psum", [P, 8, COLS], F32))
        used = [0]

        def stat(*dims):
            n = math.prod(dims)
            used[0] += n
            assert used[0] <= 960, used
            r = small[:, used[0] - n:used[0]]
            return r.rearrange("p (a b) -> p a b", a=dims[0]) if len(dims) == 2 else r

        def at(word, *dims):
            n = math.prod(dims)
            assert word + n <= ARENA, (word, dims)
            r = arena[:, word:word + n]
            if len(dims) == 2:
                return r.rearrange("p (a b) -> p a b", a=dims[0])
            if len(dims) == 3:
                return r.rearrange("p (a b c) -> p a b c", a=dims[0], b=dims[1])
            return r

        def spread(ap, *shape):
            return ap.broadcast_to(list(shape))

        g1, g2 = stat(DC), stat(DC)
        rope = stat(NT, 16)
        qk_g = stat(2, HD)
        sub_g = stat(2 * HD)
        h0 = stat(2 * GP)
        skip = stat(GROUPS)
        lam_in = stat(4, HD)
        ssq, var, rstd = stat(NT), stat(NT), stat(NT)
        nlam = stat(1)
        lam2 = stat(2)
        mx, nb, z, rz = stat(2, 2), stat(2, 2), stat(2, 2), stat(2, 2)
        hs, hv, hr = stat(32), stat(32), stat(32)

        xT = at(0, DC, T)
        x_tok = at(5120, NT, D)
        proj = at(5120, 4, NT, 1024)
        sq_full = at(17408, D)
        WX = [at(17408, GP, 128), at(21504, GP, 128)]
        CA = [at(25600, GP, 128), at(29696, GP, 128)]
        tmp_big = at(33792, GP, 128)
        PWR, PWI = at(37888, 9, GP), at(38176, 9, GP)
        AJR, AJI = at(38464, 8, GP), at(38720, 8, GP)
        bcin = at(38976, 4, 512)
        nci = at(41024, 512)
        prm = at(41536, 3, GP)
        sm_ = [at(41632 + 32 * i, GP) for i in range(11)]
        smi = at(41632 + 32 * 11, GP)
        k7 = at(42016, 1024)
        bbar = [at(42016, 512), at(42528, 512)]
        Tm = at(33792, STEP, 1024)
        mask = at(43040, 2, 256)
        dmask = at(43552, 16)
        qkT = at(0, 16, T)
        ckT, cv = at(5120, HEADS, PAST), at(7168, 2, 1024)
        sm = at(9216, 2, 2, T)
        wT = at(10496, 2, 3, 128)
        o_tok = at(14336, NT, 1024)
        sq_head = at(14336, 2048)
        rt = at(16384, 4, 256)
        sq_o = at(42016, 1024)
        X = at(0, STEP * 1024)
        Xg = at(10752, 2, 1024)
        UG = at(8192, GROUPS, CH)
        FS = at(10752, CH, 2 * GP)
        WTs = at(42016, 2, 512)
        HP = at(0, CH + 2, 2 * GP)
        t1, t2 = at(13312, 2, 64), at(13440, 2, 64)
        HCt = at(2688, 2 * GP, CH)
        Y = at(17408, STEP * 1024)
        y_tok = at(25600, NT, 1024)
        yT = at(28672, 8, T)
        z_tok = at(31232, NT, 1024)
        mixT = at(34304, DC, T)
        bglu = at(39424, 1024)
        x2 = at(0, NT, D)
        xn2 = at(6144, NT, D)
        qT = at(17408, HC, T)
        keys = at(22528, D)
        sc = at(10240, NT, D)
        sc2 = at(16384, HC, PK)
        cand, cand2 = at(18432, PH, 256), at(16384, PH, 256)
        eq_k = at(18432, PH * TOPK, TOPK)
        base = 20480
        sv = at(base, HC, TOPK)
        si = at(base + 256, HC * TOPK).bitcast(U32).rearrange("p (a b) -> p a b", a=HC)
        sif = at(base + 512, HC, TOPK)
        fv = at(base + 768, PH, TOPK)
        fp = at(base + 896, 128).bitcast(U32).rearrange("p (a b) -> p a b", a=PH)
        gate, pick_i, pick_j = at(base + 1024, NT, 128), at(base + 1408, NT, 128), at(base + 1792, NT, 128)
        pa_u, pb_u = at(base + 2176, 128).bitcast(U32), at(base + 2304, 128).bitcast(U32)
        pa, pb = at(base + 2432, PH, TOPK), at(base + 2560, PH, TOPK)
        gs = at(base + 2688, PH)
        gT, grest = gates_T[:, 0, :], gates_T[:, 1, :]

        def ex(word, n, dt=F32):
            r = experts[:, word:word + n]
            return r if dt == F32 else r.bitcast(dt)

        H = ex(0, SEC * T).rearrange("p (i t) -> p i t", i=SEC)
        GM = ex(10240, SEC * T).rearrange("p (i t) -> p i t", i=SEC)
        acc = ex(20480, DC * T).rearrange("p (a b) -> p a b", a=DC)
        oneB = [ex(25600 + 640 * i, 640, BF16).rearrange("p (a b) -> p a b", a=TOK) for i in range(2)]
        oneA = [ex(26880 + 480 * i, 480, BF16).rearrange("p (a b) -> p a b", a=3) for i in range(2)]
        eqA = [ex(27840 + 160 * i, 160, BF16).rearrange("p (a b) -> p a b", a=TOK) for i in range(2)]
        iT, jT = ex(28160, 160, BF16), ex(28320, 160, BF16)
        gpart = ex(28480, 480, BF16).rearrange("p (a b) -> p a b", a=3)
        x3 = ex(0, NT * D).rearrange("p (a b) -> p a b", a=NT)
        def a_block(s):
            return N_PQ + 2 * SEC * s

        def b_block(s, half):
            return a_block(s) + SEC + half * SEC // 2

        def bank(b, n=COLS):
            return psum[:, b, 0:n]

        names = """consts x0 x1 x2 ssq var std rst xn tr1 xT
            slot0 slot1 slot2 slot3 used in_mm in_out u_saved s5in
            lam_e lam s5dt s5exp s5sin s5w k7mm k7out k7st tz v_out k_out
            hvar hstd qk_ready qk_tr qkT  xg cache s_mm s_sm s_mx s_exp w_ready w_tr wT pv o_out
            ovar ostd o_ready x_in xs ug_tr ug wt_tr wt f_mm f_out hp hc h_out y_mm y_gl y_save y_in
            yT_tr yT glu_mm glu_b glu_s s_ready mix_tr mixT x_re out_mm out_x bg
            ssq2 var2 std2 xn2 tr2 xn2T keys x_hi pq_mm qT sc_mm sc_out gmx gex picks pick_tr pickT
            x_lo w_hi w_lo w_used one eq gs_mm gs_out h_g e_w g_lo g_hi e_o e_acc x_sv x_bk fin_tr fin y_out dve act pool rec""".split()
        S = {n: sem(n) for n in names}

        def loaded(eng, block):
            eng.wait_ge(S[f"slot{block % SLOTS}"], 16 * (block // SLOTS + 1))

        class Chain:

            def __init__(self, eng, name):
                self.eng, self.sem, self.n = eng, S[name], 0

            def add(self, ins):
                self.n += 1
                ins.then_inc(self.sem, 1)

            def wait(self):
                self.eng.wait_ge(self.sem, self.n)

            def __call__(self, ins):
                self.add(ins)
                self.wait()

        block = ctx.enter_context(nc.Block())

        CONSTS = [(ident[:, :], io["ident"]), (g1, io["norm1_g"]), (g2, io["norm2_g"]),
                  (iota, io["iota"].partition_broadcast(P)), (rope, io["rope"]), (qk_g[:, 0, :], io["q_g"].partition_broadcast(P)),
                  (qk_g[:, 1, :], io["k_g"].partition_broadcast(P)), (sub_g, io["sub_g"].partition_broadcast(P)),
                  (h0[:, 0:GP], io["h0_re"]), (h0[:, GP:], io["h0_im"]), (mask, io["mask"]), (dmask, io["dmask"]),
                  (skip, io["skip"])] + [
                      (lam_in[:, i, :], io[n].partition_broadcast(P)) for i, n in enumerate(("lq1", "lq2", "lk1", "lk2"))]
        S5IN = [(prm[:, 0, :], io["a_re"]), (prm[:, 1, :], io["a_im"]), (prm[:, 2, :], io["log_dt"])] + [
            (bcin[:, i, :], io[n]) for i, n in enumerate(("b_re", "b_im", "c_re", "c_im"))]
        ALL_CONSTS = 16 * len(CONSTS)

        @block.sync
        def _(sp):
            for n, (t0, r) in enumerate(TILES):
                sp.dma_start(x_tok[0:r, n, :], io["x"][t0:t0 + r, :]).then_inc(S[f"x{n}"], 16)

            def turn(source, first, base, i, free=True):
                for s in range(SLOTS):
                    src = io[source][bass.ds(i * SLOTS + (first + s), 1)].rearrange("o p n -> (o p) n")
                    if free:
                        sp.wait_ge(S["used"], i * SLOTS + (base + s - SLOTS + 1))
                    sp.dma_start(ring[:, s, :], src).then_inc(S[f"slot{s}"], 16)

            turn("w_in", 0, B_IN, 0, free=False)
            with sp.Fori(1, N_IN // SLOTS) as i:
                turn("w_in", 0, B_IN, i)
            turn("w_glu", 0, B_GLU, 0)
            with sp.Fori(0, N_OUT // SLOTS) as i:
                turn("w_out", 0, B_OUT, i)
            def turn_parts(source, first, b0, i, free=True):
                for s in range(SLOTS):
                    src = io[source][bass.ds(i * SLOTS + (first + s), 1)].rearrange("o p n -> (o p) n")
                    if free:
                        sp.wait_ge(S["w_lo"], i * (4 * SLOTS) + 4 * (b0 + s - SLOTS + 1))
                    sp.dma_start(ring[:, s, :], src).then_inc(S[f"slot{s}"], 16)

            turn("w_pq", 0, B_PQ, 0)
            with sp.Fori(1, N_PQ // SLOTS) as i:
                turn_parts("w_pq", 0, 0, i)
            for s in range(SECTIONS):
                with sp.Fori(0, SEC // SLOTS) as i:
                    turn_parts("peer_u", s * SEC, a_block(s), i)
                with sp.Fori(0, SEC // SLOTS) as i:
                    turn_parts("peer_v", s * SEC, b_block(s, 0), i)
            sp.wait_ge(S["g_lo"], 2 * PK)
            sp.wait_ge(S["x_sv"], 16 * NT)
            for n, (t0, r) in enumerate(TILES):
                sp.dma_start(x3[0:r, n, :], io["x_tmp"][t0:t0 + r, :]).then_inc(S["x_bk"], 16)
            for n, (t0, r) in enumerate(TILES):
                sp.wait_ge(S["fin"], 4 * (n + 1))
                sp.dma_start(io["y"][t0:t0 + r, :], x3[0:r, n, :]).then_inc(S["y_out"], 16)
            sp.wait_ge(S["y_out"], 16 * NT)

        @block.gpsimd
        def _(pool):
            for dst, src in S5IN:
                pool.dma_start(dst, src).then_inc(S["s5in"], 16)
            pool.wait_ge(S["in_out"], 2 * NT)
            for n, (t0, r) in enumerate(TILES):
                pool.dma_start(io["u_tmp"][t0:t0 + r, :], proj[0:r, 3, n, :]).then_inc(S["u_saved"], 16)
            pool.wait_ge(S["k7out"], 1)
            pool.memset(Tm, 0.0).then_inc(S["tz"], 1)
            pool.wait_ge(S["tz"], 1)
            for j in range(STEP):
                n = SSM_P * (j + 1)
                pool.dma_start(Tm[0:n, j, :], k7[P - n:P, :]).then_inc(S["k7st"], 16)
            pool.wait_ge(S["in_out"], 8 * NT)
            for n, (t0, r) in enumerate(TILES):
                pool.dma_start(io["v_all"][t0:t0 + r, :], proj[0:r, 2, n, :]).then_inc(S["v_out"], 16)
            pool.wait_ge(S["qk_ready"], NT)
            for n, (t0, r) in enumerate(TILES):
                pool.dma_start(io["k_all"][t0:t0 + r, :], proj[0:r, 1, n, :]).then_inc(S["k_out"], 16)
            pool.wait_ge(S["k_out"], 16 * NT)
            pool.wait_ge(S["qkT"], 12)
            pool.dma_start(ckT, io["cache_k"]).then_inc(S["cache"], 16)
            for b in range(2):
                pool.dma_start(cv[:, b, :], io["cache_v"][b * P:(b + 1) * P, :]).then_inc(S["cache"], 16)
            pool.wait_ge(S["pv"], NT * HEADS)
            pool.wait_ge(S["v_out"], 16 * NT)
            pool.wait_ge(S["u_saved"], 16 * NT)
            pool.dma_start(X[0:CH, :], io["u_tmp"].rearrange("(c i) n -> c (i n)", i=STEP)).then_inc(S["xs"], 16)
            pool.wait_ge(S["hp"], 1)
            pool.dma_start(io["states"][:, 0, :], HP[:, CH_PROMPT, :]).then_inc(S["h_out"], 16)
            pool.dma_start(io["states"][:, 1, :], HP[:, CH + 1, :]).then_inc(S["h_out"], 16)
            pool.wait_ge(S["y_gl"], 16)
            pool.dma_start(io["y_tmp"].rearrange("(c i) n -> c (i n)", i=STEP), Y[0:CH, :]).then_inc(S["y_save"], 16)
            pool.wait_ge(S["y_save"], 16)
            for n, (t0, r) in enumerate(TILES):
                pool.dma_start(y_tok[0:r, n, :], io["y_tmp"][t0:t0 + r, :]).then_inc(S["y_in"], 16)
            pool.dma_start(bglu, io["b_glu"].partition_broadcast(P)).then_inc(S["bg"], 16)
            pool.wait_ge(S["h_out"], 32)
            pool.wait_ge(S["y_mm"], 16)
            for n, (t0, r) in enumerate(TILES):
                pool.dma_start(x2[0:r, n, :], io["x"][t0:t0 + r, :]).then_inc(S["x_re"], 16)
            pool.wait_ge(S["mixT"], 12)
            pool.dma_start(keys, io["keys"]).then_inc(S["keys"], 16)
            pool.wait_ge(S["out_x"], 12)
            for n, (t0, r) in enumerate(TILES):
                pool.dma_start(io["x_tmp"][t0:t0 + r, :], x2[0:r, n, :]).then_inc(S["x_sv"], 16)
            with pool.Fori(0, (N_PQ + 2 * PK) // SLOTS) as i:
                for k in range(SLOTS):
                    for q in range(4):
                        pool.wait_ge(S["w_hi"], i * (4 * SLOTS) + (4 * k + q + 1))
                        pool.tensor_tensor(w_parts[:, q, 1, :], ring[:, k, 512 * q:512 * (q + 1)], w_parts[:, q, 0, :].bitcast(F32),
                                           ALU.subtract).then_inc(S["w_lo"], 1)

        @block.scalar
        def _(act):
            chain = Chain(act, "act")
            for dst, src in CONSTS:
                act.dma_start(dst, src).then_inc(S["consts"], 16)

            def root(source, n, var_sem, std_sem, ap):
                act.wait_ge(S[var_sem], n)
                act.activation(ap, ap, ACT.Sqrt).then_inc(S[std_sem], 1)

            for n, (t0, r) in enumerate(TILES):
                act.wait_ge(S[f"x{n}"], 16)
                act.activation(sq_full[0:r, :], x_tok[0:r, n, :], ACT.Square, accum_out=ssq[0:r, n:n + 1]).then_inc(S["ssq"], 1)
                act.wait_ge(S["ssq"], n + 1)
            for n, (t0, r) in enumerate(TILES):
                act.wait_ge(S["var"], n + 1)
                act.activation(var[0:r, n:n + 1], var[0:r, n:n + 1], ACT.Sqrt).then_inc(S["std"], 1)
            act.wait_ge(S["lam_e"], 1)
            act.activation(lam2, lam2, ACT.Exp).then_inc(S["lam"], 1)
            act.wait_ge(S["s5in"], 16 * len(S5IN))
            act.activation(prm[:, 2, :], prm[:, 2, :], ACT.Exp).then_inc(S["s5exp"], 1)
            act.wait_ge(S["s5dt"], 1)
            act.activation(sm_[0], sm_[0], ACT.Exp).then_inc(S["s5exp"], 1)
            act.wait_ge(S["s5dt"], 2)
            act.activation(sm_[1], sm_[1], ACT.Sin).then_inc(S["s5sin"], 1)
            act.activation(sm_[2], sm_[2], ACT.Sin).then_inc(S["s5sin"], 1)

            def evac_in(i, kind):
                for c2 in range(2):
                    for n, (t0, r) in enumerate(TILES):
                        dst = proj[0:r, bass.ds(kind, 1), n, c2 * COLS:(c2 + 1) * COLS].rearrange("p o n -> p (o n)")
                        act.wait_ge(S["in_mm"], i * (2 * NT) + (c2 * NT + n + 1))
                        act.activation(dst, psum[0:r, 3 * c2 + n, :], ACT.Copy).then_inc(S["in_out"], 1)

            evac_in(0, 3)
            with act.Fori(1, 4) as i:
                evac_in(i, i - 1)

            for n, (t0, r) in enumerate(TILES):
                act.wait_ge(S["hvar"], n + 1)
                act.activation(hv[0:r, :], hv[0:r, :], ACT.Sqrt).then_inc(S["hstd"], 1)
            for n, (t0, r) in enumerate(TILES):
                for j in range(4):
                    act.wait_ge(S["qk_tr"], 4 * n + j + 1)
                    act.activation(qkT[:, 4 * j:4 * j + 4, t0:t0 + r],
                                   bank((4 * n + j) % 8).rearrange("p (a b) -> p a b", a=4)[:, :, 0:r], ACT.Copy).then_inc(S["qkT"], 1)
            keys_of = [128, 256, 320]

            def weights_T(u):
                n, h = divmod(u, HEADS)
                r, kk = TILES[n][1], keys_of[n]
                act.wait_ge(S["w_tr"], u + 1)
                if u >= 2:
                    act.wait_ge(S["pv"], u - 1)
                full = kk // P
                src = bank(4 + u % 2).rearrange("p (a b) -> p a b", a=4)
                act.activation(wT[:, u % 2, 0:full, 0:r], src[:, 0:full, 0:r], ACT.Copy).then_inc(S["wT"], 1)
                if kk % P:
                    act.activation(wT[0:64, u % 2, full, 0:r], src[0:64, full, 0:r], ACT.Copy).then_inc(S["wT"], 1)
                else:
                    act.sem_inc(S["wT"], 1)

            for u in range(NT * HEADS):
                n, h = divmod(u, HEADS)
                r, kk = TILES[n][1], keys_of[n]
                for c in range(2):
                    act.wait_ge(S["s_mx"], u + 1)
                    act.activation(sm[0:r, u % 2, c, 0:kk], sm[0:r, u % 2, c, 0:kk], ACT.Exp,
                                   bias=nb[0:r, u % 2, c:c + 1], scale=HD ** -0.5,
                                   accum_out=z[0:r, u % 2, c:c + 1]).then_inc(S["s_exp"], 1)
                if u:
                    weights_T(u - 1)
            weights_T(NT * HEADS - 1)
            for n, (t0, r) in enumerate(TILES):
                act.wait_ge(S["ovar"], n + 1)
                act.activation(hv[0:r, 0:HEADS], hv[0:r, 0:HEADS], ACT.Sqrt).then_inc(S["ostd"], 1)

            for k in range(8):
                act.wait_ge(S["ug_tr"], k + 1)
                act.activation(UG[:, 8 * k:8 * k + 8, :], bank(k, 320).rearrange("p (a b) -> p a b", a=8), ACT.Copy).then_inc(S["ug"], 1)
            for q in range(16):
                act.wait_ge(S["wt_tr"], q + 1)
                if q >= 2:
                    act.wait_ge(S["f_mm"], q - 1)
                act.activation(WTs[:, q % 2, :], bank(6 + q % 2), ACT.Copy).then_inc(S["wt"], 1)
            for q in range(16):
                act.wait_ge(S["y_mm"], q + 1)
                dst = Y[0:CH, :].rearrange("p (j g n) -> p g j n", j=STEP, g=GROUPS)
                for g4 in range(4):
                    ins = act.activation(dst[:, 8 * (q // 2) + 2 * g4 + q % 2], psum[0:CH, q % 8, 128 * g4:128 * g4 + 128].rearrange("p (j n) -> p j n", j=STEP),
                                         ACT.Gelu_apprx_tanh)
                ins.then_inc(S["y_gl"], 1)
            for n, (t0, r) in enumerate(TILES):
                for j in range(2):
                    act.wait_ge(S["yT_tr"], 2 * n + j + 1)
                    act.activation(yT[:, 4 * j:4 * j + 4, t0:t0 + r],
                                   bank(2 * n + j).rearrange("p (a b) -> p a b", a=4)[:, :, 0:r], ACT.Copy).then_inc(S["yT"], 1)
            for c in range(2):
                for n, (t0, r) in enumerate(TILES):
                    act.wait_ge(S["glu_b"], 3 * c + n + 1)
                    zz = z_tok[0:r, n, c * COLS:(c + 1) * COLS]
                    act.activation(zz, zz, ACT.Sigmoid).then_inc(S["glu_s"], 1)
            for n, (t0, r) in enumerate(TILES):
                for j in range(4):
                    act.wait_ge(S["mix_tr"], 4 * n + j + 1)
                    act.activation(mixT[:, 4 * j:4 * j + 4, t0:t0 + r],
                                   bank((4 * n + j) % 8).rearrange("p (a b) -> p a b", a=4)[:, :, 0:r], ACT.Copy).then_inc(S["mixT"], 1)

            for n, (t0, r) in enumerate(TILES):
                act.wait_ge(S["out_x"], 9 + n + 1)
                act.activation(xn2[0:r, n, :], x2[0:r, n, :], ACT.Square, accum_out=ssq[0:r, n:n + 1]).then_inc(S["ssq2"], 1)
                act.wait_ge(S["ssq2"], n + 1)
            for n, (t0, r) in enumerate(TILES):
                act.wait_ge(S["var2"], n + 1)
                act.activation(var[0:r, n:n + 1], var[0:r, n:n + 1], ACT.Sqrt).then_inc(S["std2"], 1)
            for m in range(12):
                n, j = divmod(m, 4)
                t0, r = TILES[n]
                act.wait_ge(S["xn2T"], m + 1)
                act.activation(x_parts[:, 0, 4 * j:4 * j + 4, t0:t0 + r], xn2T[:, 4 * j:4 * j + 4, t0:t0 + r], ACT.Copy).then_inc(S["x_hi"], 1)

            def high(i, b, first=False):
                k = b % SLOTS
                act.wait_ge(S[f"slot{k}"], i * 16 + 16 * ((B_PQ + b) // SLOTS + 1))
                for q in range(4):
                    if not first:
                        act.wait_ge(S["w_used"], i * 16 + (4 * b + q - 3))
                    act.activation(w_parts[:, q, 0, :], ring[:, k, 512 * q:512 * (q + 1)], ACT.Copy).then_inc(S["w_hi"], 1)

            def queries_out(c):
                act.wait_ge(S["w_used"], 16 * (c + 1))
                for k in range(4):
                    act.activation(qT[:, 4 * c + k, :], bank(4 * (c % 2) + k, T), ACT.Copy).then_inc(S["qT"], 1)

            for b in range(N_PQ):
                high(0, b, b == 0)
                if b and b % 4 == 0:
                    queries_out(b // 4 - 1)
            high(0, a_block(0))
            queries_out(3)
            for n, (t0, r) in enumerate(TILES):
                for k in range(4):
                    act.wait_ge(S["sc_mm"], 4 * n + k + 1)
                    act.activation(sc[0:r, n, COLS * k:COLS * (k + 1)], psum[0:r, (4 * n + k) % 8, :], ACT.Copy).then_inc(S["sc_out"], 1)

            def gelu(s, i, k):
                act.wait_ge(S["w_used"], i * 16 + 4 * (a_block(s) + k + 1))
                act.activation(H[:, bass.ds(i * 4 + k, 1), :].rearrange("p o t -> p (o t)"), bank(k % 2, T),
                               ACT.Gelu_apprx_tanh).then_inc(S["h_g"], 1)

            def gates_out(s, i, k):
                dst = GM[:, :, bass.ds(i * (4 * TOK) + k * TOK, TOK)].rearrange("p i t -> p t i")
                act.wait_ge(S["gs_mm"], i * 4 + (SEC * s + k + 1))
                act.activation(dst, bank(2 + k % 2, TOK * SEC).rearrange("p (t i) -> p t i", t=TOK), ACT.Copy).then_inc(S["gs_out"], 1)

            act.wait_ge(S["x_sv"], 16 * NT)
            turns = SEC // SLOTS
            for s in range(SECTIONS):
                a, b0 = a_block(s), b_block(s, 0)
                if s:
                    act.wait_ge(S["e_w"], SEC * s)
                    act.wait_ge(S["g_lo"], 2 * SEC * s)

                def after(i, k):
                    gelu(s, i, k)
                    if s:
                        gates_out(s, i, k)

                for k in range(1, SLOTS):
                    high(0, a + k)
                    after(0, k - 1)
                with act.Fori(1, turns) as i:
                    for k in range(SLOTS):
                        high(i, a + k)
                        after(i + (-1 if k == 0 else 0), (k - 1) % SLOTS)
                high(0, b0)
                after(turns - 1, SLOTS - 1)
                if s == 0:
                    for n, (t0, r) in enumerate(TILES):
                        act.wait_ge(S["gmx"], n + 1)
                        act.activation(gate[0:r, n, :], gate[0:r, n, :], ACT.Exp).then_inc(S["gex"], 1)
                    with act.Fori(0, turns) as i:
                        for k in range(SLOTS):
                            gates_out(0, i, k)
                for k in range(1, SLOTS):
                    high(0, b0 + k)
                with act.Fori(1, turns) as i:
                    for k in range(SLOTS):
                        high(i, b0 + k)
                if s + 1 < SECTIONS:
                    high(0, a_block(s + 1))

        @block.vector
        def _(dve):
            chain = Chain(dve, "dve")

            def tt(out, a, b, op):
                return dve.tensor_tensor(out, a, b, op)

            def var_of(dst, src, n):
                return dve.tensor_scalar(dst, src, 1.0 / n, EPS, ALU.mult, ALU.add)

            def norm_rows(src, dst, ssq_s, var_s, std_s, xn_s):
                for n, (t0, r) in enumerate(TILES):
                    dve.wait_ge(S[ssq_s], n + 1)
                    var_of(var[0:r, n:n + 1], ssq[0:r, n:n + 1], D).then_inc(S[var_s], 1)
                for n, (t0, r) in enumerate(TILES):
                    dve.wait_ge(S[std_s], n + 1)
                    chain(dve.reciprocal(rstd[0:r, n:n + 1], var[0:r, n:n + 1]))
                    dve.tensor_scalar(dst[0:r, n, :], src[0:r, n, :], rstd[0:r, n:n + 1], None, ALU.mult).then_inc(S[xn_s], 1)

            def gain_out(dst, gain, tr_s, out_s):
                for n, (t0, r) in enumerate(TILES):
                    for j in range(4):
                        dve.wait_ge(S[tr_s], 4 * n + j + 1)
                        tt(dst[:, 4 * j:4 * j + 4, t0:t0 + r],
                           bank((4 * n + j) % 8).rearrange("p (a b) -> p a b", a=4)[:, :, 0:r],
                           spread(gain[:, 4 * j:4 * j + 4].unsqueeze(2), P, 4, r), ALU.mult).then_inc(S[out_s], 1)

            norm_rows(x_tok, x_tok, "ssq", "var", "std", "xn")
            dve.wait_ge(S["consts"], ALL_CONSTS)
            gain_out(xT, g1, "tr1", "xT")

            chain(tt(lam_in[:, 0:2, :], lam_in[:, 0:2, :], lam_in[:, 2:4, :], ALU.mult))
            dve.tensor_reduce(lam2, lam_in[:, 0:2, :], AX.X, ALU.add).then_inc(S["lam_e"], 1)
            dve.wait_ge(S["lam"], 1)
            chain(tt(nlam, lam2[:, 1:2], lam2[:, 0:1], ALU.subtract))
            chain(dve.tensor_scalar(nlam, nlam, -LAM_INIT, None, ALU.add))

            are, aim, dt = prm[:, 0, :], prm[:, 1, :], prm[:, 2, :]
            mag, half, full = sm_[0], sm_[1], sm_[2]
            ang, cosv, den, nr, cr, ci, ta, tb = sm_[3:11]
            dve.wait_ge(S["s5exp"], 1)
            tt(mag, dt, are, ALU.mult).then_inc(S["s5dt"], 1)
            chain(tt(ang, dt, aim, ALU.mult))
            chain(dve.tensor_scalar(ta, ang, 1.0 / (2 * math.pi), None, ALU.mult))
            chain(dve.tensor_copy(smi.bitcast(I32), ta))
            chain(dve.tensor_copy(tb, smi.bitcast(I32)))
            for part in TWO_PI:
                chain(dve.scalar_tensor_tensor(ang, tb, -part, ang, ALU.mult, ALU.add))
            chain(dve.tensor_scalar(full, ang, 3.1415925, -3.1415925, ALU.min, ALU.max))
            dve.tensor_scalar(half, ang, 0.5, None, ALU.mult).then_inc(S["s5dt"], 1)
            dve.wait_ge(S["s5exp"], 2)
            dve.wait_ge(S["s5sin"], 2)
            chain(tt(cosv, half, half, ALU.mult))
            chain(dve.tensor_scalar(cosv, cosv, -2.0, 1.0, ALU.mult, ALU.add))
            chain(dve.memset(PWR[:, 8, :], 1.0))
            chain(dve.memset(PWI[:, 8, :], 0.0))
            chain(tt(AJR[:, 0, :], mag, cosv, ALU.mult))
            chain(tt(AJI[:, 0, :], mag, full, ALU.mult))
            chain(tt(den, are, are, ALU.mult))
            chain(tt(ta, aim, aim, ALU.mult))
            chain(tt(den, den, ta, ALU.add))
            chain(dve.reciprocal(den, den))
            chain(dve.tensor_scalar(nr, AJR[:, 0, :], -1.0, None, ALU.add))
            chain(tt(cr, nr, are, ALU.mult))
            chain(tt(ta, AJI[:, 0, :], aim, ALU.mult))
            chain(tt(cr, cr, ta, ALU.add))
            chain(tt(cr, cr, den, ALU.mult))
            chain(tt(ci, AJI[:, 0, :], are, ALU.mult))
            chain(tt(ta, nr, aim, ALU.mult))
            chain(tt(ci, ci, ta, ALU.subtract))
            chain(tt(ci, ci, den, ALU.mult))

            def times(outr, outi, ar, ai, br, bi, tmp):
                chain(tt(outr, ar, br, ALU.mult))
                chain(tt(tmp, ai, bi, ALU.mult))
                chain(tt(outr, outr, tmp, ALU.subtract))
                chain(tt(outi, ar, bi, ALU.mult))
                chain(tt(tmp, ai, br, ALU.mult))
                chain(tt(outi, outi, tmp, ALU.add))

            for k in (1, 2, 4):
                shape = (P, k, GP)
                by = (spread(AJR[:, k - 1:k, :], *shape), spread(AJI[:, k - 1:k, :], *shape))
                scr = tmp_big[:, 0:1, :].rearrange("p a b -> p (a b)")[:, 0:k * GP].rearrange("p (a b) -> p a b", a=k)
                times(AJR[:, k:2 * k, :], AJI[:, k:2 * k, :], AJR[:, 0:k, :], AJI[:, 0:k, :], *by, scr)
            for k in range(1, 9):
                chain(dve.tensor_copy(PWR[:, 8 - k, :], AJR[:, k - 1, :]))
                chain(dve.tensor_copy(PWI[:, 8 - k, :], AJI[:, k - 1, :]))
            def per_channel(ap):
                return spread(ap.unsqueeze(2), P, GP, SSM_P)

            def grp(ap):
                return ap.rearrange("p (g n) -> p g n", g=GP)

            times(grp(bbar[0]), grp(bbar[1]), per_channel(cr), per_channel(ci), grp(bcin[:, 0, :]), grp(bcin[:, 1, :]),
                  grp(tmp_big.rearrange("p a b -> p (a b)")[:, 0:512]))

            four = (P, GP, STEP, SSM_P)

            def cols(ap):
                return ap.rearrange("p g (j n) -> p g j n", j=STEP)

            def steps(ap):
                return spread(ap.rearrange("p j g -> p g j").unsqueeze(3), *four)

            def chans(ap):
                return spread(grp(ap).unsqueeze(2), *four)

            qr, qi, br, bi = steps(PWR[:, 1:9, :]), steps(PWI[:, 1:9, :]), chans(bbar[0]), chans(bbar[1])
            chain(tt(cols(WX[0]), qr, br, ALU.mult))
            chain(tt(cols(CA[0]), qi, bi, ALU.mult))
            chain(tt(WX[0], WX[0], CA[0], ALU.subtract))
            chain(tt(cols(WX[1]), qr, bi, ALU.mult))
            chain(tt(cols(CA[1]), qi, br, ALU.mult))
            chain(tt(WX[1], WX[1], CA[1], ALU.add))
            chain(dve.tensor_scalar(nci, bcin[:, 3, :], -1.0, None, ALU.mult))
            dve.sem_inc(S["s5w"], 1)
            rr, ri, cre, cim, ncim = steps(AJR), steps(AJI), chans(bcin[:, 2, :]), chans(bcin[:, 3, :]), chans(nci)
            chain(tt(cols(CA[0]), rr, cre, ALU.mult))
            chain(tt(cols(tmp_big), ri, cim, ALU.mult))
            chain(tt(CA[0], CA[0], tmp_big, ALU.subtract))
            chain(tt(cols(CA[1]), rr, ncim, ALU.mult))
            chain(tt(cols(tmp_big), ri, cre, ALU.mult))
            chain(tt(CA[1], CA[1], tmp_big, ALU.subtract))
            a8 = lam_in.rearrange("p a b -> p (a b)")
            a8r, a8n = a8[:, 0:64], a8[:, 64:128]
            chain(dve.tensor_copy(a8r[:, 0:32], AJR[:, 7, :]))
            chain(dve.tensor_copy(a8r[:, 32:64], AJR[:, 7, :]))
            chain(dve.tensor_scalar(a8n[:, 0:32], AJI[:, 7, :], -1.0, None, ALU.mult))
            chain(dve.tensor_copy(a8n[:, 32:64], AJI[:, 7, :]))
            dve.sem_inc(S["s5w"], 1)
            dprod = tmp_big.rearrange("p a b -> p (a b)")[:, 0:1024].rearrange("p (g n) -> p g n", g=GROUPS)
            chain(tt(dprod, spread(skip.unsqueeze(2), P, GROUPS, SSM_P), spread(dmask.unsqueeze(1), P, GROUPS, SSM_P), ALU.mult))
            dve.wait_ge(S["k7mm"], 1)
            for b in range(2):
                chain(tt(k7.rearrange("p (g c n) -> p c g n", c=2, n=SSM_P)[:, b], bank(6 + b).rearrange("p (g n) -> p g n", g=GP),
                         dprod.rearrange("p (g c) n -> p c g n", c=2)[:, b], ALU.add))
            dve.sem_inc(S["k7out"], 1)

            dve.wait_ge(S["in_out"], 8 * NT)
            dve.wait_ge(S["u_saved"], 16 * NT)
            for n, (t0, r) in enumerate(TILES):
                v = proj[0:r, 0:2, n, :].rearrange("p k (h d) -> p k h d", d=HD)
                sq = sq_head[0:r, :].rearrange("p (k h d) -> p k h d", k=2, d=HD)
                heads = (r, 2, 16, HD)

                def per_head(ap):
                    return spread(ap[0:r, :].rearrange("p (k h) -> p k h", k=2).unsqueeze(3), *heads)

                chain(tt(sq, v, v, ALU.mult))
                chain(dve.tensor_reduce(hs[0:r, :], sq_head[0:r, :].rearrange("p (g d) -> p g d", d=HD), AX.X, ALU.add))
                var_of(hv[0:r, :], hs[0:r, :], HD).then_inc(S["hvar"], 1)
                dve.wait_ge(S["hstd"], n + 1)
                chain(dve.reciprocal(hr[0:r, :], hv[0:r, :]))
                chain(tt(v, v, per_head(hr), ALU.mult))
                chain(tt(v, v, spread(qk_g[0:r].unsqueeze(2), *heads), ALU.mult))
                half = (r, 2, 16, 8)
                a, b = v[:, :, :, 0:8], v[:, :, :, 8:16]
                cosr = spread(rope[0:r, n, 0:8].unsqueeze(1).unsqueeze(1), *half)
                sinr = spread(rope[0:r, n, 8:16].unsqueeze(1).unsqueeze(1), *half)
                m = [rt[0:r, k, :].rearrange("p (k h d) -> p k h d", k=2, d=8) for k in range(4)]
                for k, (e, f) in enumerate(((a, cosr), (b, sinr), (b, cosr), (a, sinr))):
                    chain(tt(m[k], e, f, ALU.mult))
                chain(tt(a, m[0], m[1], ALU.subtract))
                chain(tt(b, m[2], m[3], ALU.add))
                dve.sem_inc(S["qk_ready"], 1)

            keys_of = [128, 256, 320]

            def scores(u):
                n, h = divmod(u, HEADS)
                r, kk, b = TILES[n][1], keys_of[n], u % 2
                dve.wait_ge(S["s_mm"], u + 1)
                if u >= 2:
                    dve.wait_ge(S["w_tr"], u - 1)
                dst, src = sm[0:r, b, :, 0:kk], psum[0:r, 2 * b:2 * b + 2, 0:kk]
                if n < 2:
                    tt(dst, src, spread(mask[0:r, n:n + 1, 0:kk], r, 2, kk), ALU.add).then_inc(S["s_sm"], 1)
                else:
                    dve.tensor_copy(dst, src).then_inc(S["s_sm"], 1)
                dve.wait_ge(S["s_sm"], u + 1)
                chain(dve.tensor_reduce(mx[0:r, b, :], dst, AX.X, ALU.max))
                dve.tensor_scalar(nb[0:r, b, :], mx[0:r, b, :], -HD ** -0.5, None, ALU.mult).then_inc(S["s_mx"], 1)

            def weights(u):
                n, h = divmod(u, HEADS)
                r, kk, b = TILES[n][1], keys_of[n], u % 2
                dve.wait_ge(S["s_exp"], 2 * (u + 1))
                chain(dve.reciprocal(rz[0:r, b, :], z[0:r, b, :]))
                chain(tt(rz[0:r, b, 1:2], rz[0:r, b, 1:2], nlam[0:r], ALU.mult))
                chain(dve.tensor_scalar(sm[0:r, b, 0, 0:kk], sm[0:r, b, 0, 0:kk], rz[0:r, b, 0:1], None, ALU.mult))
                dve.scalar_tensor_tensor(sm[0:r, b, 0, 0:kk], sm[0:r, b, 1, 0:kk], rz[0:r, b, 1:2], sm[0:r, b, 0, 0:kk],
                                         ALU.mult, ALU.add).then_inc(S["w_ready"], 1)

            def head_out(u):
                n, h = divmod(u, HEADS)
                r = TILES[n][1]
                dve.wait_ge(S["pv"], u + 1)
                dve.tensor_copy(o_tok[0:r, n, 128 * h:128 * h + 128], psum[0:r, 6 + u % 2, 0:128]).then_inc(S["o_out"], 1)

            units = NT * HEADS
            for u in range(units + 2):
                if u < units:
                    scores(u)
                if 1 <= u <= units:
                    weights(u - 1)
                if u >= 2:
                    head_out(u - 2)
            dve.wait_ge(S["o_out"], units)
            dve.wait_ge(S["k7st"], 16 * STEP)
            for n, (t0, r) in enumerate(TILES):
                o = o_tok[0:r, n, :].rearrange("p (h d) -> p h d", h=HEADS)
                sq = sq_o[0:r, :].rearrange("p (h d) -> p h d", h=HEADS)
                chain(tt(sq, o, o, ALU.mult))
                chain(dve.tensor_reduce(hs[0:r, 0:HEADS], sq, AX.X, ALU.add))
                var_of(hv[0:r, 0:HEADS], hs[0:r, 0:HEADS], 2 * HD).then_inc(S["ovar"], 1)
                dve.wait_ge(S["ostd"], n + 1)
                chain(dve.reciprocal(hr[0:r, 0:HEADS], hv[0:r, 0:HEADS]))
                chain(dve.tensor_scalar(hr[0:r, 0:HEADS], hr[0:r, 0:HEADS], 1.0 - LAM_INIT, None, ALU.mult))
                chain(tt(o, o, spread(hr[0:r, 0:HEADS].unsqueeze(2), r, HEADS, 2 * HD), ALU.mult))
                tt(o, o, spread(sub_g[0:r].unsqueeze(1), r, HEADS, 2 * HD), ALU.mult).then_inc(S["o_ready"], 1)

            dve.wait_ge(S["xs"], 16)
            Xv = X[0:CH, :].rearrange("p (i g n) -> p g i n", i=STEP, g=GROUPS)
            for k in range(8):
                if k >= 2:
                    dve.wait_ge(S["ug_tr"], k - 1)
                dve.tensor_copy(Xg[0:CH, k % 2, :].rearrange("p (g i n) -> p g i n", g=8, i=STEP), Xv[:, 8 * k:8 * k + 8]).then_inc(S["xg"], 1)
            dve.wait_ge(S["f_mm"], 16)
            for ri in range(2):
                for b in range(3):
                    k = min(12, GP - 12 * b)
                    chain(dve.tensor_copy(FS[:, :, 32 * ri + 12 * b:32 * ri + 12 * b + k].rearrange("p c g -> p g c"),
                                          bank(3 * ri + b, 40 * k).rearrange("p (g c) -> p g c", g=k)))
            dve.sem_inc(S["f_out"], 1)
            chain(dve.memset(HP[:, 0, :], 0.0))
            chain(dve.tensor_copy(HP[:, CH_PROMPT + 1, :], h0))

            def chunk(i, old, new, add, k):
                a8rs, u1, u2 = spread(a8r.unsqueeze(1), P, k, 64), t1[:, 0:k, :], t2[:, 0:k, :]
                tt(u1, old, a8rs, ALU.mult).then_inc(S["rec"], 1)
                tt(u2[:, :, 0:GP], old[:, :, GP:], spread(a8n[:, 0:GP].unsqueeze(1), P, k, GP), ALU.mult).then_inc(S["rec"], 1)
                tt(u2[:, :, GP:], old[:, :, 0:GP], spread(a8n[:, GP:].unsqueeze(1), P, k, GP), ALU.mult).then_inc(S["rec"], 1)
                dve.wait_ge(S["rec"], i * 5 + 3)
                tt(u1, u1, u2, ALU.add).then_inc(S["rec"], 1)
                dve.wait_ge(S["rec"], i * 5 + 4)
                tt(new, u1, add, ALU.add).then_inc(S["rec"], 1)
                dve.wait_ge(S["rec"], i * 5 + 5)

            off = CH_PROMPT + 1
            for i in range(CH_SAMPLE):
                chunk(i, HP[:, i:i + off + 1:off, :], HP[:, i + 1:i + off + 2:off, :],
                      FS[:, i:i + CH_PROMPT + 1:CH_PROMPT, :], 2)
            with dve.Fori(CH_SAMPLE, CH_PROMPT) as i:
                chunk(i, HP[:, bass.ds(i, 1), :], HP[:, bass.ds(i + 1, 1), :], FS[:, bass.ds(i, 1), :], 1)
            dve.sem_inc(S["hp"], 1)
            dve.tensor_copy(HCt[:, :, 0:CH_PROMPT], HP[:, 0:CH_PROMPT, :].rearrange("p c x -> p x c")).then_inc(S["hc"], 1)
            dve.tensor_copy(HCt[:, :, CH_PROMPT:], HP[:, off:off + CH_SAMPLE, :].rearrange("p c x -> p x c")).then_inc(S["hc"], 1)

            dve.wait_ge(S["bg"], 16)
            for c in range(2):
                for n, (t0, r) in enumerate(TILES):
                    dve.wait_ge(S["glu_mm"], 3 * c + n + 1)
                    cc = slice(c * COLS, (c + 1) * COLS)
                    tt(z_tok[0:r, n, cc], psum[0:r, 3 * c + n, :], bglu[0:r, cc], ALU.add).then_inc(S["glu_b"], 1)
            dve.wait_ge(S["y_in"], 16 * NT)
            dve.wait_ge(S["glu_s"], 2 * NT)
            for n, (t0, r) in enumerate(TILES):
                tt(z_tok[0:r, n, :], z_tok[0:r, n, :], y_tok[0:r, n, :], ALU.mult).then_inc(S["s_ready"], 1)
            dve.wait_ge(S["x_re"], 16 * NT)
            for c in range(4):
                for n, (t0, r) in enumerate(TILES):
                    dve.wait_ge(S["out_mm"], 3 * c + n + 1)
                    xx = x2[0:r, n, c * COLS:(c + 1) * COLS]
                    tt(xx, psum[0:r, 3 * (c % 2) + n, :], xx, ALU.add).then_inc(S["out_x"], 1)

            norm_rows(x2, xn2, "ssq2", "var2", "std2", "xn2")
            gain_out(xn2T, g2, "tr2", "xn2T")
            for m in range(12):
                n, j = divmod(m, 4)
                t0, r = TILES[n]
                dve.wait_ge(S["x_hi"], m + 1)
                part = (slice(None), slice(4 * j, 4 * j + 4), slice(t0, t0 + r))
                tt(x_parts[:, 1][part], xn2T[part], x_parts[:, 0][part].bitcast(F32), ALU.subtract).then_inc(S["x_lo"], 1)

            def top16(rows, values, value_of, index_of, rest_of, count):
                for k in range(count):
                    chain.add(dve.max(value_of(k)[:, 0:8], values(k)))
                chain.wait()
                for k in range(count):
                    chain.add(dve.max_index(index_of(k)[:, 0:8], value_of(k)[:, 0:8], values(k)))
                    chain.add(dve.match_replace(rest_of(k), value_of(k)[:, 0:8], values(k), LOW))
                chain.wait()
                for k in range(count):
                    chain.add(dve.max(value_of(k)[:, 8:16], rest_of(k)))
                chain.wait()
                for k in range(count):
                    chain.add(dve.max_index(index_of(k)[:, 8:16], value_of(k)[:, 8:16], rest_of(k)))
                chain.wait()

            dve.wait_ge(S["sc_out"], 4 * NT)
            for n, (t0, r) in enumerate(TILES):
                top16(r, lambda k: sc[0:r, n, PK * k:PK * (k + 1)], lambda k: sv[0:r, k, :], lambda k: si[0:r, k, :],
                      lambda k: sc2[0:r, k, :], HC)
                chain(dve.tensor_copy(sif[0:r], si[0:r]))
                four = (r, PH, TOPK, TOPK)
                s4 = sv[0:r].rearrange("p (h c) k -> p h c k", c=2)
                f4 = sif[0:r].rearrange("p (h c) k -> p h c k", c=2)
                chain(tt(cand[0:r].rearrange("p h (a b) -> p h a b", a=TOPK), spread(s4[:, :, 0, :].unsqueeze(3), *four),
                         spread(s4[:, :, 1, :].unsqueeze(2), *four), ALU.add))
                top16(r, lambda k: cand[0:r, k, :], lambda k: fv[0:r, k, :], lambda k: fp[0:r, k, :],
                      lambda k: cand2[0:r, k, :], PH)
                tt(gate[0:r, n, :].rearrange("p (h k) -> p h k", h=PH), fv[0:r], spread(fv[0:r, :, 0:1], r, PH, TOPK),
                   ALU.subtract).then_inc(S["gmx"], 1)
                fpu = fp[0:r].rearrange("p h k -> p (h k)")
                chain(dve.tensor_scalar(pa_u[0:r], fpu, 4, None, ALU.logical_shift_right))
                chain(dve.tensor_scalar(pb_u[0:r], fpu, 15, None, ALU.bitwise_and))
                for c, (pu, pf, pick) in enumerate(((pa_u, pa, pick_i), (pb_u, pb, pick_j))):
                    flat = pf[0:r].rearrange("p h k -> p (h k)")
                    chain(dve.tensor_copy(flat, pu[0:r]))
                    chain(tt(eq_k[0:r], spread(iota[0:r, 0:TOPK].unsqueeze(1), r, PH * TOPK, TOPK),
                             spread(flat.unsqueeze(2), r, PH * TOPK, TOPK), ALU.is_equal))
                    e4 = eq_k[0:r].rearrange("p (h k) a -> p h k a", h=PH)
                    chain(tt(e4, e4, spread(f4[:, :, c, :].unsqueeze(2), *four), ALU.mult))
                    chain(dve.tensor_reduce(pick[0:r, n, :], eq_k[0:r], AX.X, ALU.add))
            for n, (t0, r) in enumerate(TILES):
                dve.wait_ge(S["gex"], n + 1)
                g3 = gate[0:r, n, :].rearrange("p (h k) -> p h k", h=PH)
                chain(dve.tensor_reduce(gs[0:r], g3, AX.X, ALU.add))
                chain(dve.reciprocal(gs[0:r], gs[0:r]))
                tt(g3, g3, spread(gs[0:r].unsqueeze(2), r, PH, TOPK), ALU.mult).then_inc(S["picks"], 1)
                dve.wait_ge(S["picks"], n + 1)
            for n, (t0, r) in enumerate(TILES):
                dve.wait_ge(S["pick_tr"], n + 1)
                for k, dst in enumerate((gT, iT, jT)):
                    chain(dve.tensor_copy(dst[:, t0:t0 + r], psum[:, 4 + n, 128 * k:128 * k + r]))
            chain(dve.tensor_copy(gpart[:, 0, :], gT))
            chain(tt(grest, gT, gpart[:, 0, :], ALU.subtract))
            chain(dve.tensor_copy(gpart[:, 1, :], grest))
            chain(tt(grest, grest, gpart[:, 1, :], ALU.subtract))
            chain(dve.tensor_copy(gpart[:, 2, :], grest))

            def one_hots(s, i, k, free=True):
                tok = bass.ds(i * (4 * TOK) + k * TOK, TOK)
                base = SEC * s + k
                if free:
                    dve.wait_ge(S["gs_mm"], i * 4 + (base - 1))
                keys_i = iota[:, SEC * s:SEC * (s + 1)]
                tt(eqA[k % 2], spread(keys_i.unsqueeze(1), P, TOK, SEC), spread(iT[:, tok].unsqueeze(2), P, TOK, SEC),
                   ALU.is_equal).then_inc(S["eq"], 1)
                tt(oneB[k % 2], spread(iota.unsqueeze(1), P, TOK, PK), spread(jT[:, tok].unsqueeze(2), P, TOK, PK),
                   ALU.is_equal).then_inc(S["one"], 1)
                dve.wait_ge(S["eq"], i * 4 + (base + 1))
                tt(oneA[k % 2].rearrange("p c (t i) -> p c t i", t=TOK), spread(eqA[k % 2].unsqueeze(1), P, 3, TOK, SEC),
                   spread(gpart[:, :, tok].unsqueeze(3), P, 3, TOK, SEC), ALU.mult).then_inc(S["one"], 1)

            def parts(s, half, i, k, free=True):
                h = H[:, bass.ds(i * 8 + k, 1), :].rearrange("p o t -> p (o t)")
                hi, lo = h_parts[:, k % 2, 0, :], h_parts[:, k % 2, 1, :]
                done = SEC * (2 * s + half) + k + 1
                if half == 0:
                    g = GM[:, bass.ds(i * 8 + k, 1), :].rearrange("p o t -> p (o t)")
                    tt(h, h, g, ALU.mult).then_inc(S["e_w"], 1)
                    dve.wait_ge(S["e_w"], i * 8 + (SEC * s + k + 1))
                if free:
                    dve.wait_ge(S["w_used"], i * 16 + (4 * b_block(s, half) + 2 * (k - 1)))
                dve.tensor_scalar(hi, h, 1.0, None, ALU.mult).then_inc(S["g_hi"], 1)
                dve.wait_ge(S["g_hi"], i * 8 + done)
                tt(lo, h, hi.bitcast(F32), ALU.subtract).then_inc(S["g_lo"], 1)

            for s in range(SECTIONS):
                for k in range(4):
                    one_hots(s, 0, k, s or k >= 2)
                with dve.Fori(1, SEC // 4) as i:
                    for k in range(4):
                        one_hots(s, i, k)
                dve.wait_ge(S["gs_out"], SEC * (s + 1))
                dve.wait_ge(S["h_g"], SEC * (s + 1))
                for k in range(8):
                    parts(s, 0, 0, k, k >= 2)
                with dve.Fori(1, SEC // 8) as i:
                    for k in range(8):
                        parts(s, 0, i, k)
                for half in range(2):
                    if half == 0:
                        parts(s, 1, 0, 0)
                    for k in range(8):
                        if k % 4 == 3:
                            dve.wait_ge(S["w_used"], 4 * b_block(s, half) + 2 * SEC - 1 + k // 4)
                        else:
                            dve.wait_ge(S["e_o"], 6 * (2 * s + half) + k - k // 4 + 1)
                        a = acc[:, 8 * half + k, :]
                        if s == 0:
                            dve.tensor_copy(a, bank(k, T)).then_inc(S["e_acc"], 1)
                        else:
                            tt(a, bank(k, T), a, ALU.add).then_inc(S["e_acc"], 1)
                    if half == 0:
                        for k in range(1, 8):
                            parts(s, 1, 0, k)
                        with dve.Fori(1, SEC // 8) as i:
                            for k in range(8):
                                parts(s, 1, i, k)
            dve.wait_ge(S["x_bk"], 16 * NT)
            for n, (t0, r) in enumerate(TILES):
                for j in range(4):
                    dve.wait_ge(S["fin_tr"], 4 * n + j + 1)
                    xx = x3[0:r, n, COLS * j:COLS * (j + 1)]
                    tt(xx, psum[0:r, (4 * n + j) % 8, :], xx, ALU.add).then_inc(S["fin"], 1)

        @block.tensor
        def _(pe):
            def transposes(src_of, ready, tr, out, quads, extra=0):
                for n, (t0, r) in enumerate(TILES):
                    pe.wait_ge(S[ready], n + 1)
                    for j in range(quads):
                        m = quads * n + j
                        if m >= 8:
                            pe.wait_ge(S[out], m - 7)
                        for k in range(4):
                            ins = pe.transpose(psum[:, m % 8, 128 * k:128 * k + r], src_of(n, r, 4 * j + k), ident[0:r, 0:r])
                        ins.then_inc(S[tr], 1)

            def dense(i, g0, per_chunk, chunks, lhs, mm, out, first=False):
                for c in range(chunks):
                    for b in range(per_chunk):
                        g = c * per_chunk + b
                        s = (g0 + g) % SLOTS
                        pe.wait_ge(S[f"slot{s}"], i * (16 * chunks * per_chunk // SLOTS) + 16 * ((g0 + g) // SLOTS + 1))
                        for d in range(4):
                            dc = 4 * b + d
                            for n, (t0, r) in enumerate(TILES):
                                if dc == 0 and not (first and c < 2):
                                    pe.wait_ge(S[out], i * (NT * chunks) + (NT * (c - 2) + n + 1))
                                ins = pe.matmul(psum[0:r, 3 * (c % 2) + n, :], lhs[:, dc, t0:t0 + r],
                                                ring[:, s, COLS * d:COLS * (d + 1)], start=dc == 0, stop=dc == 4 * per_chunk - 1)
                                if dc == 4 * per_chunk - 1:
                                    if n < NT - 1:
                                        ins.then_inc(S[mm], 1)
                        if b < per_chunk - 1:
                            ins.then_inc(S["used"], 1)
                        else:
                            ins.then_inc(S[mm], 1)
                            pe.wait_ge(S[mm], i * (NT * chunks) + NT * (c + 1))
                            pe.sem_inc(S["used"], 1)

            pe.wait_ge(S["consts"], ALL_CONSTS)
            transposes(lambda n, r, dc: x_tok[0:r, n, 128 * dc:128 * (dc + 1)], "xn", "tr1", "xT", 4)
            pe.wait_ge(S["xT"], 12)
            dense(0, B_IN, 4, 2, xT, "in_mm", "in_out", first=True)
            with pe.Fori(1, 4) as i:
                dense(i, B_IN, 4, 2, xT, "in_mm", "in_out")

            pe.wait_ge(S["s5w"], 2)
            for g in range(GROUPS):
                pr, gp = slice(64 * (g % 2), 64 * (g % 2) + 64), g // 2
                out = psum[:, 6 + g % 2, 16 * gp:16 * gp + 16]
                pe.matmul(out, WX[0][pr, gp, :], bcin[pr, 2, 16 * gp:16 * gp + 16], start=True, stop=False)
                ins = pe.matmul(out, WX[1][pr, gp, :], nci[pr, 16 * gp:16 * gp + 16], start=False, stop=True)
            ins.then_inc(S["k7mm"], 1)

            pe.wait_ge(S["in_out"], 8 * NT)
            pe.wait_ge(S["k7out"], 1)
            transposes(lambda n, r, hh: proj[0:r, hh // 8, n, 128 * (hh % 8):128 * (hh % 8) + 128], "qk_ready", "qk_tr", "qkT", 4)
            pe.wait_ge(S["qkT"], 12)
            pe.wait_ge(S["cache"], 48)
            keys_of = [128, 256, 320]

            def scores(u):
                n, h = divmod(u, HEADS)
                (t0, r), kk = TILES[n], keys_of[n]
                if u >= 2:
                    pe.wait_ge(S["s_sm"], u - 1)
                for c in range(2):
                    hp = slice(64 * c, 64 * c + 64)
                    q, out = qkT[hp, h, t0:t0 + r], psum[0:r, 2 * (u % 2) + c, :]
                    if n < 2:
                        ins = pe.matmul(out[:, 0:kk], q, qkT[hp, 8 + h, 0:kk], start=True, stop=True)
                    else:
                        pe.matmul(out[:, 0:PAST], q, ckT[hp, h, :], start=True, stop=True)
                        ins = pe.matmul(out[:, PAST:kk], q, qkT[hp, 8 + h, t0:t0 + r], start=True, stop=True)
                ins.then_inc(S["s_mm"], 1)

            def values(u):
                n, h = divmod(u, HEADS)
                (t0, r), kk, b = TILES[n], keys_of[n], u % 2
                blocks = [min(P, kk - a) for a in range(0, kk, P)]
                pe.wait_ge(S["w_ready"], u + 1)
                if u >= 2:
                    pe.wait_ge(S["wT"], 2 * (u - 1))
                for k, w in enumerate(blocks):
                    ins = pe.transpose(psum[0:w, 4 + b, 128 * k:128 * k + r], sm[0:r, b, 0, 128 * k:128 * k + w], ident[0:r, 0:r])
                ins.then_inc(S["w_tr"], 1)
                pe.wait_ge(S["wT"], 2 * (u + 1))
                if u >= 2:
                    pe.wait_ge(S["o_out"], u - 1)
                for k, w in enumerate(blocks):
                    if n < 2:
                        v = proj[0:w, 2, k, 128 * h:128 * h + 128]
                    else:
                        v = cv[0:w, k, 128 * h:128 * h + 128] if k < 2 else proj[0:w, 2, 2, 128 * h:128 * h + 128]
                    ins = pe.matmul(psum[0:r, 6 + b, 0:128], wT[0:w, b, k, 0:r], v, start=k == 0, stop=k == len(blocks) - 1)
                ins.then_inc(S["pv"], 1)

            units = NT * HEADS
            for u in range(units + 1):
                if u < units:
                    scores(u)
                if u:
                    values(u - 1)

            pe.wait_ge(S["o_out"], units)
            for k in range(8):
                pe.wait_ge(S["xg"], k + 1)
                for j in range(8):
                    ins = pe.transpose(psum[:, k, CH * j:CH * (j + 1)], Xg[0:CH, k % 2, 128 * j:128 * (j + 1)], ident[0:CH, 0:CH])
                ins.then_inc(S["ug_tr"], 1)
            pe.wait_ge(S["ug"], 8)
            def state_matrices(q):
                if q >= 2:
                    pe.wait_ge(S["wt"], q - 1)
                for k in range(4):
                    ins = pe.transpose(psum[:, 6 + q % 2, 128 * k:128 * k + 128], WX[k % 2][:, 2 * q + k // 2, :], ident[:, :])
                ins.then_inc(S["wt_tr"], 1)

            def state_inputs(q):
                pe.wait_ge(S["wt"], q + 1)
                for k in range(8):
                    gp, ri, par = 2 * q + k // 4, (k // 2) % 2, k % 2
                    ins = pe.matmul(psum[64 * par:64 * par + 64, 3 * ri + gp // 12, CH * (gp % 12):CH * (gp % 12) + CH],
                                    WTs[:, q % 2, 128 * (2 * (k // 4) + ri) + 64 * par:128 * (2 * (k // 4) + ri) + 64 * par + 64],
                                    UG[:, 2 * gp + par, :], start=True, stop=True)
                ins.then_inc(S["f_mm"], 1)

            for q in range(17):
                if q < 16:
                    state_matrices(q)
                if q:
                    state_inputs(q - 1)
            pe.wait_ge(S["hc"], 2)
            pe.wait_ge(S["f_out"], 1)
            pe.wait_ge(S["k7st"], 16 * STEP)
            Tg = Tm.rearrange("p j (g n) -> p j g n", g=GROUPS)
            for q in range(16):
                if q >= 8:
                    pe.wait_ge(S["y_gl"], q - 7)
                for k in range(4):
                    g = 8 * (q // 2) + 2 * k + q % 2
                    pr, gp = slice(64 * (g % 2), 64 * (g % 2) + 64), g // 2
                    out = psum[0:CH, q % 8, 128 * k:128 * k + 128]
                    pe.matmul(out, UG[:, g, :], Tg[:, :, g, :], start=True, stop=False)
                    pe.matmul(out, HCt[pr, gp, :], CA[0][pr, gp, :], start=False, stop=False)
                    ins = pe.matmul(out, HCt[pr, GP + gp, :], CA[1][pr, gp, :], start=False, stop=True)
                ins.then_inc(S["y_mm"], 1)
            pe.wait_ge(S["y_gl"], 16)
            pe.wait_ge(S["y_in"], 16 * NT)
            for n, (t0, r) in enumerate(TILES):
                for j in range(2):
                    for k in range(4):
                        ins = pe.transpose(psum[:, 2 * n + j, 128 * k:128 * k + r],
                                           y_tok[0:r, n, 128 * (4 * j + k):128 * (4 * j + k + 1)], ident[0:r, 0:r])
                    ins.then_inc(S["yT_tr"], 1)
            pe.wait_ge(S["yT"], 6)
            dense(0, B_GLU, 2, 2, yT, "glu_mm", "glu_b", first=True)
            pe.wait_ge(S["glu_b"], 6)
            pe.wait_ge(S["o_ready"], NT)
            transposes(lambda n, r, dc: (o_tok if dc < 8 else z_tok)[0:r, n, 128 * (dc % 8):128 * (dc % 8) + 128], "s_ready", "mix_tr", "mixT", 4)
            pe.wait_ge(S["mixT"], 12)
            dense(0, B_OUT, 4, 4, mixT, "out_mm", "out_x", first=True)

            pe.wait_ge(S["out_x"], 12)
            transposes(lambda n, r, dc: xn2[0:r, n, 128 * dc:128 * (dc + 1)], "xn2", "tr2", "xn2T", 4)
            pe.wait_ge(S["xn2T"], 12)
            pe.wait_ge(S["x_lo"], 12)

            def product(out, q, column, moving, start, stop):
                c = slice(column, column + 128)
                pe.matmul(out, w_parts[:, q, 0, c], moving(0), start=start, stop=False)
                pe.matmul(out, w_parts[:, q, 0, c], moving(1), start=False, stop=False)
                return pe.matmul(out, w_parts[:, q, 1, c], moving(0), start=False, stop=stop)

            for c in range(4):
                for b in range(4):
                    for q in range(4):
                        pe.wait_ge(S["w_lo"], 16 * c + 4 * b + q + 1)
                        for k in range(4):
                            if c >= 2 and b == q == 0:
                                pe.wait_ge(S["qT"], 4 * (c - 2) + k + 1)
                            ins = product(psum[:, 4 * (c % 2) + k, 0:T], q, 128 * k, lambda p: x_parts[:, p, 4 * b + q, :],
                                          b == q == 0, b == q == 3)
                        ins.then_inc(S["w_used"], 1)
            pe.wait_ge(S["qT"], 16)
            pe.wait_ge(S["keys"], 16)
            for n, (t0, r) in enumerate(TILES):
                for k in range(4):
                    m = 4 * n + k
                    if m >= 8:
                        pe.wait_ge(S["sc_out"], m - 7)
                    for j in range(4):
                        hc = 4 * k + j
                        ins = pe.matmul(psum[0:r, m % 8, 128 * j:128 * j + 128], qT[:, hc, t0:t0 + r], keys[:, 128 * hc:128 * (hc + 1)],
                                        start=True, stop=True)
                    ins.then_inc(S["sc_mm"], 1)
            pe.wait_ge(S["sc_out"], 12)
            def spread_gates(s, i, k, free=True):
                base = SEC * s + k
                pe.wait_ge(S["one"], i * 8 + 2 * (base + 1))
                if free:
                    pe.wait_ge(S["gs_out"], i * 4 + (base - 1))
                for t in range(TOK):
                    for c in range(3):
                        ins = pe.matmul(psum[:, 2 + k % 2, SEC * t:SEC * (t + 1)], oneB[k % 2][:, t, :],
                                        oneA[k % 2][:, c, SEC * t:SEC * (t + 1)], start=c == 0, stop=c == 2)
                ins.then_inc(S["gs_mm"], 1)

            for s in range(SECTIONS):
                def experts_in(i, first=False):
                    for k in range(SLOTS):
                        if not (first and s == 0 and k < 2):
                            pe.wait_ge(S["h_g"], i * 4 + (SEC * s + k - 1))
                        for q in range(4):
                            pe.wait_ge(S["w_lo"], i * 16 + (4 * (a_block(s) + k) + q + 1))
                            for d in range(4):
                                dc = 4 * q + d
                                ins = product(bank(k % 2, T), q, 128 * d, lambda p: x_parts[:, p, dc, :], dc == 0, dc == DC - 1)
                            ins.then_inc(S["w_used"], 1)
                        if s:
                            spread_gates(s, i, k)

                if s:
                    pe.wait_ge(S["e_acc"], 16 * s - 4)
                experts_in(0, True)
                with pe.Fori(1, SEC // SLOTS) as i:
                    experts_in(i)
                if s == 0:
                    for n, (t0, r) in enumerate(TILES):
                        pe.wait_ge(S["picks"], n + 1)
                        for k, src in enumerate((gate, pick_i, pick_j)):
                            ins = pe.transpose(psum[:, 4 + n, 128 * k:128 * k + r], src[0:r, n, :], ident[0:r, 0:r])
                        ins.then_inc(S["pick_tr"], 1)
                    for k in range(4):
                        spread_gates(0, 0, k, k >= 2)
                    with pe.Fori(1, SEC // 4) as i:
                        for k in range(4):
                            spread_gates(0, i, k)
                pe.wait_ge(S["gs_out"], SEC * (s + 1))
                for half in range(2):
                    def experts_out(i, first=False, last=False):
                        for k in range(SLOTS):
                            for q in range(4):
                                ii = q // 2
                                if q % 2 == 0:
                                    pe.wait_ge(S["g_lo"], i * 8 + (SEC * (2 * s + half) + 2 * k + ii + 1))
                                pe.wait_ge(S["w_lo"], i * 16 + (4 * (b_block(s, half) + k) + q + 1))
                                start, stop = first and k == ii == 0, last and k == 3 and ii == 1
                                for d in range(4):
                                    dd = 4 * (q % 2) + d
                                    if start and (s or half):
                                        pe.wait_ge(S["e_acc"], 8 * (2 * s + half - 1) + dd + 1)
                                    ins = product(bank(dd, T), q, 128 * d, lambda p: h_parts[:, ii, p, :], start, stop)
                                    if stop and d < 3:
                                        ins.then_inc(S["e_o"], 1)
                                ins.then_inc(S["w_used"], 1)

                    experts_out(0, first=True)
                    with pe.Fori(1, SEC // 8 - 1) as i:
                        experts_out(i)
                    experts_out(SEC // 8 - 1, last=True)
            for n, (t0, r) in enumerate(TILES):
                for j in range(4):
                    m = 4 * n + j
                    if m == 0:
                        pe.wait_ge(S["e_acc"], 16 * SECTIONS)
                    if m >= 8:
                        pe.wait_ge(S["fin"], m - 7)
                    for k in range(4):
                        ins = pe.transpose(psum[0:r, m % 8, 128 * k:128 * k + 128], acc[:, 4 * j + k, t0:t0 + r], ident[:, :])
                    ins.then_inc(S["fin_tr"], 1)


def stream(w, order=None):
    rows, columns = w.shape
    b = w.reshape(rows // COLS, 4, P, columns // COLS, COLS).transpose(3, 0, 2, 1, 4)
    if order is not None:
        b = b[order]
    return np.ascontiguousarray(b.reshape(-1, P, BLOCK))


def states(a):
    a = a.reshape(GP, 2, SSM_N, *a.shape[2:])
    return np.ascontiguousarray(np.moveaxis(a, 0, 2).reshape(P, GP, *a.shape[3:]).reshape(P, -1))


def kernel(**inputs):
    import concourse.bacc as bacc
    from concourse.bass_utils import run_bass_kernel_spmd

    a = {k: np.asarray(v) for k, v in inputs.items()}
    x = np.concatenate([a["x_prompt"][0], a["x_sample"][0]])
    pos = np.arange(T, dtype=np.float32)
    inv = np.float32(500000.0) ** (-np.arange(8, dtype=np.float32) * np.float32(2.0 / 16))
    ang = (pos[:, None] * inv[None, :]).astype(np.float32)
    rope = np.zeros((P, NT, 16), np.float32)
    for n, (t0, r) in enumerate(TILES):
        rope[:r, n, 0:8] = np.cos(ang[t0:t0 + r])
        rope[:r, n, 8:16] = np.sin(ang[t0:t0 + r])
    mask = np.zeros((P, 2, 256), np.float32)
    for n in range(2):
        q_chunk = (np.arange(P) + 128 * n) // 64
        mask[:, n] = np.where(np.arange(256)[None, :] // 64 <= q_chunk[:, None], 0.0, -1e30)
    dmask = np.zeros((P, SSM_P), np.float32)
    dmask[P - SSM_P:] = np.eye(SSM_P)
    skip = np.concatenate([np.zeros((P - SSM_P, GROUPS), np.float32), a["ssm_d"][0].reshape(GROUPS, SSM_P).T])
    u = a["peer_u"][0].reshape(PK, P, DC, P)
    v = a["peer_v"][0].reshape(SECTIONS, SEC // 2, 2, P, 2, 1024)
    arrays = {
        "x": x, "ident": np.eye(P, dtype=np.float32), "iota": np.arange(P, dtype=np.float32), "rope": rope.reshape(P, -1),
        "mask": mask, "dmask": dmask, "skip": skip,
        "norm1_g": a["norm1_g"][0].reshape(DC, P).T, "norm2_g": a["norm2_g"][0].reshape(DC, P).T,
        "q_g": a["q_norm_g"][0], "k_g": a["k_norm_g"][0], "sub_g": a["subln_g"][0],
        "lq1": a["lambda_q1"][0], "lk1": a["lambda_k1"][0], "lq2": a["lambda_q2"][0], "lk2": a["lambda_k2"][0],
        "a_re": states(a["ssm_a_re"][0]), "a_im": states(a["ssm_a_im"][0]),
        "log_dt": states(np.broadcast_to(a["ssm_log_dt"][0][:, None], (GROUPS, SSM_N))),
        "b_re": states(a["ssm_b_re"][0]), "b_im": states(a["ssm_b_im"][0]),
        "c_re": states(a["ssm_c_re"][0].transpose(0, 2, 1)), "c_im": states(a["ssm_c_im"][0].transpose(0, 2, 1)),
        "h0_re": states(a["state_ssm_re"][0, 0]), "h0_im": states(a["state_ssm_im"][0, 0]),
        "cache_k": a["cache_k"][0, 0].reshape(PAST, HEADS, P).transpose(2, 1, 0),
        "cache_v": a["cache_v"][0, 0].reshape(PAST, 1024),
        "b_glu": a["b_glu"][0],
        "keys": a["peer_keys"][0].transpose(3, 0, 1, 2).reshape(P, D),
        "w_in": stream(a["w_in"][0], [6, 7, 0, 1, 2, 3, 4, 5]),
        "w_glu": stream(a["w_glu"][0]), "w_out": stream(a["w_out"][0]), "w_pq": stream(a["w_peer_q"][0]),
        "peer_u": u.transpose(0, 3, 2, 1).reshape(PK, P, BLOCK),
        "peer_v": v.transpose(0, 4, 1, 3, 2, 5).reshape(PK, P, BLOCK),
    }
    arrays = {k: np.ascontiguousarray(v) for k, v in arrays.items()}
    nc = bacc.Bacc("TRN2", target_bir_lowering=False, num_devices=1)
    io = {k: nc.dram_tensor(f"in_{k}", v.shape, F32, kind="ExternalInput").ap() for k, v in arrays.items()}
    outs = {"y": (T, D), "k_all": (T, 1024), "v_all": (T, 1024), "states": (P, 2, 2 * GP)}
    for k, shape in outs.items():
        io[k] = nc.dram_tensor(f"out_{k}", shape, F32, kind="ExternalOutput").ap()
    for k, n in (("u_tmp", 1024), ("y_tmp", 1024), ("x_tmp", D)):
        io[k] = nc.dram_tensor(k, (T, n), F32, kind="Internal").ap()
    build(nc, io)
    res = run_bass_kernel_spmd(nc, [{f"in_{k}": v for k, v in arrays.items()}], core_ids=[0]).results[0]
    y, k, v, st = (np.asarray(res[f"out_{n}"]) for n in outs)
    st = st.reshape(2, SSM_N, 2, 2, GP).transpose(2, 3, 4, 0, 1).reshape(2, 2, 1, 1, GROUPS, SSM_N)
    kp, ks = (k[s].reshape(1, 1, -1, HEADS, 2, HD) for s in (slice(0, T_PROMPT), slice(T_PROMPT, T)))
    vp, vs = (v[s].reshape(1, 1, -1, HEADS, 2 * HD) for s in (slice(0, T_PROMPT), slice(T_PROMPT, T)))
    return (y[None, :T_PROMPT], y[None, T_PROMPT:], kp, vp, st[0, 0], st[0, 1], ks, vs, st[1, 0], st[1, 1])
```

```python
import math

import numpy as np
import concourse.bass as bass
from concourse import mybir
from contextlib import ExitStack

F32 = mybir.dt.float32
F32R = mybir.dt.float32r
BF16 = mybir.dt.bfloat16
U32 = mybir.dt.uint32
I32 = mybir.dt.int32
ALU = mybir.AluOpType
ACT = mybir.ActivationFunctionType
AX = mybir.AxisListType

P = 128
D = 2048
T_PROMPT, T_SAMPLE = 256, 64
T = T_PROMPT + T_SAMPLE
TILES = [(0, 128), (128, 128), (256, 64)]
NT = len(TILES)
DC = D // P
COLS = 512
BLOCK = 2048
HEADS, HD = 8, 64
PAST = 256
SSM_P, GROUPS, SSM_N = 16, 64, 64
GP = GROUPS // 2
STEP = 8
CH_PROMPT, CH_SAMPLE = T_PROMPT // STEP, T_SAMPLE // STEP
CH = CH_PROMPT + CH_SAMPLE
SEG = CH_SAMPLE
SEGS = CH // SEG
PH, PK, TOPK = 8, 128, 16
HC = 2 * PH
EPS = 1e-6
LAM_INIT = 0.8 - 0.6 * math.exp(-0.3 * 0)
SLOTS = 4
SECTIONS = 4
SEC = PK // SECTIONS
TOK = T // SEC
LOW = -3.0e38
TWO_PI = (6.28125, 0.0019350051879882812, 3.0199159819e-07)

N_IN, N_GLU, N_OUT, N_PQ = 32, 4, 16, 16
B_IN, B_GLU = 0, N_IN
B_OUT = B_GLU + N_GLU
B_PQ = B_OUT + N_OUT
B_EXP = B_PQ + N_PQ


def build(nc, io):
    ctx = ExitStack()

    def sb(name, shape, dt=F32):
        return ctx.enter_context(nc.sbuf_tensor(name, shape, dt))

    def sem(name):
        return ctx.enter_context(nc.semaphore(name))

    with ctx:
        ARENA = 43590
        ring = sb("ring", [P, SLOTS, BLOCK])
        ident = sb("ident", [P, P])
        iota = sb("iota", [P, PK])[:, :]
        with ExitStack() as front:
            arena = front.enter_context(nc.sbuf_tensor("arena", [P, ARENA], F32))
            small = front.enter_context(nc.sbuf_tensor("small", [P, 960], F32))
        with ExitStack() as front:
            xT = front.enter_context(nc.sbuf_tensor("xT", [P, DC, T], F32))[:, :, :]
        with ExitStack() as front:
            front.enter_context(nc.sbuf_tensor("arena_before_xn2T", [P, 12288], F32))
            xn2T = front.enter_context(nc.sbuf_tensor("xn2T", [P, DC, T], F32))[:, :, :]
            front.enter_context(nc.sbuf_tensor("arena_before_gates", [P, 23184 - 17408], F32))
            gates_T = front.enter_context(nc.sbuf_tensor("gates_T", [P, 2, T], F32))
        experts = sb("experts", [P, 28960])
        x_parts = sb("x_parts", [P, 2, DC, T], F32R)
        w_parts = sb("w_parts", [P, 4, 2, 512], F32R)
        h_parts = sb("h_parts", [P, 2, 2, T], F32R)
        psum = ctx.enter_context(nc.psum_tensor("psum", [P, 8, COLS], F32))
        used = [0]

        def stat(*dims):
            n = math.prod(dims)
            used[0] += n
            assert used[0] <= 960, used
            r = small[:, used[0] - n:used[0]]
            return r.rearrange("p (a b) -> p a b", a=dims[0]) if len(dims) == 2 else r

        def at(word, *dims):
            n = math.prod(dims)
            assert word + n <= ARENA, (word, dims)
            r = arena[:, word:word + n]
            if len(dims) == 2:
                return r.rearrange("p (a b) -> p a b", a=dims[0])
            if len(dims) == 3:
                return r.rearrange("p (a b c) -> p a b c", a=dims[0], b=dims[1])
            return r

        def spread(ap, *shape):
            return ap.broadcast_to(list(shape))

        g1, g2 = stat(DC), stat(DC)
        rope = stat(NT, 16)
        qk_g = stat(2, HD)
        sub_g = stat(2 * HD)
        h0 = stat(2 * GP)
        skip = stat(GROUPS)
        lam_in = stat(4, HD)
        ssq, var, rstd = stat(NT), stat(NT), stat(NT)
        nlam = stat(1)
        lam2 = stat(2)
        mx, nb, z, rz = stat(2, 2), stat(2, 2), stat(2, 2), stat(2, 2)
        hs, hv, hr = stat(32), stat(32), stat(32)

        x_tok = at(5120, NT, D)
        proj = at(5120, 4, NT, 1024)
        sq_full = at(17408, D)
        WX = [at(17408, GP, 128), at(21504, GP, 128)]
        tmp_big = at(0, GP, 128)
        bbar = [at(4096, 512), at(4608, 512)]
        PWR, PWI = at(14336, 9, GP), at(14624, 9, GP)
        prm = at(14912, 3, GP)
        sm_ = [at(15008 + 32 * i, GP) for i in range(11)]
        smi = at(15008 + 32 * 11, GP)
        bcin = at(25600, 4, 512)
        nci = at(27648, 512)
        AJR, AJI = at(28160, 8, GP), at(28416, 8, GP)
        CA = [at(29696, GP, 128), at(25600, GP, 128)]
        tmp_ca = [at(33792, GP, 128), at(37888, GP, 128)]
        k7 = at(42016, 1024)
        Tm = at(33792, STEP, 1024)
        mask = at(43040, 2, 256)
        dmask = at(43552, 16)
        qkT = at(0, 16, T)
        ckT, cv = at(5120, HEADS, PAST), at(7168, 2, 1024)
        sm = [at(9216, 2, T), at(9856, 2, T), at(28672, 2, T)]
        wT = at(10496, 2, 3, 128)
        o_tok = at(11264, NT, 1024)
        sq_head = at(5120, 2048)
        rt = at(7168, 4, 256)
        sq_o = at(16384, 1024)
        X = at(0, STEP * 1024)
        dprod = at(6464, GROUPS, SSM_P)
        Xg = at(14336, 2, 1024)
        UG = at(8192, GROUPS, CH)
        FS = at(14336, CH, 2 * GP)
        WTs = at(5440, 2, 512)
        HP = at(0, SEGS * (SEG + 1), 2 * GP).rearrange("p (s c) x -> p s c x", s=SEGS)
        HCt = at(2880, 2 * GP, CH)
        t1, t2 = at(7488, SEGS, 64), at(7808, SEGS, 64)
        far1, far2 = (at(14336 + 1344 * i, 3 * 7, 64).rearrange("p (s c) x -> p s c x", s=3) for i in range(2))
        pw_r, pw_i, pw_t = at(16384, SEG, GP), at(16640, SEG, GP), at(16896, SEG // 2, GP)
        AR, AN = at(43040, SEG, 2 * GP), at(10752, SEG, 2 * GP)
        Y = at(17408, STEP * 1024)
        y_tok = at(14336, NT, 1024)
        z_tok = at(17408, NT, 1024)
        bglu = at(20480, 1024)
        x2 = at(0, NT, D)
        xn2 = at(6144, NT, D)
        qT = at(17408, HC, T)
        keys = at(22528, D)
        sc = at(10240, NT, D)
        sc2 = at(16384, 4, PK)
        cand, cand2 = at(18432, PH, 256), at(16384, PH, 256)
        eq_k = at(18432, PH * TOPK, TOPK)
        base = 24576
        sv, sif = at(base, NT * HC, TOPK), at(base + 768, NT * HC, TOPK)
        si = at(base + 1536, 4 * TOPK).bitcast(U32).rearrange("p (a b) -> p a b", a=4)
        fv = at(base + 1600, PH, TOPK)
        fp = at(base + 1728, 128).bitcast(U32).rearrange("p (a b) -> p a b", a=PH)
        pa_u, pb_u = at(base + 1856, 128).bitcast(U32), at(base + 1984, 128).bitcast(U32)
        pa, pb = at(base + 2112, PH, TOPK), at(base + 2240, PH, TOPK)
        gs = at(base + 2368, PH)
        gate, pick_i, pick_j = at(base + 2376, NT, 128), at(base + 2760, NT, 128), at(base + 3144, NT, 128)
        gT, grest = gates_T[:, 0, :], gates_T[:, 1, :]

        def ex(word, n, dt=F32):
            r = experts[:, word:word + n]
            return r if dt == F32 else r.bitcast(dt)

        H = ex(0, SEC * T).rearrange("p (i t) -> p i t", i=SEC)
        GM = ex(10240, SEC * T).rearrange("p (i t) -> p i t", i=SEC)
        acc = ex(20480, DC * T).rearrange("p (a b) -> p a b", a=DC)
        oneB = [ex(25600 + 640 * i, 640, BF16).rearrange("p (a b) -> p a b", a=TOK) for i in range(2)]
        oneA = [ex(26880 + 480 * i, 480, BF16).rearrange("p (a b) -> p a b", a=3) for i in range(2)]
        eqA = [ex(27840 + 160 * i, 160, BF16).rearrange("p (a b) -> p a b", a=TOK) for i in range(2)]
        iT, jT = ex(28160, 160, BF16), ex(28320, 160, BF16)
        gpart = ex(28480, 480, BF16).rearrange("p (a b) -> p a b", a=3)
        x3 = ex(0, NT * D).rearrange("p (a b) -> p a b", a=NT)
        def a_block(s):
            return B_EXP + 2 * SEC * s

        def b_block(s, half):
            return a_block(s) + SEC + half * SEC // 2

        xd = x_parts[:, :, :, :].rearrange("p a d t -> p (a d t)").rearrange("p (d c) -> p d c", d=DC)
        LOW_AT = (384, 512, 320)

        def dense_part(p, j, n):
            t0 = LOW_AT[n] if p else TILES[n][0]
            return xd[:, 4 * j:4 * j + 4, t0:t0 + TILES[n][1]]

        def peer_part(p, j, n):
            t0, r = TILES[n]
            return x_parts[:, p, 4 * j:4 * j + 4, t0:t0 + r]

        fold = at(25600, COLS)

        def bank(b, n=COLS):
            return psum[:, b, 0:n]

        names = """consts x0 x1 x2 ssq var std xn tr1 xT x1_hi x1_lo mask ca dk
            slot0 slot1 slot2 slot3 in_mm in_out in_fold u_saved s5in
            lam_e lam s5dt s5exp s5sin s5w k7mm k7out k7st tz v_out k_out
            hvar hstd qk_ready qk_tr qkT  xg cache s_mm s_sm s_mx s_exp w_ready w_tr wT wT_part pv o_out
            ovar ostd o_ready xs ug_tr ug wt_tr wt f_mm f_out hp hc h_out y_mm y_gl y_save y_in0 y_in1
            yT_tr y_hi y_lo glu_mm glu_b glu_s s_ready mix_tr mix_hi mix_lo x_re out_mm out_x bg
            ssq2 var2 std2 xn2 tr2 xn2T keys x_hi qT sc_mm sc_out gmx gex picks pick_tr
            x_lo w_hi w_lo w_used one eq gs_mm gs_out h_g e_w g_lo g_hi e_o e_acc x_sv x_bk fin_tr fin y_out dve rec""".split()
        S = {n: sem(n) for n in names}

        class Chain:

            def __init__(self, eng, name):
                self.eng, self.sem, self.n = eng, S[name], 0

            def add(self, ins):
                self.n += 1
                ins.then_inc(self.sem, 1)

            def wait(self):
                self.eng.wait_ge(self.sem, self.n)

            def __call__(self, ins):
                self.add(ins)
                self.wait()

        block = ctx.enter_context(nc.Block())

        CONSTS = [(ident[:, :], io["ident"]), (g1, io["norm1_g"]), (g2, io["norm2_g"]),
                  (iota, io["iota"].partition_broadcast(P)), (rope, io["rope"]), (qk_g[:, 0, :], io["q_g"].partition_broadcast(P)),
                  (qk_g[:, 1, :], io["k_g"].partition_broadcast(P)), (sub_g, io["sub_g"].partition_broadcast(P)),
                  (h0[:, 0:GP], io["h0_re"]), (h0[:, GP:], io["h0_im"]), (dmask, io["dmask"]),
                  (skip, io["skip"])] + [
                      (lam_in[:, i, :], io[n].partition_broadcast(P)) for i, n in enumerate(("lq1", "lq2", "lk1", "lk2"))]
        S5IN = [(prm[:, 0, :], io["a_re"]), (prm[:, 1, :], io["a_im"]), (prm[:, 2, :], io["log_dt"])] + [
            (bcin[:, i, :], io[n]) for i, n in enumerate(("b_re", "b_im", "c_re", "c_im"))]
        ALL_CONSTS = 16 * len(CONSTS)

        @block.sync
        def _(sp):
            for n, (t0, r) in enumerate(TILES):
                sp.dma_start(x_tok[0:r, n, :], io["x"][t0:t0 + r, :]).then_inc(S[f"x{n}"], 16)

            def turn(source, first, base, i, free=True):
                for s in range(SLOTS):
                    src = io[source][bass.ds(i * SLOTS + (first + s), 1)].rearrange("o p n -> (o p) n")
                    if free:
                        sp.wait_ge(S["w_lo"], i * (4 * SLOTS) + 4 * (base + s - SLOTS + 1))
                    sp.dma_start(ring[:, s, :], src).then_inc(S[f"slot{s}"], 16)

            sp.wait_ge(S["x2"], 16)
            turn("w_in", 0, B_IN, 0, free=False)
            with sp.Fori(1, N_IN // SLOTS // 2) as i:
                turn("w_in", 0, B_IN, i)
            sp.wait_ge(S["in_out"], 2 * NT)
            sp.wait_ge(S["in_fold"], 2)
            for n, (t0, r) in enumerate(TILES):
                sp.dma_start(io["u_tmp"][t0:t0 + r, :], proj[0:r, 0, n, :]).then_inc(S["u_saved"], 16)
            with sp.Fori(N_IN // SLOTS // 2, N_IN // SLOTS) as i:
                turn("w_in", 0, B_IN, i)
            turn("w_glu", 0, B_GLU, 0)
            sp.wait_ge(S["qk_ready"], NT)
            for n, (t0, r) in enumerate(TILES):
                sp.dma_start(io["k_all"][t0:t0 + r, :], proj[0:r, 2, n, :]).then_inc(S["k_out"], 16)
            sp.wait_ge(S["in_out"], 8 * NT)
            sp.wait_ge(S["in_fold"], 8)
            for n, (t0, r) in enumerate(TILES):
                sp.dma_start(io["v_all"][t0:t0 + r, :], proj[0:r, 3, n, :]).then_inc(S["v_out"], 16)
            sp.wait_ge(S["k_out"], 16 * NT)
            sp.wait_ge(S["qkT"], 12)
            sp.wait_ge(S["u_saved"], 16 * NT)
            sp.dma_start(ckT, io["cache_k"]).then_inc(S["cache"], 16)
            for b in range(2):
                sp.dma_start(cv[:, b, :], io["cache_v"][b * P:(b + 1) * P, :]).then_inc(S["cache"], 16)
            sp.wait_ge(S["pv"], NT * HEADS)
            sp.wait_ge(S["v_out"], 16 * NT)
            sp.dma_start(X[0:CH, :], io["u_tmp"].rearrange("(c i) n -> c (i n)", i=STEP)).then_inc(S["xs"], 16)
            sp.wait_ge(S["hp"], 1)
            sp.dma_start(io["states"][:, 0, :], HP[:, SEGS - 2, SEG, :]).then_inc(S["h_out"], 16)
            sp.dma_start(io["states"][:, 1, :], HP[:, SEGS - 1, SEG, :]).then_inc(S["h_out"], 16)
            for half in range(2):
                cc = slice(512 * half, 512 * (half + 1))
                sp.wait_ge(S["y_gl"], 8 * (half + 1))
                sp.dma_start(io["y_tmp"].rearrange("(c i) n -> c i n", i=STEP)[:, :, cc],
                               Y[0:CH, :].rearrange("p (i n) -> p i n", i=STEP)[:, :, cc]).then_inc(S["y_save"], 16)
                sp.wait_ge(S["hc"], 1)
                sp.wait_ge(S["y_save"], 16 * (half + 1))
                for n, (t0, r) in enumerate(TILES):
                    sp.dma_start(y_tok[0:r, n, cc], io["y_tmp"][t0:t0 + r, cc]).then_inc(S[f"y_in{half}"], 16)
            sp.dma_start(bglu, io["b_glu"].partition_broadcast(P)).then_inc(S["bg"], 16)
            sp.wait_ge(S["h_out"], 32)
            sp.wait_ge(S["y_mm"], 16)
            for n, (t0, r) in enumerate(TILES):
                sp.dma_start(x2[0:r, n, :], io["x"][t0:t0 + r, :]).then_inc(S["x_re"], 16)
            sp.dma_start(keys, io["keys"]).then_inc(S["keys"], 16)
            with sp.Fori(0, N_OUT // SLOTS) as i:
                turn("w_out", 0, B_OUT, i)
            turn("w_pq", 0, B_PQ, 0)
            sp.wait_ge(S["out_x"], 12)
            for n, (t0, r) in enumerate(TILES):
                sp.dma_start(io["x_tmp"][t0:t0 + r, :], x2[0:r, n, :]).then_inc(S["x_sv"], 16)
            with sp.Fori(1, N_PQ // SLOTS) as i:
                turn("w_pq", 0, B_PQ, i)
            for s in range(SECTIONS):
                with sp.Fori(0, SEC // SLOTS) as i:
                    turn("peer_u", s * SEC, a_block(s), i)
                with sp.Fori(0, SEC // SLOTS) as i:
                    turn("peer_v", s * SEC, b_block(s, 0), i)
            sp.wait_ge(S["g_lo"], 2 * PK)
            sp.wait_ge(S["x_sv"], 16 * NT)
            for n, (t0, r) in enumerate(TILES):
                sp.dma_start(x3[0:r, n, :], io["x_tmp"][t0:t0 + r, :]).then_inc(S["x_bk"], 16)
            for n, (t0, r) in enumerate(TILES):
                sp.wait_ge(S["fin"], 4 * (n + 1))
                sp.dma_start(io["y"][t0:t0 + r, :], x3[0:r, n, :]).then_inc(S["y_out"], 16)
            sp.wait_ge(S["y_out"], 16 * NT)

        @block.gpsimd
        def _(pool):
            pool.wait_ge(S["x2"], 16)
            for dst, src in S5IN:
                pool.dma_start(dst, src).then_inc(S["s5in"], 16)

            def low_parts(first, end):
                with pool.Fori(first // SLOTS, end // SLOTS) as i:
                    for k in range(SLOTS):
                        for q in range(4):
                            pool.wait_ge(S["w_hi"], i * (4 * SLOTS) + (4 * k + q + 1))
                            pool.tensor_tensor(w_parts[:, q, 1, :], ring[:, k, 512 * q:512 * (q + 1)], w_parts[:, q, 0, :].bitcast(F32),
                                               ALU.subtract).then_inc(S["w_lo"], 1)

            low_parts(B_IN, B_IN + N_IN)
            pool.wait_ge(S["in_out"], 8 * NT)
            pool.dma_start(mask, io["mask"]).then_inc(S["mask"], 16)
            pool.wait_ge(S["s5w"], 1)
            four = (P, GP, STEP, SSM_P)

            def cols(ap):
                return ap.rearrange("p g (j n) -> p g j n", j=STEP)

            def steps(ap):
                return spread(ap.rearrange("p j g -> p g j").unsqueeze(3), *four)

            def chans(ap):
                return spread(ap.rearrange("p (g n) -> p g n", g=GP).unsqueeze(2), *four)

            rr, ri, cre, cim, ncim = steps(AJR), steps(AJI), chans(bcin[:, 2, :]), chans(bcin[:, 3, :]), chans(nci)
            pool.tensor_tensor(cols(CA[0]), rr, cre, ALU.mult).then_inc(S["ca"], 1)
            pool.tensor_tensor(cols(tmp_ca[0]), ri, cim, ALU.mult).then_inc(S["ca"], 1)
            pool.wait_ge(S["ca"], 2)
            pool.tensor_tensor(CA[0], CA[0], tmp_ca[0], ALU.subtract).then_inc(S["ca"], 1)
            pool.tensor_tensor(cols(tmp_ca[1]), ri, cre, ALU.mult).then_inc(S["ca"], 1)
            pool.wait_ge(S["ca"], 3)
            pool.tensor_tensor(cols(tmp_ca[0]), rr, ncim, ALU.mult).then_inc(S["ca"], 1)
            pool.wait_ge(S["ca"], 5)
            pool.wait_ge(S["k7mm"], 2)
            pool.wait_ge(S["w_tr"], NT * HEADS)
            pool.tensor_tensor(CA[1], tmp_ca[0], tmp_ca[1], ALU.subtract).then_inc(S["ca"], 1)
            pool.wait_ge(S["ca"], 6)
            pool.memset(Tm, 0.0).then_inc(S["tz"], 1)
            pool.wait_ge(S["tz"], 1)
            pool.wait_ge(S["k7out"], 2)
            pool.wait_ge(S["xg"], 8)
            pool.tensor_tensor(dprod, spread(skip.unsqueeze(2), P, GROUPS, SSM_P), spread(dmask.unsqueeze(1), P, GROUPS, SSM_P),
                               ALU.mult).then_inc(S["dk"], 1)
            pool.wait_ge(S["dk"], 1)
            pool.tensor_tensor(k7, k7, dprod.rearrange("p g n -> p (g n)"), ALU.add).then_inc(S["dk"], 1)
            pool.wait_ge(S["dk"], 2)
            for j in range(STEP):
                n = SSM_P * (j + 1)
                pool.dma_start(Tm[0:n, j, :], k7[P - n:P, :]).then_inc(S["k7st"], 16)
            low_parts(B_GLU, B_EXP + 2 * PK)

        @block.scalar
        def _(act):
            for dst, src in CONSTS:
                act.dma_start(dst, src).then_inc(S["consts"], 16)

            for n, (t0, r) in enumerate(TILES):
                act.wait_ge(S[f"x{n}"], 16)
                act.activation(sq_full[0:r, :], x_tok[0:r, n, :], ACT.Square, accum_out=ssq[0:r, n:n + 1]).then_inc(S["ssq"], 1)
                act.wait_ge(S["ssq"], n + 1)
            for n, (t0, r) in enumerate(TILES):
                act.wait_ge(S["var"], n + 1)
                act.activation(var[0:r, n:n + 1], var[0:r, n:n + 1], ACT.Sqrt).then_inc(S["std"], 1)
            def high_rows(j, part, ready, hi_s, src=None):
                for n, (t0, r) in enumerate(TILES):
                    m = NT * j + n
                    act.wait_ge(S[ready], m + 1)
                    rows = bank(4 + m % 4).rearrange("p (a b) -> p a b", a=4)[:, :, 0:r] if src is None else src[:, 4 * j:4 * j + 4, t0:t0 + r]
                    act.activation(part(0, j, n), rows, ACT.Copy).then_inc(S[hi_s], 1)

            def start_product(block, *rows):
                high_rows(0, *rows)
                high_rows(1, *rows)
                for b in range(1, 4):
                    high(0, block + b)
                    if b < 3:
                        high_rows(b + 1, *rows)

            def high(i, b, turn=SLOTS):
                k = b % SLOTS
                act.wait_ge(S[f"slot{k}"], i * (16 * turn // SLOTS) + 16 * (b // SLOTS + 1))
                for q in range(4):
                    if not (isinstance(i, int) and i == b == 0):
                        act.wait_ge(S["w_used"], i * (4 * turn) + (4 * b + q - 3))
                    act.activation(w_parts[:, q, 0, :], ring[:, k, 512 * q:512 * (q + 1)], ACT.Copy).then_inc(S["w_hi"], 1)

            high(0, B_IN)
            start_product(B_IN, dense_part, "xT", "x1_hi", xT)
            act.wait_ge(S["lam_e"], 1)
            act.activation(lam2, lam2, ACT.Exp).then_inc(S["lam"], 1)
            act.wait_ge(S["s5in"], 16 * len(S5IN))
            act.activation(prm[:, 2, :], prm[:, 2, :], ACT.Exp).then_inc(S["s5exp"], 1)
            act.wait_ge(S["s5dt"], 1)
            act.activation(sm_[0], sm_[0], ACT.Exp).then_inc(S["s5exp"], 1)
            act.wait_ge(S["s5dt"], 2)
            act.activation(sm_[1], sm_[1], ACT.Sin).then_inc(S["s5sin"], 1)
            act.activation(sm_[2], sm_[2], ACT.Sin).then_inc(S["s5sin"], 1)

            def evac_in(i, c2):
                for n, (t0, r) in enumerate(TILES):
                    dst = proj[0:r, bass.ds(i, 1), n, c2 * COLS:(c2 + 1) * COLS].rearrange("p o n -> p (o n)")
                    act.wait_ge(S["in_mm"], i * (2 * NT) + (c2 * NT + n + 1))
                    act.activation(dst, psum[0:r, 3 * c2 + n, :] if n < 2 else psum[64:128, 3 * c2 + n, :], ACT.Copy).then_inc(S["in_out"], 1)

            for b in range(4, 8):
                high(0, b)
                if b == 4:
                    evac_in(0, 0)
            with act.Fori(1, 3) as i:
                for b in range(8):
                    high(i, b, 8)
                    if b == 0:
                        evac_in(i - 1, 1)
                    if b == 4:
                        evac_in(i, 0)
            act.wait_ge(S["s5w"], 1)
            for b in range(8):
                high(3, b, 8)
                if b == 0:
                    evac_in(2, 1)
                if b == 4:
                    evac_in(3, 0)
                if b in (1, 3, 5):
                    n, r = b // 2, TILES[b // 2][1]
                    act.wait_ge(S["hvar"], n + 1)
                    act.activation(hv[0:r, :], hv[0:r, :], ACT.Sqrt).then_inc(S["hstd"], 1)
            evac_in(3, 1)

            for n, (t0, r) in enumerate(TILES):
                for j in range(4):
                    act.wait_ge(S["qk_tr"], 4 * n + j + 1)
                    act.activation(qkT[:, 4 * j:4 * j + 4, t0:t0 + r],
                                   bank((4 * n + j) % 8).rearrange("p (a b) -> p a b", a=4)[:, :, 0:r], ACT.Copy).then_inc(S["qkT"], 1)
            keys_of = [128, 256, 320]

            def products_out(parity):
                act.wait_ge(S["k7mm"], parity + 1)
                act.activation(k7.rearrange("p (g c n) -> p c g n", c=2, n=SSM_P)[:, parity],
                               bank(5).rearrange("p (g n) -> p g n", g=GP), ACT.Copy).then_inc(S["k7out"], 1)

            def weights_T(u):
                n, h = divmod(u, HEADS)
                r, kk = TILES[n][1], keys_of[n]
                act.wait_ge(S["w_tr"], u + 1)
                if u >= 2:
                    act.wait_ge(S["pv"], u - 1)
                full = kk // P
                src = bank(4).rearrange("p (a b) -> p a b", a=4)
                act.activation(wT[:, u % 2, 0:full, 0:r], src[:, 0:full, 0:r], ACT.Copy).then_inc(S["wT"], 1)
                if kk % P:
                    act.activation(wT[0:64, u % 2, full, 0:r], src[0:64, full, 0:r], ACT.Copy).then_inc(S["wT_part"], 1)

            for u in range(NT * HEADS):
                n, h = divmod(u, HEADS)
                r, kk = TILES[n][1], keys_of[n]
                for c in range(2):
                    act.wait_ge(S["s_mx"], u + 1)
                    act.activation(sm[u % 3][0:r, c, 0:kk], sm[u % 3][0:r, c, 0:kk], ACT.Exp,
                                   bias=nb[0:r, u % 2, c:c + 1], scale=HD ** -0.5,
                                   accum_out=z[0:r, u % 2, c:c + 1]).then_inc(S["s_exp"], 1)
                if u:
                    weights_T(u - 1)
                if u == 12:
                    products_out(0)
            weights_T(NT * HEADS - 1)
            products_out(1)
            for k in range(8):
                act.wait_ge(S["ug_tr"], k + 1)
                act.activation(UG[:, 8 * k:8 * k + 8, :], bank(k, 320).rearrange("p (a b) -> p a b", a=8), ACT.Copy).then_inc(S["ug"], 1)
            for q in range(16):
                act.wait_ge(S["wt_tr"], q + 1)
                if q >= 2:
                    act.wait_ge(S["f_mm"], q - 1)
                act.activation(WTs[:, q % 2, :], bank(6 + q % 2), ACT.Copy).then_inc(S["wt"], 1)
                if q in (2, 5, 8):
                    n, r = q // 3, TILES[q // 3][1]
                    act.wait_ge(S["ovar"], n + 1)
                    act.activation(hv[0:r, 0:HEADS], hv[0:r, 0:HEADS], ACT.Sqrt).then_inc(S["ostd"], 1)
            for q in range(16):
                act.wait_ge(S["y_mm"], q + 1)
                dst = Y[0:CH, :].rearrange("p (j g n) -> p g j n", j=STEP, g=GROUPS)
                for g4 in range(4):
                    ins = act.activation(dst[:, 8 * (q // 2) + 2 * g4 + q % 2], psum[0:CH, q % 8, 128 * g4:128 * g4 + 128].rearrange("p (j n) -> p j n", j=STEP),
                                         ACT.Gelu_apprx_tanh)
                ins.then_inc(S["y_gl"], 1)
            high(0, B_GLU)
            high_rows(0, dense_part, "yT_tr", "y_hi")
            high(0, B_GLU + 1)
            high_rows(1, dense_part, "yT_tr", "y_hi")
            for b in range(2, N_GLU):
                high(0, B_GLU + b)
            high(0, B_OUT)
            for c in range(2):
                for n, (t0, r) in enumerate(TILES):
                    act.wait_ge(S["glu_b"], 3 * c + n + 1)
                    zz = z_tok[0:r, n, c * COLS:(c + 1) * COLS]
                    act.activation(zz, zz, ACT.Sigmoid).then_inc(S["glu_s"], 1)
            start_product(B_OUT, dense_part, "mix_tr", "mix_hi")
            with act.Fori(1, N_OUT // SLOTS) as i:
                for b in range(SLOTS):
                    high(i, B_OUT + b)
            high(0, B_PQ)

            for n, (t0, r) in enumerate(TILES):
                act.wait_ge(S["out_x"], 9 + n + 1)
                act.activation(xn2[0:r, n, :], x2[0:r, n, :], ACT.Square, accum_out=ssq[0:r, n:n + 1]).then_inc(S["ssq2"], 1)
                act.wait_ge(S["ssq2"], n + 1)
            for n, (t0, r) in enumerate(TILES):
                act.wait_ge(S["var2"], n + 1)
                act.activation(var[0:r, n:n + 1], var[0:r, n:n + 1], ACT.Sqrt).then_inc(S["std2"], 1)
            start_product(B_PQ, peer_part, "xn2T", "x_hi", xn2T)

            def queries_out(c):
                act.wait_ge(S["w_used"], 4 * B_PQ + 16 * (c + 1))
                for k in range(4):
                    act.activation(qT[:, 4 * c + k, :], bank(4 * (c % 2) + k, T), ACT.Copy).then_inc(S["qT"], 1)

            def scores_out(c):
                for n, (t0, r) in enumerate(TILES):
                    act.wait_ge(S["sc_mm"], NT * c + n + 1)
                    act.activation(sc[0:r, n, COLS * c:COLS * (c + 1)], psum[0:r, 4 * (c % 2) + n, :], ACT.Copy).then_inc(S["sc_out"], 1)

            for b in range(4, N_PQ):
                high(0, B_PQ + b)
                if b % 4 == 0:
                    queries_out(b // 4 - 1)
                if b > 4 and b % 4 == 1:
                    scores_out(b // 4 - 1)
            high(0, a_block(0))
            queries_out(3)

            def gelu(s, i, k):
                act.wait_ge(S["w_used"], i * 16 + 4 * (a_block(s) + k + 1))
                act.activation(H[:, bass.ds(i * 4 + k, 1), :].rearrange("p o t -> p (o t)"), bank(k % 2, T),
                               ACT.Gelu_apprx_tanh).then_inc(S["h_g"], 1)

            act.wait_ge(S["x_sv"], 16 * NT)
            turns = SEC // SLOTS
            for s in range(SECTIONS):
                a, b0 = a_block(s), b_block(s, 0)
                if s:
                    act.wait_ge(S["e_w"], SEC * s)
                    act.wait_ge(S["g_lo"], 2 * SEC * s)

                def gelus(i, first, first_k=0):
                    for k in range(first_k, SLOTS):
                        high(i, a + first + k)
                        gelu(s, i + (-1 if k == 0 else 0), first + (k - 1) % SLOTS)

                high(0, a + 1)
                gelu(s, 0, 0)
                if s == 0:
                    scores_out(3)
                gelus(0, 0, 2)
                if s == 0:
                    with act.Fori(1, turns // 2) as i:
                        gelus(i, 0)
                    high(0, a + SEC // 2)
                    gelu(0, 0, SEC // 2 - 1)
                    for n, (t0, r) in enumerate(TILES):
                        act.wait_ge(S["gmx"], n + 1)
                        act.activation(gate[0:r, n, :], gate[0:r, n, :], ACT.Exp).then_inc(S["gex"], 1)
                    gelus(0, SEC // 2, 1)
                    with act.Fori(1 + turns // 2, turns) as i:
                        gelus(i, 0)
                else:
                    with act.Fori(1, turns) as i:
                        gelus(i, 0)
                high(0, b0)
                gelu(s, turns - 1, SLOTS - 1)
                for k in range(1, SLOTS):
                    high(0, b0 + k)
                with act.Fori(1, turns) as i:
                    for k in range(SLOTS):
                        high(i, b0 + k)
                if s + 1 < SECTIONS:
                    high(0, a_block(s + 1))

        @block.vector
        def _(dve):
            chain = Chain(dve, "dve")

            def tt(out, a, b, op):
                return dve.tensor_tensor(out, a, b, op)

            def var_of(dst, src, n):
                return dve.tensor_scalar(dst, src, 1.0 / n, EPS, ALU.mult, ALU.add)

            def norm_rows(src, dst, ssq_s, var_s, std_s, xn_s):
                for n, (t0, r) in enumerate(TILES):
                    dve.wait_ge(S[ssq_s], n + 1)
                    var_of(var[0:r, n:n + 1], ssq[0:r, n:n + 1], D).then_inc(S[var_s], 1)
                for n, (t0, r) in enumerate(TILES):
                    dve.wait_ge(S[std_s], n + 1)
                    chain(dve.reciprocal(rstd[0:r, n:n + 1], var[0:r, n:n + 1]))
                    dve.tensor_scalar(dst[0:r, n, :], src[0:r, n, :], rstd[0:r, n:n + 1], None, ALU.mult).then_inc(S[xn_s], 1)

            def folded(b):
                chain(dve.tensor_copy(fold[0:64, :], psum[64:128, b, :]))
                chain(tt(fold[0:64, :], psum[0:64, b, :], fold[0:64, :], ALU.add))
                return fold[0:64, :]

            def gain_out(j, dst, gain, tr_s, out_s):
                for n, (t0, r) in enumerate(TILES):
                    m = NT * j + n
                    dve.wait_ge(S[tr_s], m + 1)
                    tt(dst[:, 4 * j:4 * j + 4, t0:t0 + r], bank(4 + m % 4).rearrange("p (a b) -> p a b", a=4)[:, :, 0:r],
                       spread(gain[:, 4 * j:4 * j + 4].unsqueeze(2), P, 4, r), ALU.mult).then_inc(S[out_s], 1)

            def low_rows(j, parts, hi_s, lo_s, src=None):
                for n, (t0, r) in enumerate(TILES):
                    m = NT * j + n
                    rows = (bank(4 + m % 4).rearrange("p (a b) -> p a b", a=4)[:, :, 0:r] if src is None
                            else src[:, 4 * j:4 * j + 4, t0:t0 + r])
                    dve.wait_ge(S[hi_s], m + 1)
                    tt(parts(1, j, n), rows, parts(0, j, n).bitcast(F32), ALU.subtract).then_inc(S[lo_s], 1)

            def rows_out(dst, gain, tr_s, out_s, parts, hi_s, lo_s):
                for j in range(5):
                    if j < 4:
                        gain_out(j, dst, gain, tr_s, out_s)
                    if j:
                        low_rows(j - 1, parts, hi_s, lo_s, dst)

            norm_rows(x_tok, x_tok, "ssq", "var", "std", "xn")
            dve.wait_ge(S["consts"], ALL_CONSTS)
            rows_out(xT, g1, "tr1", "xT", dense_part, "x1_hi", "x1_lo")

            chain(tt(lam_in[:, 0:2, :], lam_in[:, 0:2, :], lam_in[:, 2:4, :], ALU.mult))
            dve.tensor_reduce(lam2, lam_in[:, 0:2, :], AX.X, ALU.add).then_inc(S["lam_e"], 1)
            dve.wait_ge(S["lam"], 1)
            chain(tt(nlam, lam2[:, 1:2], lam2[:, 0:1], ALU.subtract))
            chain(dve.tensor_scalar(nlam, nlam, -LAM_INIT, None, ALU.add))

            are, aim, dt = prm[:, 0, :], prm[:, 1, :], prm[:, 2, :]
            mag, half, full = sm_[0], sm_[1], sm_[2]
            ang, cosv, den, nr, cr, ci, ta, tb = sm_[3:11]
            dve.wait_ge(S["s5exp"], 1)
            tt(mag, dt, are, ALU.mult).then_inc(S["s5dt"], 1)
            chain(tt(ang, dt, aim, ALU.mult))
            chain(dve.tensor_scalar(ta, ang, 1.0 / (2 * math.pi), None, ALU.mult))
            chain(dve.tensor_copy(smi.bitcast(I32), ta))
            chain(dve.tensor_copy(tb, smi.bitcast(I32)))
            for part in TWO_PI:
                chain(dve.scalar_tensor_tensor(ang, tb, -part, ang, ALU.mult, ALU.add))
            chain(dve.tensor_scalar(full, ang, 3.1415925, -3.1415925, ALU.min, ALU.max))
            dve.tensor_scalar(half, ang, 0.5, None, ALU.mult).then_inc(S["s5dt"], 1)
            dve.wait_ge(S["s5exp"], 2)
            dve.wait_ge(S["s5sin"], 2)
            chain(tt(cosv, half, half, ALU.mult))
            chain(dve.tensor_scalar(cosv, cosv, -2.0, 1.0, ALU.mult, ALU.add))
            chain(dve.memset(PWR[:, 8, :], 1.0))
            chain(dve.memset(PWI[:, 8, :], 0.0))
            chain(tt(AJR[:, 0, :], mag, cosv, ALU.mult))
            chain(tt(AJI[:, 0, :], mag, full, ALU.mult))
            chain(tt(den, are, are, ALU.mult))
            chain(tt(ta, aim, aim, ALU.mult))
            chain(tt(den, den, ta, ALU.add))
            chain(dve.reciprocal(den, den))
            chain(dve.tensor_scalar(nr, AJR[:, 0, :], -1.0, None, ALU.add))
            chain(tt(cr, nr, are, ALU.mult))
            chain(tt(ta, AJI[:, 0, :], aim, ALU.mult))
            chain(tt(cr, cr, ta, ALU.add))
            chain(tt(cr, cr, den, ALU.mult))
            chain(tt(ci, AJI[:, 0, :], are, ALU.mult))
            chain(tt(ta, nr, aim, ALU.mult))
            chain(tt(ci, ci, ta, ALU.subtract))
            chain(tt(ci, ci, den, ALU.mult))

            def times(outr, outi, ar, ai, br, bi, tmp):
                chain(tt(outr, ar, br, ALU.mult))
                chain(tt(tmp, ai, bi, ALU.mult))
                chain(tt(outr, outr, tmp, ALU.subtract))
                chain(tt(outi, ar, bi, ALU.mult))
                chain(tt(tmp, ai, br, ALU.mult))
                chain(tt(outi, outi, tmp, ALU.add))

            for k in (1, 2, 4):
                shape = (P, k, GP)
                by = (spread(AJR[:, k - 1:k, :], *shape), spread(AJI[:, k - 1:k, :], *shape))
                scr = tmp_big[:, 0:1, :].rearrange("p a b -> p (a b)")[:, 0:k * GP].rearrange("p (a b) -> p a b", a=k)
                times(AJR[:, k:2 * k, :], AJI[:, k:2 * k, :], AJR[:, 0:k, :], AJI[:, 0:k, :], *by, scr)
            for k in range(1, 9):
                chain(dve.tensor_copy(PWR[:, 8 - k, :], AJR[:, k - 1, :]))
                chain(dve.tensor_copy(PWI[:, 8 - k, :], AJI[:, k - 1, :]))
            def per_channel(ap):
                return spread(ap.unsqueeze(2), P, GP, SSM_P)

            def grp(ap):
                return ap.rearrange("p (g n) -> p g n", g=GP)

            times(grp(bbar[0]), grp(bbar[1]), per_channel(cr), per_channel(ci), grp(bcin[:, 0, :]), grp(bcin[:, 1, :]),
                  grp(tmp_big.rearrange("p a b -> p (a b)")[:, 0:512]))

            def fold_in(c):
                kind, c2 = divmod(c, 2)
                dst = proj[0:64, kind, 2, c2 * COLS:(c2 + 1) * COLS]
                dve.wait_ge(S["in_out"], NT * (c + 1))
                tt(dst, psum[0:64, 3 * c2 + 2, :], dst, ALU.add).then_inc(S["in_fold"], 1)

            four = (P, GP, STEP, SSM_P)

            def cols(ap):
                return ap.rearrange("p g (j n) -> p g j n", j=STEP)

            def steps(ap):
                return spread(ap.rearrange("p j g -> p g j").unsqueeze(3), *four)

            def chans(ap):
                return spread(grp(ap).unsqueeze(2), *four)

            qr, qi, br, bi = steps(PWR[:, 1:9, :]), steps(PWI[:, 1:9, :]), chans(bbar[0]), chans(bbar[1])
            for w, x, y, op in ((WX[0], br, bi, ALU.subtract), (WX[1], bi, br, ALU.add)):
                chain(tt(cols(w), qr, x, ALU.mult))
                chain(tt(cols(tmp_big), qi, y, ALU.mult))
                chain(tt(w, w, tmp_big, op))
                if w is WX[0]:
                    fold_in(0)
            chain(dve.tensor_scalar(nci, bcin[:, 3, :], -1.0, None, ALU.mult))
            a8 = lam_in.rearrange("p a b -> p (a b)")
            a8r, a8n = a8[:, 0:64], a8[:, 64:128]
            chain(dve.tensor_copy(a8r[:, 0:32], AJR[:, 7, :]))
            chain(dve.tensor_copy(a8r[:, 32:64], AJR[:, 7, :]))
            chain(dve.tensor_scalar(a8n[:, 0:32], AJI[:, 7, :], -1.0, None, ALU.mult))
            chain(dve.tensor_copy(a8n[:, 32:64], AJI[:, 7, :]))
            dve.sem_inc(S["s5w"], 1)
            for c in range(1, 6):
                fold_in(c)
            dve.wait_ge(S["in_fold"], 6)
            dve.wait_ge(S["u_saved"], 16 * NT)
            for n, (t0, r) in enumerate(TILES):
                v = proj[0:r, 1:3, n, :].rearrange("p k (h d) -> p k h d", d=HD)
                sq = sq_head[0:r, :].rearrange("p (k h d) -> p k h d", k=2, d=HD)
                heads = (r, 2, 16, HD)

                def per_head(ap):
                    return spread(ap[0:r, :].rearrange("p (k h) -> p k h", k=2).unsqueeze(3), *heads)

                chain(tt(sq, v, v, ALU.mult))
                chain(dve.tensor_reduce(hs[0:r, :], sq_head[0:r, :].rearrange("p (g d) -> p g d", d=HD), AX.X, ALU.add))
                var_of(hv[0:r, :], hs[0:r, :], HD).then_inc(S["hvar"], 1)
                dve.wait_ge(S["hstd"], n + 1)
                chain(dve.reciprocal(hr[0:r, :], hv[0:r, :]))
                chain(tt(v, v, per_head(hr), ALU.mult))
                chain(tt(v, v, spread(qk_g[0:r].unsqueeze(2), *heads), ALU.mult))
                half = (r, 2, 16, 8)
                a, b = v[:, :, :, 0:8], v[:, :, :, 8:16]
                cosr = spread(rope[0:r, n, 0:8].unsqueeze(1).unsqueeze(1), *half)
                sinr = spread(rope[0:r, n, 8:16].unsqueeze(1).unsqueeze(1), *half)
                m = [rt[0:r, k, :].rearrange("p (k h d) -> p k h d", k=2, d=8) for k in range(4)]
                for k, (e, f) in enumerate(((a, cosr), (b, sinr), (b, cosr), (a, sinr))):
                    chain(tt(m[k], e, f, ALU.mult))
                chain(tt(a, m[0], m[1], ALU.subtract))
                chain(tt(b, m[2], m[3], ALU.add))
                dve.sem_inc(S["qk_ready"], 1)

            fold_in(6)
            fold_in(7)

            keys_of = [128, 256, 320]

            def head_out(u):
                n, h = divmod(u, HEADS)
                r = TILES[n][1]
                dve.wait_ge(S["pv"], u + 1)
                dve.tensor_copy(o_tok[0:r, n, 128 * h:128 * h + 128], psum[0:r, 6 + u % 2, 0:128]).then_inc(S["o_out"], 1)

            dve.wait_ge(S["mask"], 16)
            dve.wait_ge(S["k_out"], 16 * NT)
            units = NT * HEADS
            for u in range(units + 3):
                scores, weights = u < units, 1 <= u <= units
                if scores:
                    n = u // HEADS
                    r, kk, b = TILES[n][1], keys_of[n], u % 2
                    dst, src = sm[u % 3][0:r, :, 0:kk], psum[0:r, 2 * b:2 * b + 2, 0:kk]
                    dve.wait_ge(S["s_mm"], u + 1)
                    if u >= 3:
                        dve.wait_ge(S["w_tr"], u - 2)
                    if n < 2:
                        tt(dst, src, spread(mask[0:r, n:n + 1, 0:kk], r, 2, kk), ALU.add).then_inc(S["s_sm"], 1)
                    else:
                        dve.tensor_copy(dst, src).then_inc(S["s_sm"], 1)
                if u >= 3:
                    head_out(u - 3)
                if weights:
                    wn = (u - 1) // HEADS
                    wr, wk, wb = TILES[wn][1], keys_of[wn], (u - 1) % 2
                    e0, e1 = (sm[(u - 1) % 3][0:wr, c, 0:wk] for c in range(2))
                if scores:
                    dve.wait_ge(S["s_sm"], u + 1)
                    chain.add(dve.tensor_reduce(mx[0:r, b, :], dst, AX.X, ALU.max))
                if weights:
                    dve.wait_ge(S["s_exp"], 2 * u)
                    chain.add(dve.reciprocal(rz[0:wr, wb, :], z[0:wr, wb, :]))
                chain.wait()
                if scores:
                    dve.tensor_scalar(nb[0:r, b, :], mx[0:r, b, :], -HD ** -0.5, None, ALU.mult).then_inc(S["s_mx"], 1)
                if weights:
                    chain.add(tt(rz[0:wr, wb, 1:2], rz[0:wr, wb, 1:2], nlam[0:wr], ALU.mult))
                    chain.add(dve.tensor_scalar(e0, e0, rz[0:wr, wb, 0:1], None, ALU.mult))
                    chain.wait()
                    dve.scalar_tensor_tensor(e0, e1, rz[0:wr, wb, 1:2], e0, ALU.mult, ALU.add).then_inc(S["w_ready"], 1)
            dve.wait_ge(S["o_out"], units)
            dve.wait_ge(S["xs"], 16)
            Xv = X[0:CH, :].rearrange("p (i g n) -> p g i n", i=STEP, g=GROUPS)
            for k in range(8):
                if k >= 2:
                    dve.wait_ge(S["ug_tr"], k - 1)
                dve.tensor_copy(Xg[0:CH, k % 2, :].rearrange("p (g i n) -> p g i n", g=8, i=STEP), Xv[:, 8 * k:8 * k + 8]).then_inc(S["xg"], 1)
            chain(dve.tensor_copy(pw_r[:, 0, :], a8r[:, 0:GP]))
            chain(dve.tensor_copy(pw_i[:, 0, :], a8n[:, GP:]))
            for k in (1, 2, 4):
                by = (spread(pw_r[:, k - 1:k, :], P, k, GP), spread(pw_i[:, k - 1:k, :], P, k, GP))
                times(pw_r[:, k:2 * k, :], pw_i[:, k:2 * k, :], pw_r[:, 0:k, :], pw_i[:, 0:k, :], *by, pw_t[:, 0:k, :])
            chain.add(dve.tensor_copy(AR[:, :, 0:GP], pw_r))
            chain.add(dve.tensor_copy(AR[:, :, GP:], pw_r))
            chain.add(dve.tensor_scalar(AN[:, :, 0:GP], pw_i, -1.0, None, ALU.mult))
            chain(dve.tensor_copy(AN[:, :, GP:], pw_i))
            for n, (t0, r) in enumerate(TILES):
                o = o_tok[0:r, n, :].rearrange("p (h d) -> p h d", h=HEADS)
                sq = sq_o[0:r, :].rearrange("p (h d) -> p h d", h=HEADS)
                chain(tt(sq, o, o, ALU.mult))
                chain(dve.tensor_reduce(hs[0:r, 0:HEADS], sq, AX.X, ALU.add))
                var_of(hv[0:r, 0:HEADS], hs[0:r, 0:HEADS], 2 * HD).then_inc(S["ovar"], 1)
                dve.wait_ge(S["ostd"], n + 1)
                chain(dve.reciprocal(hr[0:r, 0:HEADS], hv[0:r, 0:HEADS]))
                chain(dve.tensor_scalar(hr[0:r, 0:HEADS], hr[0:r, 0:HEADS], 1.0 - LAM_INIT, None, ALU.mult))
                chain(tt(o, o, spread(hr[0:r, 0:HEADS].unsqueeze(2), r, HEADS, 2 * HD), ALU.mult))
                tt(o, o, spread(sub_g[0:r].unsqueeze(1), r, HEADS, 2 * HD), ALU.mult).then_inc(S["o_ready"], 1)

            dve.wait_ge(S["f_mm"], 16)
            for ri in range(2):
                for b in range(3):
                    k = min(12, GP - 12 * b)
                    chain(dve.tensor_copy(FS[:, :, 32 * ri + 12 * b:32 * ri + 12 * b + k].rearrange("p c g -> p g c"),
                                          bank(3 * ri + b, 40 * k).rearrange("p (g c) -> p g c", g=k)))
            dve.sem_inc(S["f_out"], 1)
            chain.add(dve.memset(HP[:, 0:SEGS - 1, 0, :], 0.0))
            chain(dve.tensor_copy(HP[:, SEGS - 1, 0, :], h0))
            with dve.Fori(0, SEG) as i:
                def slot(k):
                    return HP[:, :, bass.ds(i + k, 1), :].rearrange("p s o x -> p s (o x)")

                old = slot(0)
                add = FS.rearrange("p (s c) x -> p s c x", s=SEGS)[:, :, bass.ds(i, 1), :].rearrange("p s o x -> p s (o x)")
                tt(t1, old, spread(a8r.unsqueeze(1), P, SEGS, 2 * GP), ALU.mult).then_inc(S["rec"], 1)
                tt(t2[:, :, 0:GP], old[:, :, GP:], spread(a8n[:, 0:GP].unsqueeze(1), P, SEGS, GP), ALU.mult).then_inc(S["rec"], 1)
                tt(t2[:, :, GP:], old[:, :, 0:GP], spread(a8n[:, GP:].unsqueeze(1), P, SEGS, GP), ALU.mult).then_inc(S["rec"], 1)
                dve.wait_ge(S["rec"], i * 5 + 3)
                tt(t1, t1, t2, ALU.add).then_inc(S["rec"], 1)
                dve.wait_ge(S["rec"], i * 5 + 4)
                tt(slot(1), t1, add, ALU.add).then_inc(S["rec"], 1)
                dve.wait_ge(S["rec"], i * 5 + 5)
            dve.wait_ge(S["rec"], 5 * SEG)

            def carried(new, add, old, ar, an, u1, u2):
                chain.add(tt(u1, old, ar, ALU.mult))
                chain.add(tt(u2[..., 0:GP], old[..., GP:], an[..., 0:GP], ALU.mult))
                chain(tt(u2[..., GP:], old[..., 0:GP], an[..., GP:], ALU.mult))
                chain(tt(u1, u1, u2, ALU.add))
                chain(tt(new, u1, add, ALU.add))

            chain(dve.tensor_copy(HP[:, 1, 0, :], HP[:, 0, SEG, :]))
            for g in (1, 2, 3):
                carried(HP[:, g + 1, 0, :] if g < 3 else HP[:, g, SEG, :], HP[:, g, SEG, :], HP[:, g, 0, :],
                        AR[:, SEG - 1, :], AN[:, SEG - 1, :], t1[:, 0, :], t2[:, 0, :])
            dve.sem_inc(S["hp"], 1)
            inner = (P, 3, SEG - 1, 2 * GP)
            carried(HP[:, 1:4, 1:SEG, :], HP[:, 1:4, 1:SEG, :], spread(HP[:, 1:4, 0:1, :], *inner),
                    spread(AR[:, 0:SEG - 1, :].unsqueeze(1), *inner), spread(AN[:, 0:SEG - 1, :].unsqueeze(1), *inner), far1, far2)
            dve.tensor_copy(HCt.rearrange("p x (s c) -> p x s c", s=SEGS),
                            HP[:, :, 0:SEG, :].rearrange("p s c x -> p x s c")).then_inc(S["hc"], 1)

            for j in range(2):
                low_rows(j, dense_part, "y_hi", "y_lo")
            dve.wait_ge(S["bg"], 16)
            for c in range(2):
                for n, (t0, r) in enumerate(TILES):
                    dve.wait_ge(S["glu_mm"], 3 * c + n + 1)
                    cc = slice(c * COLS, (c + 1) * COLS)
                    out = psum[0:r, 3 * c + n, :] if n < 2 else folded(3 * c + n)
                    tt(z_tok[0:r, n, cc], out, bglu[0:r, cc], ALU.add).then_inc(S["glu_b"], 1)
                dve.wait_ge(S["glu_b"], NT * (c + 1))
            for j in range(2):
                low_rows(j, dense_part, "mix_hi", "mix_lo")
            for half in range(2):
                dve.wait_ge(S[f"y_in{half}"], 16 * NT)
            dve.wait_ge(S["glu_s"], 2 * NT)
            for n, (t0, r) in enumerate(TILES):
                tt(z_tok[0:r, n, :], z_tok[0:r, n, :], y_tok[0:r, n, :], ALU.mult).then_inc(S["s_ready"], 1)
            for j in (2, 3):
                low_rows(j, dense_part, "mix_hi", "mix_lo")
            dve.wait_ge(S["x_re"], 16 * NT)
            for c in range(4):
                for n, (t0, r) in enumerate(TILES):
                    dve.wait_ge(S["out_mm"], 3 * c + n + 1)
                    xx = x2[0:r, n, c * COLS:(c + 1) * COLS]
                    out = psum[0:r, 3 * (c % 2) + n, :] if n < 2 else folded(3 * (c % 2) + n)
                    tt(xx, out, xx, ALU.add).then_inc(S["out_x"], 1)
                dve.wait_ge(S["out_x"], NT * (c + 1))

            norm_rows(x2, xn2, "ssq2", "var2", "std2", "xn2")
            rows_out(xn2T, g2, "tr2", "xn2T", peer_part, "x_hi", "x_lo")

            def top16(rows, values, value_of, index_of, rest_of, count):
                for k in range(count):
                    chain.add(dve.max(value_of(k)[:, 0:8], values(k)))
                chain.wait()
                for k in range(count):
                    chain.add(dve.max_index(index_of(k)[:, 0:8], value_of(k)[:, 0:8], values(k)))
                    chain.add(dve.match_replace(rest_of(k), value_of(k)[:, 0:8], values(k), LOW))
                chain.wait()
                for k in range(count):
                    chain.add(dve.max(value_of(k)[:, 8:16], rest_of(k)))
                chain.wait()
                for k in range(count):
                    chain.add(dve.max_index(index_of(k)[:, 8:16], value_of(k)[:, 8:16], rest_of(k)))
                chain.wait()

            for c in range(4):
                for n, (t0, r) in enumerate(TILES):
                    dve.wait_ge(S["sc_out"], NT * c + n + 1)
                    at_c = slice(HC * n + 4 * c, HC * n + 4 * c + 4)
                    top16(r, lambda k: sc[0:r, n, PK * (4 * c + k):PK * (4 * c + k + 1)], lambda k: sv[0:r, HC * n + 4 * c + k, :],
                          lambda k: si[0:r, k, :], lambda k: sc2[0:r, k, :], 4)
                    chain(dve.tensor_copy(sif[0:r, at_c], si[0:r]))
            for n, (t0, r) in enumerate(TILES):
                four = (r, PH, TOPK, TOPK)
                s4 = sv[0:r, HC * n:HC * (n + 1)].rearrange("p (h c) k -> p h c k", c=2)
                f4 = sif[0:r, HC * n:HC * (n + 1)].rearrange("p (h c) k -> p h c k", c=2)
                chain(tt(cand[0:r].rearrange("p h (a b) -> p h a b", a=TOPK), spread(s4[:, :, 0, :].unsqueeze(3), *four),
                         spread(s4[:, :, 1, :].unsqueeze(2), *four), ALU.add))
                top16(r, lambda k: cand[0:r, k, :], lambda k: fv[0:r, k, :], lambda k: fp[0:r, k, :],
                      lambda k: cand2[0:r, k, :], PH)
                tt(gate[0:r, n, :].rearrange("p (h k) -> p h k", h=PH), fv[0:r], spread(fv[0:r, :, 0:1], r, PH, TOPK),
                   ALU.subtract).then_inc(S["gmx"], 1)
                fpu = fp[0:r].rearrange("p h k -> p (h k)")
                chain(dve.tensor_scalar(pa_u[0:r], fpu, 4, None, ALU.logical_shift_right))
                chain(dve.tensor_scalar(pb_u[0:r], fpu, 15, None, ALU.bitwise_and))
                for c, (pu, pf, pick) in enumerate(((pa_u, pa, pick_i), (pb_u, pb, pick_j))):
                    flat = pf[0:r].rearrange("p h k -> p (h k)")
                    chain(dve.tensor_copy(flat, pu[0:r]))
                    chain(tt(eq_k[0:r], spread(iota[0:r, 0:TOPK].unsqueeze(1), r, PH * TOPK, TOPK),
                             spread(flat.unsqueeze(2), r, PH * TOPK, TOPK), ALU.is_equal))
                    e4 = eq_k[0:r].rearrange("p (h k) a -> p h k a", h=PH)
                    chain(tt(e4, e4, spread(f4[:, :, c, :].unsqueeze(2), *four), ALU.mult))
                    chain(dve.tensor_reduce(pick[0:r, n, :], eq_k[0:r], AX.X, ALU.add))
            for n, (t0, r) in enumerate(TILES):
                dve.wait_ge(S["gex"], n + 1)
                g3 = gate[0:r, n, :].rearrange("p (h k) -> p h k", h=PH)
                chain(dve.tensor_reduce(gs[0:r], g3, AX.X, ALU.add))
                chain(dve.reciprocal(gs[0:r], gs[0:r]))
                tt(g3, g3, spread(gs[0:r].unsqueeze(2), r, PH, TOPK), ALU.mult).then_inc(S["picks"], 1)
                dve.wait_ge(S["picks"], n + 1)
            dve.wait_ge(S["pick_tr"], NT)
            for n, (t0, r) in enumerate(TILES):
                for k, dst in enumerate((gT, iT, jT)):
                    chain(dve.tensor_copy(dst[:, t0:t0 + r], psum[:, 4 + n, 128 * k:128 * k + r]))
            chain(dve.tensor_copy(gpart[:, 0, :], gT))
            chain(tt(grest, gT, gpart[:, 0, :], ALU.subtract))
            chain(dve.tensor_copy(gpart[:, 1, :], grest))
            chain(tt(grest, grest, gpart[:, 1, :], ALU.subtract))
            chain(dve.tensor_copy(gpart[:, 2, :], grest))

            def one_hots(s, i, k, free=True):
                tok = bass.ds(i * (4 * TOK) + k * TOK, TOK)
                base = SEC * s + k
                if free:
                    dve.wait_ge(S["gs_mm"], i * 4 + (base - 1))
                keys_i = iota[:, SEC * s:SEC * (s + 1)]
                tt(eqA[k % 2], spread(keys_i.unsqueeze(1), P, TOK, SEC), spread(iT[:, tok].unsqueeze(2), P, TOK, SEC),
                   ALU.is_equal).then_inc(S["eq"], 1)
                tt(oneB[k % 2], spread(iota.unsqueeze(1), P, TOK, PK), spread(jT[:, tok].unsqueeze(2), P, TOK, PK),
                   ALU.is_equal).then_inc(S["one"], 1)
                dve.wait_ge(S["eq"], i * 4 + (base + 1))
                tt(oneA[k % 2].rearrange("p c (t i) -> p c t i", t=TOK), spread(eqA[k % 2].unsqueeze(1), P, 3, TOK, SEC),
                   spread(gpart[:, :, tok].unsqueeze(3), P, 3, TOK, SEC), ALU.mult).then_inc(S["one"], 1)

            def gates_out(s, i, k):
                three = psum[:, 2 + 2 * (k % 2):4 + 2 * (k % 2), 0:TOK // 2 * 3 * SEC].rearrange("p b (t c i) -> p b t i c", t=TOK // 2, c=3)
                dst = GM[:, :, bass.ds(i * (4 * TOK) + k * TOK, TOK)].rearrange("p i (b t) -> p b t i", b=2)
                dve.wait_ge(S["gs_mm"], i * 4 + (SEC * s + k + 1))
                dve.tensor_reduce(dst, three, AX.X, ALU.add).then_inc(S["gs_out"], 1)

            def group(s, i, k, first=False):
                one_hots(s, i, k, not (first and s == 0 and k < 2))
                if not (first and k == 0):
                    gates_out(s, i + (-1 if k == 0 else 0), (k - 1) % 4)

            def parts(s, half, i, k, free=True):
                h = H[:, bass.ds(i * 8 + k, 1), :].rearrange("p o t -> p (o t)")
                hi, lo = h_parts[:, k % 2, 0, :], h_parts[:, k % 2, 1, :]
                done = SEC * (2 * s + half) + k + 1
                if half == 0:
                    g = GM[:, bass.ds(i * 8 + k, 1), :].rearrange("p o t -> p (o t)")
                    tt(h, h, g, ALU.mult).then_inc(S["e_w"], 1)
                    dve.wait_ge(S["e_w"], i * 8 + (SEC * s + k + 1))
                if free:
                    dve.wait_ge(S["w_used"], i * 16 + (4 * b_block(s, half) + 2 * (k - 1)))
                dve.tensor_scalar(hi, h, 1.0, None, ALU.mult).then_inc(S["g_hi"], 1)
                dve.wait_ge(S["g_hi"], i * 8 + done)
                tt(lo, h, hi.bitcast(F32), ALU.subtract).then_inc(S["g_lo"], 1)

            for s in range(SECTIONS):
                for k in range(4):
                    group(s, 0, k, first=True)
                with dve.Fori(1, SEC // 4) as i:
                    for k in range(4):
                        group(s, i, k)
                gates_out(s, SEC // 4 - 1, 3)
                dve.wait_ge(S["gs_out"], SEC * (s + 1))
                dve.wait_ge(S["h_g"], SEC * (s + 1))
                for k in range(8):
                    parts(s, 0, 0, k, k >= 2)
                with dve.Fori(1, SEC // 8) as i:
                    for k in range(8):
                        parts(s, 0, i, k)
                for half in range(2):
                    if half == 0:
                        parts(s, 1, 0, 0)
                    for k in range(8):
                        if k % 4 == 3:
                            dve.wait_ge(S["w_used"], 4 * b_block(s, half) + 2 * SEC - 1 + k // 4)
                        else:
                            dve.wait_ge(S["e_o"], 6 * (2 * s + half) + k - k // 4 + 1)
                        a = acc[:, 8 * half + k, :]
                        if s == 0:
                            dve.tensor_copy(a, bank(k, T)).then_inc(S["e_acc"], 1)
                        else:
                            tt(a, bank(k, T), a, ALU.add).then_inc(S["e_acc"], 1)
                    if half == 0:
                        for k in range(1, 8):
                            parts(s, 1, 0, k)
                        with dve.Fori(1, SEC // 8) as i:
                            for k in range(8):
                                parts(s, 1, i, k)
            dve.wait_ge(S["x_bk"], 16 * NT)
            for n, (t0, r) in enumerate(TILES):
                for j in range(4):
                    dve.wait_ge(S["fin_tr"], 4 * n + j + 1)
                    xx = x3[0:r, n, COLS * j:COLS * (j + 1)]
                    tt(xx, psum[0:r, (4 * n + j) % 8, :], xx, ALU.add).then_inc(S["fin"], 1)

        @block.tensor
        def _(pe):
            def transposes(src_of, ready, tr, out, quads):
                for n, (t0, r) in enumerate(TILES):
                    pe.wait_ge(S[ready], n + 1)
                    for j in range(quads):
                        m = quads * n + j
                        if m >= 8:
                            pe.wait_ge(S[out], m - 7)
                        for k in range(4):
                            ins = pe.transpose(psum[:, m % 8, 128 * k:128 * k + r], src_of(n, r, 4 * j + k), ident[0:r, 0:r])
                        ins.then_inc(S[tr], 1)

            def rows_T(j, src_of, ready, tr, out):
                for n, (t0, r) in enumerate(TILES):
                    m = NT * j + n
                    if ready:
                        pe.wait_ge(S[ready], n + 1)
                    if m >= 4:
                        pe.wait_ge(S[out], m - 3)
                    for k in range(4):
                        ins = pe.transpose(psum[:, 4 + m % 4, 128 * k:128 * k + r], src_of(n, r, 4 * j + k), ident[0:r, 0:r])
                    ins.then_inc(S[tr], 1)

            def rows_ahead(b, lo_s, *rows):
                if b == 0:
                    rows_T(0, *rows)
                if b < 3:
                    rows_T(b + 1, *rows)
                pe.wait_ge(S[lo_s], NT * (b + 1))

            def dense(i, g0, per_chunk, chunks, mm, out, first=False, ahead=None, fold_s=None):
                for c in range(chunks):
                    for dc in range(4 * per_chunk):
                        q = dc % 4
                        if ahead and c == q == 0:
                            ahead(dc // 4)
                        pe.wait_ge(S["w_lo"], i * (4 * chunks * per_chunk) + (4 * (g0 + c * per_chunk) + dc + 1))
                        for n, (t0, r) in enumerate(TILES):
                            if dc == 0 and not (first and c < 2):
                                pe.wait_ge(S[out], i * (NT * chunks) + (NT * (c - 2) + n + 1))
                                if fold_s and n == 2:
                                    pe.wait_ge(S[fold_s], i * chunks + (c - 1))
                            start, stop = dc == 0, dc == 4 * per_chunk - 1
                            b = 3 * (c % 2) + n
                            if n < 2:
                                o, xh, xl = psum[:, b, :], xd[:, dc, t0:t0 + r], xd[:, dc, LOW_AT[n]:LOW_AT[n] + r]
                                pe.matmul(o, xh, w_parts[:, q, 0, :], start=start, stop=False)
                                pe.matmul(o, xh, w_parts[:, q, 1, :], start=False, stop=False)
                                ins = pe.matmul(o, xl, w_parts[:, q, 0, :], start=False, stop=stop)
                            else:
                                both = xd[:, dc, t0:t0 + 2 * r]
                                pe.matmul(psum[:, b, :], both, w_parts[:, q, 0, :], start=start, stop=False)
                                ins = pe.matmul(psum[:, b, :], both, w_parts[:, q, 1, :], start=False, stop=stop)
                            if stop:
                                ins.then_inc(S[mm], 1)
                        if not stop:
                            ins.then_inc(S["w_used"], 1)
                        else:
                            pe.wait_ge(S[mm], i * (NT * chunks) + NT * (c + 1))
                            pe.sem_inc(S["w_used"], 1)

            pe.wait_ge(S["consts"], ALL_CONSTS)
            dense(0, B_IN, 4, 2, "in_mm", "in_out", first=True, ahead=lambda b: rows_ahead(
                b, "x1_lo", lambda n, r, dc: x_tok[0:r, n, 128 * dc:128 * (dc + 1)], "xn", "tr1", "xT"))
            with pe.Fori(1, 4) as i:
                dense(i, B_IN, 4, 2, "in_mm", "in_out", fold_s="in_fold")

            pe.wait_ge(S["in_out"], 8 * NT)
            pe.wait_ge(S["in_fold"], 8)
            transposes(lambda n, r, hh: proj[0:r, 1 + hh // 8, n, 128 * (hh % 8):128 * (hh % 8) + 128], "qk_ready", "qk_tr", "qkT", 4)
            pe.wait_ge(S["qkT"], 12)
            keys_of = [128, 256, 320]

            def scores(u):
                n, h = divmod(u, HEADS)
                (t0, r), kk = TILES[n], keys_of[n]
                if u >= 2:
                    pe.wait_ge(S["s_sm"], u - 1)
                if u == 2 * HEADS:
                    pe.wait_ge(S["cache"], 48)
                for c in range(2):
                    hp = slice(64 * c, 64 * c + 64)
                    q, out = qkT[hp, h, t0:t0 + r], psum[0:r, 2 * (u % 2) + c, :]
                    if n < 2:
                        ins = pe.matmul(out[:, 0:kk], q, qkT[hp, 8 + h, 0:kk], start=True, stop=True)
                    else:
                        pe.matmul(out[:, 0:PAST], q, ckT[hp, h, :], start=True, stop=True)
                        ins = pe.matmul(out[:, PAST:kk], q, qkT[hp, 8 + h, t0:t0 + r], start=True, stop=True)
                ins.then_inc(S["s_mm"], 1)

            def key_blocks(n):
                return [min(P, keys_of[n] - a) for a in range(0, keys_of[n], P)]

            def weights_T(u):
                n, r, b = u // HEADS, TILES[u // HEADS][1], u % 2
                pe.wait_ge(S["w_ready"], u + 1)
                if u:
                    pe.wait_ge(S["wT"], u)
                if u > 2 * HEADS:
                    pe.wait_ge(S["wT_part"], u - 2 * HEADS)
                for k, w in enumerate(key_blocks(n)):
                    ins = pe.transpose(psum[0:w, 4, 128 * k:128 * k + r], sm[u % 3][0:r, 0, 128 * k:128 * k + w], ident[0:r, 0:r])
                ins.then_inc(S["w_tr"], 1)

            def values(u):
                (n, h), b = divmod(u, HEADS), u % 2
                r, blocks = TILES[n][1], key_blocks(n)
                pe.wait_ge(S["wT"], u + 1)
                if n == 2:
                    pe.wait_ge(S["wT_part"], h + 1)
                if u >= 2:
                    pe.wait_ge(S["o_out"], u - 1)
                for k, w in enumerate(blocks):
                    if n < 2:
                        v = proj[0:w, 3, k, 128 * h:128 * h + 128]
                    else:
                        v = cv[0:w, k, 128 * h:128 * h + 128] if k < 2 else proj[0:w, 3, 2, 128 * h:128 * h + 128]
                    ins = pe.matmul(psum[0:r, 6 + b, 0:128], wT[0:w, b, k, 0:r], v, start=k == 0, stop=k == len(blocks) - 1)
                ins.then_inc(S["pv"], 1)

            units = NT * HEADS
            def s5_products(u):
                parity, part = divmod(u, units // 2)
                pr = slice(64 * parity, 64 * parity + 64)
                if u == units // 2:
                    pe.wait_ge(S["k7out"], 1)
                for gp in range(3 * part, min(3 * part + 3, GP)):
                    out = psum[:, 5, 16 * gp:16 * gp + 16]
                    pe.matmul(out, WX[0][pr, gp, :], bcin[pr, 2, 16 * gp:16 * gp + 16], start=True, stop=False)
                    ins = pe.matmul(out, WX[1][pr, gp, :], nci[pr, 16 * gp:16 * gp + 16], start=False, stop=True)
                    if gp == GP - 1:
                        ins.then_inc(S["k7mm"], 1)

            pe.wait_ge(S["s5w"], 1)
            scores(0)
            scores(1)
            for u in range(units + 1):
                if u + 2 < units:
                    scores(u + 2)
                if u < units:
                    weights_T(u)
                if u:
                    values(u - 1)
                if u < units:
                    s5_products(u)

            pe.wait_ge(S["o_out"], units)
            pe.wait_ge(S["k7out"], 2)
            for k in range(8):
                pe.wait_ge(S["xg"], k + 1)
                for j in range(8):
                    ins = pe.transpose(psum[:, k, CH * j:CH * (j + 1)], Xg[0:CH, k % 2, 128 * j:128 * (j + 1)], ident[0:CH, 0:CH])
                ins.then_inc(S["ug_tr"], 1)
            pe.wait_ge(S["ug"], 8)
            def state_matrices(q):
                if q >= 2:
                    pe.wait_ge(S["wt"], q - 1)
                for k in range(4):
                    ins = pe.transpose(psum[:, 6 + q % 2, 128 * k:128 * k + 128], WX[k % 2][:, 2 * q + k // 2, :], ident[:, :])
                ins.then_inc(S["wt_tr"], 1)

            def state_inputs(q):
                pe.wait_ge(S["wt"], q + 1)
                for k in range(8):
                    gp, ri, par = 2 * q + k // 4, (k // 2) % 2, k % 2
                    ins = pe.matmul(psum[64 * par:64 * par + 64, 3 * ri + gp // 12, CH * (gp % 12):CH * (gp % 12) + CH],
                                    WTs[:, q % 2, 128 * (2 * (k // 4) + ri) + 64 * par:128 * (2 * (k // 4) + ri) + 64 * par + 64],
                                    UG[:, 2 * gp + par, :], start=True, stop=True)
                ins.then_inc(S["f_mm"], 1)

            for q in range(17):
                if q < 16:
                    state_matrices(q)
                if q:
                    state_inputs(q - 1)
            pe.wait_ge(S["f_out"], 1)
            pe.wait_ge(S["k7st"], 16 * STEP)
            Tg = Tm.rearrange("p j (g n) -> p j g n", g=GROUPS)

            def own_inputs(q, k):
                g = 8 * (q // 2) + 2 * k + q % 2
                pe.matmul(psum[0:CH, q % 8, 128 * k:128 * k + 128], UG[:, g, :], Tg[:, :, g, :], start=k == 0, stop=False)

            for q in range(8):
                for k in range(4):
                    own_inputs(q, k)
            pe.wait_ge(S["hc"], 1)
            pe.wait_ge(S["ca"], 6)
            for q in range(16):
                if q >= 8:
                    pe.wait_ge(S["y_gl"], q - 7)
                for k in range(4):
                    if q >= 8:
                        own_inputs(q, k)
                    g = 8 * (q // 2) + 2 * k + q % 2
                    pr, gp = slice(64 * (g % 2), 64 * (g % 2) + 64), g // 2
                    out = psum[0:CH, q % 8, 128 * k:128 * k + 128]
                    pe.matmul(out, HCt[pr, gp, :], CA[0][pr, gp, :], start=False, stop=False)
                    ins = pe.matmul(out, HCt[pr, GP + gp, :], CA[1][pr, gp, :], start=False, stop=k == 3)
                ins.then_inc(S["y_mm"], 1)
            pe.wait_ge(S["y_gl"], 16)

            def y_ahead(b):
                pe.wait_ge(S[f"y_in{b}"], 16 * NT)
                rows_T(b, lambda n, r, dc: y_tok[0:r, n, 128 * dc:128 * (dc + 1)], None, "yT_tr", "y_lo")
                pe.wait_ge(S["y_lo"], NT * (b + 1))

            dense(0, B_GLU, 2, 2, "glu_mm", "glu_b", first=True, ahead=y_ahead)
            pe.wait_ge(S["glu_b"], 6)
            pe.wait_ge(S["o_ready"], NT)
            dense(0, B_OUT, 4, 4, "out_mm", "out_x", first=True, ahead=lambda b: rows_ahead(
                b, "mix_lo", lambda n, r, dc: (o_tok if dc < 8 else z_tok)[0:r, n, 128 * (dc % 8):128 * (dc % 8) + 128],
                "s_ready" if b else "o_ready", "mix_tr", "mix_lo"))

            pe.wait_ge(S["out_x"], 12)
            def product(out, q, column, moving, start, stop):
                c = slice(column, column + 128)
                pe.matmul(out, w_parts[:, q, 0, c], moving(0), start=start, stop=False)
                pe.matmul(out, w_parts[:, q, 0, c], moving(1), start=False, stop=False)
                return pe.matmul(out, w_parts[:, q, 1, c], moving(0), start=False, stop=stop)

            def key_scores(c):
                pe.wait_ge(S["qT"], 4 * (c + 1))
                for n, (t0, r) in enumerate(TILES):
                    for j in range(4):
                        hc = 4 * c + j
                        ins = pe.matmul(psum[0:r, 4 * (c % 2) + n, 128 * j:128 * j + 128], qT[:, hc, t0:t0 + r],
                                        keys[:, 128 * hc:128 * (hc + 1)], start=True, stop=True)
                    ins.then_inc(S["sc_mm"], 1)

            pe.wait_ge(S["keys"], 16)
            for c in range(4):
                for b in range(4):
                    if c == 0:
                        rows_ahead(b, "x_lo", lambda n, r, dc: xn2[0:r, n, 128 * dc:128 * (dc + 1)], "xn2", "tr2", "xn2T")
                    if c and b == 1:
                        key_scores(c - 1)
                    for q in range(4):
                        pe.wait_ge(S["w_lo"], 4 * B_PQ + 16 * c + 4 * b + q + 1)
                        for k in range(4):
                            if c >= 2 and b == q == k == 0:
                                pe.wait_ge(S["sc_out"], NT * (c - 1))
                            ins = product(psum[:, 4 * (c % 2) + k, 0:T], q, 128 * k, lambda p: x_parts[:, p, 4 * b + q, :],
                                          b == q == 0, b == q == 3)
                        ins.then_inc(S["w_used"], 1)
            pe.wait_ge(S["sc_out"], 3 * NT)

            def spread_gates(i, step, g, free=True):
                pe.wait_ge(S["one"], i * (2 * step) + 2 * (g + 1))
                if free:
                    pe.wait_ge(S["gs_out"], i * step + (g - 1))
                for t in range(TOK):
                    b, n = divmod(t, TOK // 2)
                    ins = pe.matmul(psum[:, 2 + 2 * (g % 2) + b, 3 * SEC * n:3 * SEC * (n + 1)], oneB[g % 2][:, t, :],
                                    oneA[g % 2][:, :, SEC * t:SEC * (t + 1)], start=True, stop=True)
                ins.then_inc(S["gs_mm"], 1)

            for s in range(SECTIONS):
                def block_in(i, b, free=True):
                    if free:
                        pe.wait_ge(S["h_g"], i * 4 + (SEC * s + b - 1))
                    for q in range(4):
                        pe.wait_ge(S["w_lo"], i * 16 + (4 * (a_block(s) + b) + q + 1))
                        for d in range(4):
                            dc = 4 * q + d
                            ins = product(bank(b % 2, T), q, 128 * d, lambda p: x_parts[:, p, dc, :], dc == 0, dc == DC - 1)
                        ins.then_inc(S["w_used"], 1)

                if s == 0:
                    for b in range(SLOTS):
                        block_in(0, b, b >= 2)
                        if b == 0:
                            key_scores(3)
                    with pe.Fori(1, SEC // SLOTS // 2) as i:
                        for b in range(SLOTS):
                            block_in(i, b)
                    for n, (t0, r) in enumerate(TILES):
                        pe.wait_ge(S["picks"], n + 1)
                        for k, src in enumerate((gate, pick_i, pick_j)):
                            ins = pe.transpose(psum[:, 4 + n, 128 * k:128 * k + r], src[0:r, n, :], ident[0:r, 0:r])
                        ins.then_inc(S["pick_tr"], 1)
                    for b in range(SLOTS):
                        block_in(0, SEC // 2 + b)
                        for g in (2 * b, 2 * b + 1):
                            spread_gates(0, 8, g, g >= 2)
                    with pe.Fori(1, SEC // SLOTS // 2) as i:
                        for b in range(SLOTS):
                            block_in(i, SEC // 2 + b)
                            for g in (2 * b, 2 * b + 1):
                                spread_gates(i, 8, g)
                else:
                    pe.wait_ge(S["e_acc"], 16 * s - 2)
                    with pe.Fori(0, SEC // SLOTS) as i:
                        for b in range(SLOTS):
                            block_in(i, b)
                            spread_gates(i, 4, SEC * s + b)
                pe.wait_ge(S["gs_out"], SEC * (s + 1))
                for half in range(2):
                    def experts_out(i, first=False, last=False):
                        for k in range(SLOTS):
                            for q in range(4):
                                ii = q // 2
                                if q % 2 == 0:
                                    pe.wait_ge(S["g_lo"], i * 8 + (SEC * (2 * s + half) + 2 * k + ii + 1))
                                pe.wait_ge(S["w_lo"], i * 16 + (4 * (b_block(s, half) + k) + q + 1))
                                start, stop = first and k == ii == 0, last and k == 3 and ii == 1
                                for d in range(4):
                                    dd = 4 * (q % 2) + d
                                    if start and (s or half):
                                        pe.wait_ge(S["e_acc"], 8 * (2 * s + half - 1) + dd + 1)
                                    ins = product(bank(dd, T), q, 128 * d, lambda p: h_parts[:, ii, p, :], start, stop)
                                    if stop and d < 3:
                                        ins.then_inc(S["e_o"], 1)
                                ins.then_inc(S["w_used"], 1)

                    experts_out(0, first=True)
                    with pe.Fori(1, SEC // 8 - 1) as i:
                        experts_out(i)
                    experts_out(SEC // 8 - 1, last=True)
            for n, (t0, r) in enumerate(TILES):
                for j in range(4):
                    m = 4 * n + j
                    if m == 0:
                        pe.wait_ge(S["e_acc"], 16 * SECTIONS)
                    if m >= 8:
                        pe.wait_ge(S["fin"], m - 7)
                    for k in range(4):
                        ins = pe.transpose(psum[0:r, m % 8, 128 * k:128 * k + 128], acc[:, 4 * j + k, t0:t0 + r], ident[:, :])
                    ins.then_inc(S["fin_tr"], 1)


def stream(w, order=None):
    rows, columns = w.shape
    b = w.reshape(rows // COLS, 4, P, columns // COLS, COLS).transpose(3, 0, 2, 1, 4)
    if order is not None:
        b = b[order]
    return np.ascontiguousarray(b.reshape(-1, P, BLOCK))


def states(a):
    a = a.reshape(GP, 2, SSM_N, *a.shape[2:])
    return np.ascontiguousarray(np.moveaxis(a, 0, 2).reshape(P, GP, *a.shape[3:]).reshape(P, -1))


def kernel(**inputs):
    import concourse.bacc as bacc
    from concourse.bass_utils import run_bass_kernel_spmd

    a = {k: np.asarray(v) for k, v in inputs.items()}
    x = np.concatenate([a["x_prompt"][0], a["x_sample"][0]])
    pos = np.arange(T, dtype=np.float32)
    inv = np.float32(500000.0) ** (-np.arange(8, dtype=np.float32) * np.float32(2.0 / 16))
    ang = (pos[:, None] * inv[None, :]).astype(np.float32)
    rope = np.zeros((P, NT, 16), np.float32)
    for n, (t0, r) in enumerate(TILES):
        rope[:r, n, 0:8] = np.cos(ang[t0:t0 + r])
        rope[:r, n, 8:16] = np.sin(ang[t0:t0 + r])
    mask = np.zeros((P, 2, 256), np.float32)
    for n in range(2):
        q_chunk = (np.arange(P) + 128 * n) // 64
        mask[:, n] = np.where(np.arange(256)[None, :] // 64 <= q_chunk[:, None], 0.0, -1e30)
    dmask = np.zeros((P, SSM_P), np.float32)
    dmask[P - SSM_P:] = np.eye(SSM_P)
    skip = np.concatenate([np.zeros((P - SSM_P, GROUPS), np.float32), a["ssm_d"][0].reshape(GROUPS, SSM_P).T])
    u = a["peer_u"][0].reshape(PK, P, DC, P)
    v = a["peer_v"][0].reshape(SECTIONS, SEC // 2, 2, P, 2, 1024)
    arrays = {
        "x": x, "ident": np.eye(P, dtype=np.float32), "iota": np.arange(P, dtype=np.float32), "rope": rope.reshape(P, -1),
        "mask": mask, "dmask": dmask, "skip": skip,
        "norm1_g": a["norm1_g"][0].reshape(DC, P).T, "norm2_g": a["norm2_g"][0].reshape(DC, P).T,
        "q_g": a["q_norm_g"][0], "k_g": a["k_norm_g"][0], "sub_g": a["subln_g"][0],
        "lq1": a["lambda_q1"][0], "lk1": a["lambda_k1"][0], "lq2": a["lambda_q2"][0], "lk2": a["lambda_k2"][0],
        "a_re": states(a["ssm_a_re"][0]), "a_im": states(a["ssm_a_im"][0]),
        "log_dt": states(np.broadcast_to(a["ssm_log_dt"][0][:, None], (GROUPS, SSM_N))),
        "b_re": states(a["ssm_b_re"][0]), "b_im": states(a["ssm_b_im"][0]),
        "c_re": states(a["ssm_c_re"][0].transpose(0, 2, 1)), "c_im": states(a["ssm_c_im"][0].transpose(0, 2, 1)),
        "h0_re": states(a["state_ssm_re"][0, 0]), "h0_im": states(a["state_ssm_im"][0, 0]),
        "cache_k": a["cache_k"][0, 0].reshape(PAST, HEADS, P).transpose(2, 1, 0),
        "cache_v": a["cache_v"][0, 0].reshape(PAST, 1024),
        "b_glu": a["b_glu"][0],
        "keys": a["peer_keys"][0].transpose(3, 0, 1, 2).reshape(P, D),
        "w_in": stream(a["w_in"][0], [6, 7, 0, 1, 2, 3, 4, 5]),
        "w_glu": stream(a["w_glu"][0]), "w_out": stream(a["w_out"][0]), "w_pq": stream(a["w_peer_q"][0]),
        "peer_u": u.transpose(0, 3, 2, 1).reshape(PK, P, BLOCK),
        "peer_v": v.transpose(0, 4, 1, 3, 2, 5).reshape(PK, P, BLOCK),
    }
    arrays = {k: np.ascontiguousarray(v) for k, v in arrays.items()}
    nc = bacc.Bacc("TRN2", target_bir_lowering=False, num_devices=1)
    io = {k: nc.dram_tensor(f"in_{k}", v.shape, F32, kind="ExternalInput").ap() for k, v in arrays.items()}
    outs = {"y": (T, D), "k_all": (T, 1024), "v_all": (T, 1024), "states": (P, 2, 2 * GP)}
    for k, shape in outs.items():
        io[k] = nc.dram_tensor(f"out_{k}", shape, F32, kind="ExternalOutput").ap()
    for k, n in (("u_tmp", 1024), ("y_tmp", 1024), ("x_tmp", D)):
        io[k] = nc.dram_tensor(k, (T, n), F32, kind="Internal").ap()
    build(nc, io)
    res = run_bass_kernel_spmd(nc, [{f"in_{k}": v for k, v in arrays.items()}], core_ids=[0]).results[0]
    y, k, v, st = (np.asarray(res[f"out_{n}"]) for n in outs)
    st = st.reshape(2, SSM_N, 2, 2, GP).transpose(2, 3, 4, 0, 1).reshape(2, 2, 1, 1, GROUPS, SSM_N)
    kp, ks = (k[s].reshape(1, 1, -1, HEADS, 2, HD) for s in (slice(0, T_PROMPT), slice(T_PROMPT, T)))
    vp, vs = (v[s].reshape(1, 1, -1, HEADS, 2 * HD) for s in (slice(0, T_PROMPT), slice(T_PROMPT, T)))
    return (y[None, :T_PROMPT], y[None, T_PROMPT:], kp, vp, st[0, 0], st[0, 1], ks, vs, st[1, 0], st[1, 1])
```
